# Optimizing a Trainium2 kernel written in Bass

```python
import math
import jax, jax.numpy as jnp
from jax import lax
import numpy as np

D_MODEL = 1024
BATCH = 1
SEQ = 1024
DEPTH = 1

EPS = 1e-6
PLE_DIM = 256

GLA_HEADS = 4
GLA_DK = D_MODEL // 16
GLA_DV = D_MODEL // 8
GLA_QK = GLA_HEADS * GLA_DK
GLA_WIDTH = GLA_HEADS * GLA_DV
GLA_GATE_RANK = 16
GLA_TAU = 16.0
GLA_CHUNK = 64

HYENA_WIDTH = D_MODEL - GLA_WIDTH
HYENA_ORDER = 2
HYENA_SHORT = 3
HYENA_BANDS = 8
HYENA_EMB = 1 + 2 * HYENA_BANDS
HYENA_FFN = 64
HYENA_DECAY_TARGET = 1e-2
HYENA_FAST_PCT = 0.3
HYENA_SLOW_PCT = 1.5
HYENA_MIN_DECAY = math.log(HYENA_DECAY_TARGET) / HYENA_SLOW_PCT
HYENA_MAX_DECAY = math.log(HYENA_DECAY_TARGET) / HYENA_FAST_PCT

N_EXPERTS = 16
EC_CAPACITY = 2
D_FF_EXPERT = 2 * D_MODEL

MIX_WIDTH = GLA_WIDTH + HYENA_WIDTH
IN_SIZES = (GLA_QK, GLA_QK, GLA_WIDTH, GLA_WIDTH, GLA_GATE_RANK, GLA_GATE_RANK,
            (HYENA_ORDER + 1) * HYENA_WIDTH)
IN_COLS = GLA_QK * 2 + GLA_WIDTH * 2 + GLA_GATE_RANK * 2 + (HYENA_ORDER + 1) * HYENA_WIDTH

kernel_name = "hybrid_gla_hyena_ec_moe_encoder"

def rmsnorm(x, w):
    xf = x.astype(jnp.float32)
    y = xf * lax.rsqrt(jnp.mean(xf * xf, axis=-1, keepdims=True) + EPS)
    return (y * w.astype(jnp.float32)).astype(x.dtype)

def gla_direction(q, k, v, loga, strict):
    B, L, H, dk = q.shape
    dv = v.shape[-1]
    n = L // GLA_CHUNK

    def chunk(t):
        return t.reshape(B, n, GLA_CHUNK, H, t.shape[-1]).transpose(0, 3, 1, 2, 4)

    q, k, v, loga = chunk(q), chunk(k), chunk(v), chunk(loga)
    b = jnp.cumsum(loga, axis=3)
    b_last = b[:, :, :, -1:, :]
    q_dec = q * jnp.exp(b)
    k_inv = k * jnp.exp(-b)
    scores = jnp.einsum('bhncd,bhnsd->bhncs', q_dec, k_inv)
    mask = jnp.tril(jnp.ones((GLA_CHUNK, GLA_CHUNK), dtype=bool), -1 if strict else 0)
    scores = jnp.where(mask, scores, 0.0)
    o_intra = jnp.einsum('bhncs,bhnsv->bhncv', scores, v)

    chunk_kv = jnp.einsum('bhncd,bhncv->bhndv', k * jnp.exp(b_last - b), v)
    chunk_decay = jnp.exp(b_last[:, :, :, 0, :])

    def step(S, inp):
        dec, kv = inp
        return dec[..., None] * S + kv, S

    S0 = jnp.zeros((B, H, dk, dv), jnp.float32)
    _, S_prev = lax.scan(step, S0, (jnp.moveaxis(chunk_decay, 2, 0), jnp.moveaxis(chunk_kv, 2, 0)))
    S_prev = jnp.moveaxis(S_prev, 0, 2)
    o = o_intra + jnp.einsum('bhncd,bhndv->bhncv', q_dec, S_prev)
    return o.transpose(0, 2, 3, 1, 4).reshape(B, L, H, dv)

def gla_mixer(q_raw, k_raw, v_raw, g_raw, af_code, ab_code, wa_f, ba_f, wa_b, ba_b, norm_w):
    B, L, _ = q_raw.shape
    f32 = jnp.float32
    q = q_raw.astype(f32).reshape(B, L, GLA_HEADS, GLA_DK) * (GLA_DK ** -0.5)
    k = k_raw.astype(f32).reshape(B, L, GLA_HEADS, GLA_DK)
    v = v_raw.astype(f32).reshape(B, L, GLA_HEADS, GLA_DV)
    loga_f = (jax.nn.log_sigmoid((af_code @ wa_f + ba_f).astype(f32)) / GLA_TAU).reshape(B, L, GLA_HEADS, GLA_DK)
    loga_b = (jax.nn.log_sigmoid((ab_code @ wa_b + ba_b).astype(f32)) / GLA_TAU).reshape(B, L, GLA_HEADS, GLA_DK)
    flip = lambda t: jnp.flip(t, axis=1)
    o = gla_direction(q, k, v, loga_f, False) + flip(
        gla_direction(flip(q), flip(k), flip(v), flip(loga_b), True))
    o = o * lax.rsqrt(jnp.mean(o * o, axis=-1, keepdims=True) + EPS) * norm_w.astype(f32)
    o = o * jax.nn.silu(g_raw.astype(f32).reshape(B, L, GLA_HEADS, GLA_DV))
    return o.reshape(B, L, GLA_WIDTH)

def short_conv_centred(u, w, b):
    L = u.shape[1]
    half = HYENA_SHORT // 2
    up = jnp.pad(u, ((0, 0), (half, half), (0, 0)))
    y = b
    for j in range(HYENA_SHORT):
        y = y + up[:, j:j + L] * w[j]
    return y

def hyena_filters(L, w1, b1, fr1, w2, b2, fr2, w3):
    f32 = jnp.float32
    t = jnp.linspace(0.0, 1.0, L, dtype=f32)[:, None]
    w_pos = 2.0 * math.pi * jnp.arange(L, dtype=f32)[:, None] / L
    f = jnp.linspace(1e-4, HYENA_BANDS - 1, HYENA_BANDS, dtype=f32)[None]
    z = jnp.concatenate([t, jnp.cos(f * w_pos), -jnp.sin(f * w_pos)], axis=-1)
    hdn = jnp.sin(fr1.astype(f32) * (z @ w1.astype(f32) + b1.astype(f32)))
    hdn = jnp.sin(fr2.astype(f32) * (hdn @ w2.astype(f32) + b2.astype(f32)))
    h = hdn @ w3.astype(f32)
    deltas = jnp.abs(jnp.linspace(HYENA_MIN_DECAY, HYENA_MAX_DECAY, HYENA_WIDTH, dtype=f32))
    decay = jnp.exp(-t * deltas[None])
    h = h.reshape(L, HYENA_ORDER, 2, HYENA_WIDTH) * decay[:, None, None, :]
    return h.transpose(1, 2, 0, 3)

def bidir_long_conv(u, h_fwd, h_bwd, bias):
    L, W = h_fwd.shape
    n = 2 * L
    kern = jnp.concatenate([h_fwd, jnp.zeros((1, W), h_fwd.dtype), h_bwd[:0:-1]], axis=0)
    y = jnp.fft.irfft(jnp.fft.rfft(u, n=n, axis=1) * jnp.fft.rfft(kern, n=n, axis=0)[None],
                      n=n, axis=1)[:, :L]
    return y + u * bias

def hyena_mixer(u_raw, conv_w, conv_b, filt, bias):
    uc = short_conv_centred(u_raw, conv_w, conv_b).astype(jnp.float32)
    parts = jnp.split(uc, HYENA_ORDER + 1, axis=-1)
    z = parts[0]
    for o in range(HYENA_ORDER):
        z = parts[o + 1] * bidir_long_conv(z, filt[o, 0], filt[o, 1], bias[o].astype(jnp.float32))
    return z

def expert_choice_moe(h, w_router, w_gate, w_up, w_down):
    B, S, D = h.shape
    cap = EC_CAPACITY * S // N_EXPERTS
    probs = jax.nn.softmax((h @ w_router).astype(jnp.float32), axis=-1)
    gate, idx = lax.top_k(jnp.swapaxes(probs, 1, 2), cap)
    xg = jnp.take_along_axis(h, idx.reshape(B, N_EXPERTS * cap)[..., None], axis=1)
    xg = xg.reshape(B, N_EXPERTS, cap, D)
    hid = jax.nn.silu(jnp.einsum('becd,edf->becf', xg, w_gate)) * jnp.einsum('becd,edf->becf', xg, w_up)
    y = jnp.einsum('becf,efd->becd', hid, w_down) * gate[..., None].astype(h.dtype)
    flat_idx = (jnp.arange(B, dtype=jnp.int32)[:, None, None] * S + idx).reshape(-1)
    out = jax.ops.segment_sum(y.reshape(-1, D), flat_idx, num_segments=B * S)
    return out.reshape(B, S, D).astype(h.dtype)

def setup_inputs(seed: int = 0) -> dict:
    key = jax.random.key(seed)
    ks = jax.random.split(key, 32)
    f32 = jnp.float32

    def nrm(k, shape, scale):
        return jax.random.normal(k, shape, f32) * scale

    def gain(k, shape):
        return 1.0 + 0.02 * jax.random.normal(k, shape, f32)

    return {
        "x": nrm(ks[0], (BATCH, SEQ, D_MODEL), 1.0),
        "p": nrm(ks[1], (DEPTH, BATCH, SEQ, PLE_DIM), 1.0),
        "ln_mix_w": gain(ks[2], (DEPTH, D_MODEL)),
        "w_in": nrm(ks[3], (DEPTH, D_MODEL, IN_COLS), D_MODEL ** -0.5),
        "gla_wa_f": nrm(ks[4], (DEPTH, GLA_GATE_RANK, GLA_QK), GLA_GATE_RANK ** -0.5),
        "gla_ba_f": nrm(ks[5], (DEPTH, GLA_QK), 0.1),
        "gla_wa_b": nrm(ks[6], (DEPTH, GLA_GATE_RANK, GLA_QK), GLA_GATE_RANK ** -0.5),
        "gla_ba_b": nrm(ks[7], (DEPTH, GLA_QK), 0.1),
        "gla_norm_w": gain(ks[8], (DEPTH, GLA_DV)),
        "hy_conv_w": nrm(ks[9], (DEPTH, HYENA_SHORT, (HYENA_ORDER + 1) * HYENA_WIDTH), HYENA_SHORT ** -0.5),
        "hy_conv_b": nrm(ks[10], (DEPTH, (HYENA_ORDER + 1) * HYENA_WIDTH), 0.02),
        "hy_f_w1": nrm(ks[11], (DEPTH, HYENA_EMB, HYENA_FFN), HYENA_EMB ** -0.5),
        "hy_f_b1": nrm(ks[12], (DEPTH, HYENA_FFN), 0.02),
        "hy_f_freq1": gain(ks[13], (DEPTH, HYENA_FFN)),
        "hy_f_w2": nrm(ks[14], (DEPTH, HYENA_FFN, HYENA_FFN), HYENA_FFN ** -0.5),
        "hy_f_b2": nrm(ks[15], (DEPTH, HYENA_FFN), 0.02),
        "hy_f_freq2": gain(ks[16], (DEPTH, HYENA_FFN)),
        "hy_f_w3": nrm(ks[17], (DEPTH, HYENA_FFN, HYENA_ORDER * 2 * HYENA_WIDTH), 0.005),
        "hy_bias": nrm(ks[18], (DEPTH, HYENA_ORDER, HYENA_WIDTH), 0.1),
        "w_out": nrm(ks[19], (DEPTH, MIX_WIDTH, D_MODEL), MIX_WIDTH ** -0.5),
        "ln_ffn_w": gain(ks[20], (DEPTH, D_MODEL)),
        "w_router": nrm(ks[21], (DEPTH, D_MODEL, N_EXPERTS), D_MODEL ** -0.5),
        "w_gate_e": nrm(ks[22], (DEPTH, N_EXPERTS, D_MODEL, D_FF_EXPERT), D_MODEL ** -0.5),
        "w_up_e": nrm(ks[23], (DEPTH, N_EXPERTS, D_MODEL, D_FF_EXPERT), D_MODEL ** -0.5),
        "w_down_e": nrm(ks[24], (DEPTH, N_EXPERTS, D_FF_EXPERT, D_MODEL), D_FF_EXPERT ** -0.5),
        "ln_ple_w": gain(ks[25], (DEPTH, D_MODEL)),
        "w_ple_gate": nrm(ks[26], (DEPTH, D_MODEL, D_MODEL), D_MODEL ** -0.5),
        "w_ple_proj": nrm(ks[27], (DEPTH, PLE_DIM, D_MODEL), PLE_DIM ** -0.5),
        "final_norm_w": gain(ks[28], (D_MODEL,)),
    }

def reference(x, p, ln_mix_w, w_in, gla_wa_f, gla_ba_f, gla_wa_b, gla_ba_b, gla_norm_w,
              hy_conv_w, hy_conv_b, hy_f_w1, hy_f_b1, hy_f_freq1, hy_f_w2, hy_f_b2, hy_f_freq2,
              hy_f_w3, hy_bias, w_out, ln_ffn_w, w_router, w_gate_e, w_up_e, w_down_e,
              ln_ple_w, w_ple_gate, w_ple_proj, final_norm_w):
    L = x.shape[1]
    split_idx = []
    acc = 0
    for s in IN_SIZES[:-1]:
        acc += s
        split_idx.append(acc)

    r = x
    for i in range(DEPTH):
        h = rmsnorm(r, ln_mix_w[i])
        proj = h @ w_in[i]
        q_raw, k_raw, v_raw, g_raw, af_code, ab_code, hy_raw = jnp.split(proj, split_idx, axis=-1)
        gla_out = gla_mixer(q_raw, k_raw, v_raw, g_raw, af_code, ab_code,
                            gla_wa_f[i], gla_ba_f[i], gla_wa_b[i], gla_ba_b[i], gla_norm_w[i])
        filt = hyena_filters(L, hy_f_w1[i], hy_f_b1[i], hy_f_freq1[i],
                             hy_f_w2[i], hy_f_b2[i], hy_f_freq2[i], hy_f_w3[i])
        hy_out = hyena_mixer(hy_raw, hy_conv_w[i], hy_conv_b[i], filt, hy_bias[i])
        mixed = jnp.concatenate([gla_out, hy_out], axis=-1).astype(r.dtype)
        r = r + mixed @ w_out[i]
        r = r + expert_choice_moe(rmsnorm(r, ln_ffn_w[i]), w_router[i],
                                  w_gate_e[i], w_up_e[i], w_down_e[i])
        gate = jax.nn.sigmoid(rmsnorm(r, ln_ple_w[i]) @ w_ple_gate[i])
        r = r + gate * (p[i] @ w_ple_proj[i])
    return rmsnorm(r, final_norm_w)


_drawn_inputs = setup_inputs


def setup_inputs(seed=0):
    import zlib

    import numpy as np

    out = dict(_drawn_inputs(seed))
    spreads = {}
    factors = {'ln_mix_w': 2.825,
     'gla_ba_f': 3.637,
     'gla_ba_b': 3.605,
     'gla_norm_w': 4.978,
     'hy_conv_b': 5.015,
     'hy_f_b1': 8.0,
     'hy_f_freq1': 8.0,
     'hy_f_b2': 8.0,
     'hy_f_freq2': 8.0,
     'hy_bias': 2.667,
     'ln_ffn_w': 4.479,
     'ln_ple_w': 8.0,
     'final_norm_w': 2.74}
    for name, (base, spread) in spreads.items():
        noise = np.random.default_rng([zlib.crc32(name.encode()), seed]).standard_normal(out[name].shape)
        drawn = base * np.exp(spread * noise) if base else spread * noise
        out[name] = __import__('jax').numpy.asarray(drawn.astype(out[name].dtype))
    for name, factor in factors.items():
        out[name] = (out[name] * factor).astype(out[name].dtype)
    return out
```

```python
from contextlib import ExitStack
import math

import numpy as np
import concourse.bass as bass
from concourse import mybir

ALU = mybir.AluOpType
ACT = mybir.ActivationFunctionType
AX_X = mybir.AxisListType.X
F32 = mybir.dt.float32
F32R = mybir.dt.float32r
I32 = mybir.dt.int32

P = 128
D = 1024
L = 1024
DT = D // P
TT = L // P
EPS = 1e-6
HEADS, DK, DV = 4, D // 16, D // 8
QK, GW, RANK = HEADS * DK, HEADS * DV, 16
TAU = 16.0
HW = D - GW
ORDER, FFN, BANDS = 2, 64, 8
EMB = 1 + 2 * BANDS
NE = 16
CAP = 2 * L // NE
FF = 2 * D
PLE = 256
Q0, K0, V0, G0 = 0, QK, 2 * QK, 2 * QK + GW
C0 = G0 + GW
H0 = C0 + 2 * RANK
IN_COLS = H0 + 3 * HW

NFFT = 2 * L
HALF = HW // 2
GROUPS = 8
RESIDUES = [(0, 0), (4, -1), (2, -1), (6, 1), (1, -1), (9, -1), (5, -1), (13, -1)]
C45 = math.cos(math.pi / 4)
C22 = math.cos(math.pi / 8)
T22 = math.tan(math.pi / 8)


def shape_constants():
    p = np.arange(P, dtype=np.float64)[:, None]
    j = np.arange(P, dtype=np.float64)[None, :]
    fwd = np.zeros((GROUPS, 4, P, P))
    weight = np.full((GROUPS, 2, P), 2.0 / NFFT)
    for g, (r, s) in enumerate(RESIDUES):
        if g == 0:
            for part, r0 in ((0, 0), (1, 8)):
                th = 2 * np.pi * p * (r0 + 16 * j[:, :64]) / NFFT
                fwd[0, part, :, 64 * part:64 * part + 64] = np.cos(th)
                fwd[0, 2 + part, :, 64 * part:64 * part + 64] = -np.sin(th)
            fwd[0, 2, :, 0] = (-1.0) ** np.arange(P)
            weight[0, :, 0] = 1.0 / NFFT
        else:
            th = 2 * np.pi * p * (r + 16 * j) / NFFT
            mr, mi = np.cos(th), -np.sin(th)
            fwd[g, 0], fwd[g, 1] = mr, -mi * s
            fwd[g, 2], fwd[g, 3] = mi, mr * s
    inv = np.zeros((GROUPS, 4, P, P))
    for g in range(GROUPS):
        for q in range(4):
            inv[g, q] = fwd[g, q].T * weight[g, q // 2][:, None]
    f32 = np.float32
    t = np.linspace(0.0, 1.0, L, dtype=f32)[:, None]
    w_pos = (f32(2.0 * math.pi) * np.arange(L, dtype=f32)[:, None] / f32(L)).astype(f32)
    f = np.linspace(1e-4, BANDS - 1, BANDS, dtype=f32)[None]
    z = np.concatenate([t, np.cos(f * w_pos), -np.sin(f * w_pos)], axis=-1).astype(f32)
    lo, hi = math.log(1e-2) / 1.5, math.log(1e-2) / 0.3
    deltas = np.abs(np.linspace(lo, hi, HW, dtype=f32))
    decay = np.exp(-t * deltas[None]).astype(f32)
    s_idx, t_idx = np.arange(P)[:, None], np.arange(P)[None, :]
    same = (s_idx // 64) == (t_idx // 64)
    masks = np.stack([same & (s_idx <= t_idx), same & (s_idx > t_idx)], 1).astype(np.int32)
    return {
        "c_fwd": np.ascontiguousarray(fwd.transpose(2, 0, 1, 3).reshape(P, -1).astype(f32)),
        "c_inv": np.ascontiguousarray(inv.transpose(2, 0, 1, 3).reshape(P, -1).astype(f32)),
        "c_z": np.ascontiguousarray(z.T),
        "c_decay": decay,
        "c_ident": np.eye(P, dtype=f32),
        "c_mask": np.ascontiguousarray(masks),
        "c_iota": np.tile(np.arange(P, dtype=f32)[None], (P, 1)),
        "c_tok": np.ascontiguousarray(np.arange(L, dtype=f32).reshape(TT, P).T),
        "c_lower": (s_idx > t_idx).astype(f32),
        "c_sel": np.ascontiguousarray(np.repeat(np.eye(NE, dtype=f32)[:, :, None], P, 2).reshape(NE, NE * P)),
    }


def raise_counts():
    raised = {}

    def one(sem):
        raised[sem] = raised.get(sem, 0) + 1
        return 1

    def so_far(sem):
        return raised.get(sem, 0)

    return one, so_far


def nothing():
    pass


def forward_tree(dve, own, one, so_far, U, V, T, tree_done, between={}):
    s, d, pp, m, A, B, x1, x3 = (T[:, a:b, :] for a, b in
                                 ((0, 4), (4, 8), (8, 10), (10, 12), (12, 14), (14, 16), (16, 18), (18, 20)))
    add, sub, mul = ALU.add, ALU.subtract, ALU.mult
    dve.tensor_tensor(s, U[:, 0:4, :], U[:, 4:8, :], add).then_inc(own, one(own))
    dve.tensor_tensor(d, U[:, 0:4, :], U[:, 4:8, :], sub).then_inc(own, one(own))
    dve.scalar_tensor_tensor(out=x1[:, 0, :], in0=U[:, 5, :], scalar=-T22, in1=U[:, 1, :], op0=mul, op1=add).then_inc(own, one(own))
    dve.scalar_tensor_tensor(out=x1[:, 1, :], in0=U[:, 1, :], scalar=T22, in1=U[:, 5, :], op0=mul, op1=add).then_inc(own, one(own))
    dve.scalar_tensor_tensor(out=x3[:, 0, :], in0=U[:, 3, :], scalar=T22, in1=U[:, 7, :], op0=mul, op1=sub).then_inc(own, one(own))
    dve.scalar_tensor_tensor(out=x3[:, 1, :], in0=U[:, 7, :], scalar=T22, in1=U[:, 3, :], op0=mul, op1=add).then_inc(own, one(own))
    between.get(0, nothing)()
    dve.wait_ge(own, so_far(own))
    dve.tensor_tensor(pp, s[:, 0:2, :], s[:, 2:4, :], add).then_inc(own, one(own))
    dve.tensor_tensor(V[:, 2:4, :], s[:, 0:2, :], s[:, 2:4, :], sub).then_inc(own, one(own))
    dve.tensor_tensor(m[:, 0, :], d[:, 1, :], d[:, 3, :], sub).then_inc(own, one(own))
    dve.tensor_tensor(m[:, 1, :], d[:, 1, :], d[:, 3, :], add).then_inc(own, one(own))
    ds = T[:, 6:1:-4, :]
    u04 = U[:, 0:5:4, :]
    dve.scalar_tensor_tensor(out=A, in0=ds, scalar=C45, in1=u04, op0=mul, op1=add).then_inc(own, one(own))
    dve.scalar_tensor_tensor(out=B, in0=ds, scalar=-C45, in1=u04, op0=mul, op1=add).then_inc(own, one(own))
    between.get(1, nothing)()
    dve.wait_ge(own, so_far(own))
    dve.tensor_tensor(V[:, 0, :], pp[:, 0, :], pp[:, 1, :], add).then_inc(own, one(own))
    dve.tensor_tensor(V[:, 1, :], pp[:, 0, :], pp[:, 1, :], sub).then_inc(own, one(own))
    d02 = T[:, 4:7:2, :]
    dve.scalar_tensor_tensor(out=V[:, 4:6, :], in0=m, scalar=C45, in1=d02, op0=mul, op1=add).then_inc(own, one(own))
    dve.scalar_tensor_tensor(out=V[:, 6:8, :], in0=m, scalar=-C45, in1=d02, op0=mul, op1=add).then_inc(own, one(own))
    Cc, Dd = T[:, 0:2, :], T[:, 2:4, :]
    dve.tensor_tensor(Cc, x1, x3, add).then_inc(own, one(own))
    dve.tensor_tensor(Dd, x1, x3, sub).then_inc(own, one(own))
    between.get(2, nothing)()
    dve.wait_ge(own, so_far(own))
    dve.scalar_tensor_tensor(out=V[:, 8:10, :], in0=Cc, scalar=C22, in1=A, op0=mul, op1=add).then_inc(own, one(own))
    dve.scalar_tensor_tensor(out=V[:, 10:12, :], in0=Cc, scalar=-C22, in1=A, op0=mul, op1=add).then_inc(own, one(own))
    Dnr, Bnr = T[:, 3:1:-1, :], T[:, 15:13:-1, :]
    dve.scalar_tensor_tensor(out=V[:, 13:15, :], in0=Dd, scalar=C22, in1=Bnr, op0=mul, op1=add).then_inc(own, one(own))
    dve.scalar_tensor_tensor(out=V[:, 12:16:3, :], in0=Dnr, scalar=-C22, in1=B, op0=mul, op1=add).then_inc(tree_done, one(tree_done))


def newton(dve, own, one, so_far, rs):
    v, r, u = rs[:, 0, :], rs[:, 2, :], rs[:, 3, :]
    dve.wait_ge(own, so_far(own))
    dve.tensor_tensor(u, r, r, ALU.mult).then_inc(own, one(own))
    dve.wait_ge(own, so_far(own))
    dve.tensor_tensor(u, u, v, ALU.mult).then_inc(own, one(own))
    dve.wait_ge(own, so_far(own))
    dve.tensor_scalar(u, u, -0.5, 1.5, ALU.mult, ALU.add).then_inc(own, one(own))
    dve.wait_ge(own, so_far(own))
    dve.tensor_tensor(r, r, u, ALU.mult).then_inc(own, one(own))
    dve.wait_ge(own, so_far(own))


def project_stage(nc, dram, scratch, tile_loaded):
    WC = 256
    WB = 2
    with ExitStack() as ctx:
        sb = lambda name, shape, dt=F32: ctx.enter_context(nc.sbuf_tensor(name, shape, dt))
        sem = lambda name: ctx.enter_context(nc.semaphore(name))
        x_sb = sb("x_sb", [P, TT, D])
        V = x_sb[:].rearrange("p t (a c) -> p (t a) c", c=HALF).rearrange("p (b s) c -> p b s c", b=2)
        hT = sb("hT", [P, DT, L])
        w_sb = sb("w_sb", [P, WB, DT, WC])
        fwd = sb("fwd", [P, GROUPS, 4, P])
        ident = sb("ident", [P, P])
        lnw = sb("lnw", [P, DT])
        ssq = sb("ssq", [P, TT])
        rstd = sb("rstd", [P, 4, TT])
        cw = sb("cw", [P, 3, 12])
        cb = sb("cb", [P, 12])
        tap = sb("tap", [P, 2, L])
        zT = sb("zT", [EMB, L])
        fw1 = sb("fw1", [EMB, FFN])
        fw2 = sb("fw2", [FFN, FFN])
        fcol = sb("fcol", [FFN, 4])
        w3 = sb("w3", [FFN, ORDER, 2, HW])
        w3eo = sb("w3eo", [FFN, 2, ORDER, HW])
        arg = sb("arg", [FFN, L])
        red = sb("red", [FFN, L])
        hdn1 = red
        hdn2 = sb("hdn2", [FFN, L])
        hbias = sb("hbias", [1, ORDER, HW])
        row0 = hbias
        decay = sb("decay", [P, TT, HALF])
        eo = sb("eo", [P, TT, HALF])
        T = sb("T", [P, 20, HALF])
        spec = sb("spec", [P, GROUPS, 2, HALF])
        nyq = sb("nyq", [1, HALF])
        stage = sb("stage", [P, 2, L])
        acc = ctx.enter_context(nc.psum_tensor("acc", [P, 2, L], F32))
        psA = ctx.enter_context(nc.psum_tensor("psA", [P, 2, 512], F32))
        psB = ctx.enter_context(nc.psum_tensor("psB", [P, 2, 512], F32))

        s_x = tile_loaded
        s_small = sem("small_loaded")
        s_tab = sem("tables_loaded")
        s_filt = sem("filter_weights_loaded")
        s_decay = sem("decay_loaded")
        s_w = [sem(f"w_loaded{i}") for i in range(WB)]
        own_dve, own_act = sem("own_dve"), sem("own_act")
        s_ssq = sem("squares_summed")
        s_var = sem("variance_ready")
        s_root = sem("root_ready")
        s_xs = sem("x_scaled")
        s_pt = sem("h_transposed")
        s_ht = sem("hT_ready")
        s_pre = sem("filter_preact")
        s_arg = sem("filter_arg_reduced")
        s_hdn = sem("filter_hidden")
        s_w3 = sem("w3_combined")
        s_row = sem("row0_product")
        s_row0 = sem("row0_ready")
        s_acc = sem("acc_done")
        s_gen = sem("filter_product")
        s_genu = sem("filter_taken")
        s_tree = sem("kernel_tree_done")
        s_spec = sem("spectrum_product")
        s_specw = sem("spectrum_staged")
        s_specs = sem("spectrum_stored")
        s_tap0 = sem("centre_tap")
        s_conv = sem("conv_done")
        s_stage = sem("stage_filled")
        s_store = [sem(f"stage_stored{i}") for i in range(2)]

        HY = 3 * HW // P
        tiles = [("h", j, H0 + P * j, P) for j in range(HY)] + [("c", 0, C0, 2 * RANK)]
        tiles += [("qk", j, Q0 + P * j, P) for j in range(2 * QK // P)]
        tiles += [("vg", (c, th), V0 + WC * c, WC) for c in range(2 * GW // WC) for th in range(2)]
        wgroups = []
        for kind, _, col, n in tiles:
            if kind in ("h", "qk"):
                if (col - (H0 if kind == "h" else 0)) % WC == 0:
                    wgroups.append((col, WC))
            elif not wgroups or wgroups[-1][0] != col:
                wgroups.append((col, n))

        def group_of(col):
            for i, (c, n) in enumerate(wgroups):
                if c <= col < c + n:
                    return i

        last_tile = {group_of(t[2]): i for i, t in enumerate(tiles)}
        rounds = [(h, o, eopart) for h in range(2) for o in range(ORDER) for eopart in range(2)]

        def taken(i):
            m = min(i // 2, len(rounds))
            return 2 * DT + 2 * (i + 1) + 4 * m + (m + 1) // 2

        with nc.Block() as block:
            @block.sync
            def _(sp):
                sp.dma_start(ident[:], dram["c_ident"]).then_inc(s_small, 16)
                sp.dma_start(lnw[:], dram["l_ln_mix"]).then_inc(s_small, 16)
                for t in range(TT):
                    sp.dma_start(x_sb[:, t, :], dram["x"][0, P * t:P * t + P, :]).then_inc(s_x[t], 16)
                sp.dma_start(zT[:], dram["c_z"]).then_inc(s_filt, 16)
                sp.dma_start(fw1[:], dram["hy_f_w1"][0]).then_inc(s_filt, 16)
                sp.dma_start(fw2[:], dram["hy_f_w2"][0]).then_inc(s_filt, 16)
                sp.dma_start(fcol[:], dram["l_filter"]).then_inc(s_filt, 16)
                sp.dma_start(w3[:], dram["hy_f_w3"][0].rearrange("k (o d c) -> k o d c", o=ORDER, d=2)).then_inc(s_filt, 16)
                sp.dma_start(hbias[:], dram["hy_bias"]).then_inc(s_filt, 16)
                for i, (c, n) in enumerate(wgroups):
                    if i >= WB:
                        sp.wait_ge(s_acc, last_tile[i - WB] + 1)
                    sp.dma_start(w_sb[:, i % WB, :, 0:n],
                                 dram["w_in"][0, :, c:c + n].rearrange("(k p) n -> p k n", p=P)).then_inc(s_w[i % WB], 16)
                    if i == 0:
                        sp.dma_start(cw[:], dram["l_conv_w"]).then_inc(s_tab, 16)
                        sp.dma_start(cb[:], dram["l_conv_b"]).then_inc(s_tab, 16)
                        sp.dma_start(fwd[:], dram["c_fwd"].rearrange("p (g q c) -> p g q c", g=GROUPS, q=4)).then_inc(s_tab, 16)
                        sp.dma_start(decay[:], dram["c_decay"][:, 0:HALF].rearrange("(a p) c -> p a c", p=P)).then_inc(s_decay, 16)
                    if i == 5:
                        sp.wait_ge(s_genu, 4 * 4)
                        sp.dma_start(decay[:], dram["c_decay"][:, HALF:HW].rearrange("(a p) c -> p a c", p=P)).then_inc(s_decay, 16)

            @block.gpsimd
            def _(pool):
                sent = 0
                for i, (kind, j, col, n) in enumerate(tiles):
                    if kind == "h":
                        pool.wait_ge(s_ht, taken(i))
                    else:
                        pool.wait_ge(s_stage, i + 1 - HY)
                    src = stage[:, i % 2, :]
                    if kind == "h":
                        dst = scratch["hy"][j * P // HW, :, (j * P) % HW:(j * P) % HW + P].rearrange("(a p) c -> p a c", p=P)
                        src = src.rearrange("p (a c) -> p a c", c=P)
                    elif kind == "c":
                        dst, src = scratch["code"][:], stage[0:2 * RANK, i % 2, :]
                    elif kind == "qk":
                        dst = scratch["qk"][j]
                    else:
                        c, th = j
                        dst = scratch["vg"][c // 2, 512 * th:512 * th + 512, WC * (c % 2):WC * (c % 2) + WC].rearrange("(a p) c -> p a c", p=P)
                        src = src.rearrange("p (a c) -> p a c", c=WC)
                    pool.dma_start(dst, src).then_inc(s_store[i % 2], 16)
                    if i % 4 == 3 and sent < len(rounds) // 2:
                        h, o, _ = rounds[2 * sent]
                        pool.wait_ge(s_specw, sent + 1)
                        pool.dma_start(scratch["spec"][o, h], spec[:]).then_inc(s_specs, 16)
                        sent += 1
                assert sent == len(rounds) // 2
                pool.wait_ge(s_store[0], 16 * ((len(tiles) + 1) // 2))
                pool.wait_ge(s_store[1], 16 * (len(tiles) // 2))
                pool.wait_ge(s_specs, 16 * sent)

            @block.tensor
            def _(pe):
                pe.wait_ge(s_filt, 16 * 6)
                for c in range(2):
                    pe.matmul(psB[0:FFN, c, :], fw1[:], zT[:, 512 * c:512 * c + 512], start=True, stop=True).then_inc(s_pre, 1)
                pe.wait_ge(s_small, 32)
                for b in range(2 * DT):
                    dt, th = b % DT, b // DT
                    if dt == 0:
                        pe.wait_ge(s_xs, 4 * th + 4)
                    if b >= 2:
                        pe.wait_ge(s_ht, b - 1)
                    for t in range(4):
                        m = pe.transpose(psA[:, b % 2, P * t:P * t + P], x_sb[:, 4 * th + t, P * dt:P * dt + P], ident[:])
                    m.then_inc(s_pt, 1)
                pe.wait_ge(s_hdn, 1)
                for c in range(2):
                    pe.matmul(psB[0:FFN, c, :], fw2[:], hdn1[:, 512 * c:512 * c + 512], start=True, stop=True).then_inc(s_pre, 1)
                pe.wait_ge(s_hdn, 2)
                for o in range(ORDER):
                    pe.matmul(psB[0:1, o, :], hdn2[:, 0:1], w3[:, o, 0, :], start=True, stop=True).then_inc(s_row, 1)
                pe.wait_ge(s_w3, 2)
                pe.wait_ge(s_row0, 1)

                def gen(r, chunks):
                    h, o, part = rounds[r]
                    for c in chunks:
                        n = 4 * r + c
                        if n >= 2:
                            pe.wait_ge(s_genu, n - 1)
                        for a in (2 * c, 2 * c + 1):
                            m = pe.matmul(psB[:, n % 2, HALF * (a % 2):HALF * (a % 2) + HALF], hdn2[:, P * a:P * a + P],
                                          w3eo[:, part, o, HALF * h:HALF * h + HALF], start=True, stop=True)
                        m.then_inc(s_gen, 1)

                used = [2 * DT]

                def spectrum(r):
                    h, o, part = rounds[r]
                    pe.wait_ge(s_tree, r + 1)
                    Vr = V[:, r % 2]
                    for c in range(4):
                        pe.wait_ge(s_ht, used[0] - 1)
                        for g in (2 * c, 2 * c + 1):
                            dst = psA[:, used[0] % 2, HALF * (g % 2):HALF * (g % 2) + HALF]
                            for q in range(2):
                                m = pe.matmul(dst, fwd[:, g, 2 * part + q, :], Vr[:, 2 * g + q, :], start=(q == 0), stop=(q == 1))
                        m.then_inc(s_pt, 1)
                        used[0] += 1
                    if part == 0:
                        pe.wait_ge(s_ht, used[0] - 1)
                        pe.matmul(psA[0:1, used[0] % 2, 0:HALF], fwd[:, 0, 2, 0:1], Vr[:, 0, :], start=True, stop=True).then_inc(s_pt, 1)
                        used[0] += 1

                def transposes(i):
                    pe.wait_ge(s_conv, i + 1)
                    for c in range(2):
                        pe.wait_ge(s_ht, used[0] - 1)
                        for a in range(4):
                            t = 4 * c + a
                            m = pe.transpose(psA[:, used[0] % 2, P * a:P * a + P], tap[:, i % 2, P * t:P * t + P], ident[:])
                        m.then_inc(s_pt, 1)
                        used[0] += 1

                pe.wait_ge(s_ht, 2 * DT)
                for i, (kind, j, col, n) in enumerate(tiles):
                    gi = group_of(col)
                    pe.wait_ge(s_w[gi % WB], 16 * (gi // WB + 1))
                    w = w_sb[:, gi % WB]
                    off = col - wgroups[gi][0]
                    if i >= 2:
                        if i - 2 < HY:
                            pe.wait_ge(s_conv, i - 1)
                        else:
                            pe.wait_ge(s_stage, i - 1 - HY)
                    if kind == "vg":
                        for tt in range(4):
                            tok = 4 * j[1] + tt
                            for k in range(DT):
                                m = pe.matmul(acc[:, i % 2, WC * tt:WC * tt + WC], hT[:, k, P * tok:P * tok + P], w[:, k, :],
                                              start=(k == 0), stop=(k == DT - 1))
                    else:
                        for c in range(2):
                            for k in range(DT):
                                m = pe.matmul(acc[0:n, i % 2, 512 * c:512 * c + 512], w[:, k, off:off + n],
                                              hT[:, k, 512 * c:512 * c + 512], start=(k == 0), stop=(k == DT - 1))
                    m.then_inc(s_acc, 1)
                    if i == 0:
                        pe.wait_ge(s_tab, 16 * 3)
                    if 1 <= i <= HY:
                        transposes(i - 1)
                    r = i // 2
                    if i % 2 == 0 and 1 <= r <= len(rounds):
                        spectrum(r - 1)
                    if r < len(rounds):
                        gen(r, (0, 1) if i % 2 == 0 else (2, 3))

            @block.vector
            def _(dve):
                one, so_far = raise_counts()

                def reduce_arg(layer):
                    for c in range(2):
                        dve.wait_ge(s_pre, 2 * layer + c + 1)
                        dve.tensor_scalar(arg[:, 512 * c:512 * c + 512], psB[0:FFN, c, :], fcol[:, 2 * layer:2 * layer + 1],
                                                   fcol[:, 2 * layer + 1:2 * layer + 2], ALU.add, ALU.mult).then_inc(own_dve, one(own_dve))
                    dve.wait_ge(own_dve, so_far(own_dve))
                    big = 1.5 * 2.0 ** 23
                    dve.tensor_scalar(red[:], arg[:], 1.0 / (2 * math.pi), big, ALU.mult, ALU.add).then_inc(own_dve, one(own_dve))
                    dve.wait_ge(own_dve, so_far(own_dve))
                    dve.tensor_scalar(red[:], red[:], big, None, ALU.subtract).then_inc(own_dve, one(own_dve))
                    dve.wait_ge(own_dve, so_far(own_dve))
                    two_pi_hi = 6.28125
                    for part in (two_pi_hi, 2 * math.pi - two_pi_hi):
                        dve.scalar_tensor_tensor(out=arg[:], in0=red[:], scalar=-part, in1=arg[:], op0=ALU.mult, op1=ALU.add).then_inc(own_dve, one(own_dve))
                        dve.wait_ge(own_dve, so_far(own_dve))
                    edge = float(np.nextafter(np.float32(math.pi), np.float32(0)))
                    dve.tensor_scalar(arg[:], arg[:], edge, -edge, ALU.min, ALU.max).then_inc(s_arg, one(s_arg))

                dve.wait_ge(s_filt, 16 * 6)
                reduce_arg(0)
                for part, op in ((0, ALU.add), (1, ALU.subtract)):
                    dve.tensor_tensor(w3eo[:, part], w3[:, :, 0, :], w3[:, :, 1, :], op).then_inc(s_w3, one(s_w3))
                dve.wait_ge(s_ssq, TT)
                dve.wait_ge(s_w3, so_far(s_w3))
                dve.tensor_scalar(rstd[:, 0, :], ssq[:], 1.0 / D, EPS, ALU.mult, ALU.add).then_inc(s_var, one(s_var))
                dve.wait_ge(s_root, 1)
                dve.reciprocal(rstd[:, 2, :], rstd[:, 1, :]).then_inc(own_dve, one(own_dve))
                dve.wait_ge(own_dve, so_far(own_dve))
                newton(dve, own_dve, one, so_far, rstd)
                for t in range(TT):
                    dve.tensor_scalar(x_sb[:, t, :], x_sb[:, t, :], rstd[:, 2, t:t + 1], None, ALU.mult).then_inc(s_xs, one(s_xs))
                dve.wait_ge(s_hdn, 1)
                reduce_arg(1)
                dve.wait_ge(s_row, 2)
                dve.wait_ge(s_arg, so_far(s_arg))
                dve.tensor_tensor(row0[:], psB[0:1, :, :], hbias[:], ALU.add).then_inc(s_row0, one(s_row0))

                def conv(i):
                    dve.wait_ge(s_tap0, i + 1)
                    t, a = tap[:, i % 2, :], acc[:, i % 2, :]
                    dve.scalar_tensor_tensor(out=t[:, 1:L], in0=a[:, 0:L - 1], scalar=cw[:, 0, i:i + 1], in1=t[:, 1:L],
                                                      op0=ALU.mult, op1=ALU.add).then_inc(own_dve, one(own_dve))
                    dve.wait_ge(own_dve, so_far(own_dve))
                    dve.scalar_tensor_tensor(out=t[:, 0:L - 1], in0=a[:, 1:L], scalar=cw[:, 2, i:i + 1], in1=t[:, 0:L - 1],
                                                        op0=ALU.mult, op1=ALU.add).then_inc(s_conv, one(s_conv))

                def take(r, chunks):
                    h, o, part = rounds[r]
                    dve.wait_ge(s_decay, 16 * (h + 1))
                    if so_far(s_conv):
                        dve.wait_ge(s_conv, so_far(s_conv))
                    if so_far(s_tree):
                        dve.wait_ge(s_tree, so_far(s_tree))
                    if so_far(s_genu):
                        dve.wait_ge(s_genu, so_far(s_genu))
                    for c in chunks:
                        dve.wait_ge(s_gen, 4 * r + c + 1)
                        dve.tensor_tensor(eo[:, 2 * c:2 * c + 2, :], psB[:, (4 * r + c) % 2, :].rearrange("p (a c) -> p a c", a=2),
                                                     decay[:, 2 * c:2 * c + 2, :], ALU.mult).then_inc(s_genu, one(s_genu))

                for i in range(2 * len(rounds)):
                    r = i // 2
                    if i < HY:
                        conv(i)
                    if i % 2 == 0:
                        take(r, (0, 1))
                    else:
                        h, o, part = rounds[r]
                        take(r, (2, 3))
                        dve.wait_ge(s_genu, so_far(s_genu))
                        if part == 0:
                            dve.tensor_copy(eo[0:1, 0, :], row0[0:1, o, HALF * h:HALF * h + HALF]).then_inc(own_dve, one(own_dve))
                        if so_far(own_dve):
                            dve.wait_ge(own_dve, so_far(own_dve))
                        if so_far(s_genu):
                            dve.wait_ge(s_genu, so_far(s_genu))
                        forward_tree(dve, own_dve, one, so_far, eo[:], V[:, r % 2], T[:], s_tree)

            @block.scalar
            def _(act):
                one, so_far = raise_counts()
                for t in range(TT):
                    act.wait_ge(s_x[t], 16)
                    if so_far(s_ssq):
                        act.wait_ge(s_ssq, so_far(s_ssq))
                    act.activation(acc[:, 0, :], x_sb[:, t, :], ACT.Square, accum_out=ssq[:, t:t + 1]).then_inc(s_ssq, one(s_ssq))
                act.wait_ge(s_var, 1)
                act.activation(rstd[:, 1, :], rstd[:, 0, :], ACT.Sqrt).then_inc(s_root, 1)
                act.wait_ge(s_arg, 1)
                act.activation(hdn1[:], arg[:], ACT.Sin).then_inc(s_hdn, 1)
                used = [0]

                def take(dst, src, **kw):
                    act.wait_ge(s_pt, used[0] + 1)
                    used[0] += 1
                    act.activation(dst, src, ACT.Identity, **kw).then_inc(s_ht, one(s_ht))

                act.wait_ge(s_small, 32)
                for b in range(2 * DT):
                    dt, th = b % DT, b // DT
                    take(hT[:, dt, 512 * th:512 * th + 512], psA[:, b % 2, :], scale=lnw[:, dt:dt + 1])
                act.wait_ge(s_arg, 2)
                act.activation(hdn2[:], arg[:], ACT.Sin).then_inc(s_hdn, 1)
                act.wait_ge(s_tab, 16 * 3)

                def spectrum(r):
                    h, o, part = rounds[r]
                    if part == 0 and r >= 2:
                        act.wait_ge(s_specs, 16 * (r // 2))
                    for c in range(4):
                        take(spec[:, 2 * c:2 * c + 2, part, :], psA[:, used[0] % 2, :].rearrange("p (g c) -> p g c", g=2))
                    if part == 0:
                        take(nyq[:], psA[0:1, used[0] % 2, 0:HALF])
                    else:
                        act.wait_ge(s_ht, so_far(s_ht))
                        act.activation(spec[0:1, 0, 1, :], nyq[:], ACT.Identity).then_inc(s_specw, one(s_specw))

                def stage_free(i):
                    if i >= 2:
                        act.wait_ge(s_store[i % 2], 16 * (i // 2))

                for i, (kind, j, col, n) in enumerate(tiles):
                    act.wait_ge(s_acc, i + 1)
                    if kind == "h":
                        act.activation(tap[:, i % 2, :], acc[:, i % 2, :], ACT.Identity, scale=cw[:, 1, i:i + 1], bias=cb[:, i:i + 1]).then_inc(s_tap0, one(s_tap0))
                    if 1 <= i <= HY:
                        stage_free(i - 1)
                        take(stage[:, (i - 1) % 2, 0:512], psA[:, used[0] % 2, :])
                        take(stage[:, (i - 1) % 2, 512:1024], psA[:, used[0] % 2, :])
                    if kind != "h":
                        stage_free(i)
                        scale = DK ** -0.5 if kind == "qk" and col < K0 else 1.0
                        act.activation(stage[0:min(n, P), i % 2, :], acc[0:min(n, P), i % 2, :], ACT.Identity, scale=scale).then_inc(s_stage, one(s_stage))
                    r = i // 2
                    if i % 2 == 0 and 1 <= r <= len(rounds):
                        spectrum(r - 1)


def inverse_tree(dve, own, one, so_far, Z, Y, X, T, done, between={}):
    add, sub, mul = ALU.add, ALU.subtract, ALU.mult
    tt, stt = dve.tensor_tensor, dve.scalar_tensor_tensor
    G, Cc, Bh, Dd, dq, m, pp, x1, x3, w = (T[:, 2 * i:2 * i + 2, :] for i in range(10))
    tt(G, Z[:, 8:10, :], Z[:, 10:12, :], add).then_inc(own, one(own))
    tt(Cc, Z[:, 8:10, :], Z[:, 10:12, :], sub).then_inc(own, one(own))
    tt(Bh, Z[:, 12:14, :], Z[:, 14:16, :], add).then_inc(own, one(own))
    tt(Dd, Z[:, 13:15, :], Z[:, 15:11:-3, :], sub).then_inc(own, one(own))
    tt(dq, Z[:, 4:6, :], Z[:, 6:8, :], add).then_inc(own, one(own))
    tt(m, Z[:, 4:6, :], Z[:, 6:8, :], sub).then_inc(own, one(own))
    tt(pp[:, 0, :], Z[:, 0, :], Z[:, 1, :], add).then_inc(own, one(own))
    tt(pp[:, 1, :], Z[:, 0, :], Z[:, 1, :], sub).then_inc(own, one(own))
    between.get(0, nothing)()
    dve.wait_ge(own, so_far(own))
    tt(x1, Cc, Dd, add).then_inc(own, one(own))
    tt(x3, Cc, Dd, sub).then_inc(own, one(own))
    tt(w, G, Bh, add).then_inc(own, one(own))
    tt(Y[:, 0:3:2, :], pp, Z[:, 2:4, :], add).then_inc(own, one(own))
    tt(Y[:, 4:7:2, :], pp, Z[:, 2:4, :], sub).then_inc(own, one(own))
    between.get(1, nothing)()
    dve.wait_ge(own, so_far(own))
    tt(Cc, G, Bh, sub).then_inc(own, one(own))
    tt(Dd[:, 0, :], m[:, 0, :], m[:, 1, :], add).then_inc(own, one(own))
    tt(Dd[:, 1, :], m[:, 1, :], m[:, 0, :], sub).then_inc(own, one(own))
    stt(out=Y[:, 1, :], in0=x1[:, 1, :], scalar=T22, in1=x1[:, 0, :], op0=mul, op1=add).then_inc(own, one(own))
    stt(out=Y[:, 5, :], in0=x1[:, 0, :], scalar=-T22, in1=x1[:, 1, :], op0=mul, op1=add).then_inc(own, one(own))
    stt(out=Y[:, 3, :], in0=x3[:, 0, :], scalar=T22, in1=x3[:, 1, :], op0=mul, op1=add).then_inc(own, one(own))
    stt(out=Y[:, 7, :], in0=x3[:, 1, :], scalar=T22, in1=x3[:, 0, :], op0=mul, op1=sub).then_inc(own, one(own))
    between.get(2, nothing)()
    dve.wait_ge(own, so_far(own))
    stt(out=dq[:, 1, :], in0=Cc[:, 0, :], scalar=C45, in1=dq[:, 1, :], op0=mul, op1=add).then_inc(own, one(own))
    stt(out=Y[:, 4, :], in0=Cc[:, 1, :], scalar=C45, in1=Y[:, 4, :], op0=mul, op1=add).then_inc(own, one(own))
    s13 = Y[:, 2:7:4, :]
    stt(out=G, in0=Dd, scalar=C45, in1=s13, op0=mul, op1=add).then_inc(own, one(own))
    stt(out=Bh, in0=Dd, scalar=-C45, in1=s13, op0=mul, op1=add).then_inc(own, one(own))
    between.get(3, nothing)()
    dve.wait_ge(own, so_far(own))
    s02 = Y[:, 0:5:4, :]
    tt(m, s02, dq, add).then_inc(own, one(own))
    tt(pp, s02, dq, sub).then_inc(own, one(own))
    stt(out=Y[:, 1:4:2, :], in0=Y[:, 1:4:2, :], scalar=C22, in1=G, op0=mul, op1=add).then_inc(own, one(own))
    stt(out=Y[:, 5:8:2, :], in0=Y[:, 5:8:2, :], scalar=C22, in1=Bh, op0=mul, op1=add).then_inc(own, one(own))
    between.get(4, nothing)()
    dve.wait_ge(own, so_far(own))
    tt(Y[:, 0:5:4, :], T[:, 10:13:2, :], w, add).then_inc(own, one(own))
    tt(Y[:, 2:7:4, :], T[:, 11:14:2, :], X[:, 2:7:4, :], mul).then_inc(own, one(own))
    tt(Y[:, 1:8:2, :], Y[:, 1:8:2, :], X[:, 1:8:2, :], mul).then_inc(own, one(own))
    between.get(5, nothing)()
    dve.wait_ge(own, so_far(own))
    tt(Y[:, 0:5:4, :], Y[:, 0:5:4, :], X[:, 0:5:4, :], mul).then_inc(done, one(done))


def mix_stage(nc, dram, scratch):
    CH = 64
    NCH = L // CH
    R = 2 * ORDER
    with ExitStack() as ctx:
        sb = lambda name, shape, dt=F32: ctx.enter_context(nc.sbuf_tensor(name, shape, dt))
        ps = lambda name: ctx.enter_context(nc.psum_tensor(name, [P, 2, 512], F32))
        sem = lambda name: ctx.enter_context(nc.semaphore(name))
        fwd = sb("m_fwd", [P, GROUPS, 4, P])
        inv = sb("m_inv", [P, GROUPS, 4, P])
        z = sb("m_z", [P, TT, HW])
        V = sb("m_V", [P, 2 * GROUPS, HALF])
        T = sb("m_T", [P, 20, HALF])
        K = sb("m_K", [P, GROUPS, 2, HALF])
        gate = sb("m_gate", [P, TT, HALF])
        M = sb("m_M", [P, 2, 2, HALF])
        Y = sb("m_Y", [P, 2, 2, HALF])
        ident = sb("m_ident", [P, P])
        q = sb("m_q", [P, L])
        k = sb("m_k", [P, L])
        v = sb("m_v", [P, TT, 2 * DV])
        g = sb("m_g", [P, TT, 2 * DV])
        code = sb("m_code", [2 * RANK, L])
        wa = sb("m_wa", [2 * RANK, 2, QK])
        ba = sb("m_ba", [P, 2, 2])
        pre = sb("m_pre", [P, 4, L])
        gx, ab, b, df = (pre[:, i, :] for i in range(4))
        nt = pre[:, 0:2, :].rearrange("p a (x d) -> p (a x) d", d=DV)
        osb = pre[:, 2:4, :].rearrange("p a (x d) -> p (a x) d", d=DV)
        starts = sb("m_starts", [P, L], mybir.dt.uint8)
        qd = sb("m_qd", [P, 2, L])
        ki = sb("m_ki", [P, 2, L])
        dec = sb("m_dec", [P, 2, NCH])
        kT = sb("m_kT", [P, TT, P])
        S = sb("m_S", [P, 2, NCH, DV])
        mask = sb("m_mask", [P, 2, P], I32)
        sc = sb("m_sc", [P, 2, 2, 2, P])
        nw = sb("m_nw", [P, DV])
        rs = sb("m_rs", [P, 4, 2 * TT])
        psU, psZ, psG, psS = ps("psU"), ps("psZ"), ps("psG"), ps("psS")

        s_tab, s_inv = sem("m_tables"), sem("m_inverse_table")
        s_z = [sem(f"m_z_loaded{h}") for h in range(2)]
        s_K = sem("m_K_loaded")
        s_gate = sem("m_gate_loaded")
        s_gl = sem("m_gla_constants")
        s_qk = sem("m_qk_loaded")
        s_vg = sem("m_vg_loaded")
        own_dve, own_act = sem("m_own_dve"), sem("m_own_act")
        s_tree = sem("m_tree_done")
        s_u = sem("m_data_spectrum")
        s_mult = sem("m_spectrum_taken")
        s_y = sem("m_product_ready")
        s_zf = sem("m_inverse_product")
        s_zt = sem("m_inverse_taken")
        s_gated = sem("m_round_done")
        s_gf = sem("m_psG_filled")
        s_gt = sem("m_psG_taken")
        s_gx = sem("m_logs_ready")
        s_b = sem("m_cumsum_ready")
        s_df = sem("m_chunk_rest_ready")
        s_ex = sem("m_exps_ready")
        s_qd = sem("m_decayed_ready")
        s_S = sem("m_states_ready")
        s_sf = sem("m_scores_filled")
        s_sm = sem("m_scores_masked")
        s_zero = sem("m_scores_zeroed")
        s_ss = sem("m_head_variance")
        s_rt = sem("m_head_root")
        s_sg = sem("m_silu_ready")
        s_gn = sem("m_silu_times_norm")
        s_on = sem("m_heads_done")
        s_st = sem("m_stored")
        s_st2 = sem("m_hyena_stored")

        FR, FB = 4, TT

        def psg_after(r):
            return FR * (r + 1) + FB * (r // 2)

        def fills_before_heads(ht):
            return psg_after(2 * ht + 1)

        with nc.Block() as block:
            @block.sync
            def _(sp):
                def round_loads(r):
                    o, h = r // 2, r % 2
                    sp.wait_ge(s_y, 8 * r)
                    sp.dma_start(K[:], scratch["spec"][o, h]).then_inc(s_K, 16)
                    sp.wait_ge(s_gated, r)
                    sp.dma_start(gate[:], scratch["hy"][1 + o, :, HALF * h:HALF * h + HALF].rearrange("(a p) c -> p a c", p=P)).then_inc(s_gate, 16)

                def head_loads(ht):
                    if ht:
                        sp.wait_ge(s_qd, 2)
                    sp.dma_start(q[:], scratch["qk"][ht]).then_inc(s_qk, 16)
                    sp.dma_start(k[:], scratch["qk"][2 + ht]).then_inc(s_qk, 16)
                    if ht:
                        sp.wait_ge(s_on, 1)
                    for i, t in enumerate((v, g)):
                        sp.dma_start(t[:], scratch["vg"][i, :, 2 * DV * ht:2 * DV * ht + 2 * DV].rearrange("(a p) c -> p a c", p=P)).then_inc(s_vg, 16)

                def half_load(h):
                    sp.dma_start(z[:, :, HALF * h:HALF * h + HALF],
                                 scratch["hy"][0, :, HALF * h:HALF * h + HALF].rearrange("(a p) c -> p a c", p=P)).then_inc(s_z[h], 16)

                half_load(0)
                sp.dma_start(code[:], scratch["code"]).then_inc(s_gl, 16)
                sp.wait_ge(s_zero, 1)
                sp.dma_start(wa[0:RANK, 0, :], dram["gla_wa_f"][0]).then_inc(s_gl, 16)
                sp.dma_start(wa[RANK:2 * RANK, 1, :], dram["gla_wa_b"][0]).then_inc(s_gl, 16)
                sp.dma_start(ba[:], dram["l_gate_b"]).then_inc(s_gl, 16)
                sp.dma_start(mask[:], dram["c_mask"]).then_inc(s_gl, 16)
                sp.dma_start(nw[:], dram["gla_norm_w"][0].partition_broadcast(P)).then_inc(s_gl, 16)
                sp.dma_start(ident[:], dram["c_ident"]).then_inc(s_tab, 16)
                sp.dma_start(fwd[:], dram["c_fwd"].rearrange("p (g q c) -> p g q c", g=GROUPS, q=4)).then_inc(s_tab, 16)
                sp.dma_start(K[:], scratch["spec"][0, 0]).then_inc(s_K, 16)
                sp.dma_start(inv[:], dram["c_inv"].rearrange("p (g q c) -> p g q c", g=GROUPS, q=4)).then_inc(s_inv, 16)
                sp.dma_start(gate[:], scratch["hy"][1, :, 0:HALF].rearrange("(a p) c -> p a c", p=P)).then_inc(s_gate, 16)
                half_load(1)
                head_loads(0)
                round_loads(1)
                round_loads(2)
                head_loads(1)
                round_loads(3)

            @block.gpsimd
            def _(pool):
                pool.memset(wa[:], 0.0).then_inc(s_zero, 1)
                pool.memset(sc[:], 0.0).then_inc(s_zero, 1)
                pool.memset(starts[:], 1).then_inc(s_zero, 1)
                pool.wait_ge(s_zero, 3)
                pool.memset(starts[:].rearrange("p (n c) -> p n c", c=CH)[:, :, 0:1], 0).then_inc(s_zero, 1)
                pool.wait_ge(s_gl, 16 * 6)
                for ht in range(2):
                    pool.wait_ge(s_sg, ht + 1)
                    gv = g[:].rearrange("p a (x d) -> p (a x) d", d=DV)
                    pool.tensor_tensor(gv, gv, nw[:].unsqueeze(1).to_broadcast([P, 2 * TT, DV]), ALU.mult).then_inc(s_gn, 1)
                    pool.wait_ge(s_on, ht + 1)
                    pool.dma_start(scratch["mix"][:, 2 * DV * ht:2 * DV * ht + 2 * DV].rearrange("(a p) c -> p a c", p=P),
                                   osb.rearrange("p (a x) d -> p a (x d)", x=2)).then_inc(s_st, 16)
                pool.wait_ge(s_gated, R)
                pool.dma_start(scratch["mix"][:, GW:D].rearrange("(a p) c -> p a c", p=P), z[:]).then_inc(s_st2, 16)
                pool.wait_ge(s_st, 32)
                pool.wait_ge(s_st2, 16)

            @block.tensor
            def _(pe):
                fills = [0]

                def fill_free():
                    if fills[0]:
                        pe.wait_ge(s_gt, fills[0])
                    fills[0] += 1

                def gate_logits(r):
                    ht, dr = r // 2, r % 2
                    fill_free()
                    for c in range(2):
                        m = pe.matmul(psG[:, c, :], wa[:, dr, P * ht:P * ht + P], code[:, 512 * c:512 * c + 512], start=True, stop=True)
                    m.then_inc(s_gf, 1)

                def hyena(r):
                    pe.wait_ge(s_tree, r + 1)
                    for i in range(GROUPS + 2):
                        if i < GROUPS:
                            n = GROUPS * r + i
                            if n >= 2:
                                pe.wait_ge(s_mult, n - 1)
                            for part in range(2):
                                for slot in range(2):
                                    mm = pe.matmul(psU[:, n % 2, HALF * part:HALF * part + HALF], fwd[:, i, 2 * part + slot, :],
                                                   V[:, 2 * i + slot, :], start=(slot == 0), stop=(slot == 1))
                            mm.then_inc(s_u, 1)
                        if i >= 2:
                            gi, n = i - 2, GROUPS * r + i - 2
                            pe.wait_ge(s_y, n + 1)
                            if n >= 2:
                                pe.wait_ge(s_zt, n - 1)
                            for slot in range(2):
                                for part in range(2):
                                    mm = pe.matmul(psZ[:, n % 2, HALF * slot:HALF * slot + HALF], inv[:, gi, 2 * part + slot, :],
                                                   Y[:, n % 2, part, :], start=(part == 0), stop=(part == 1))
                            mm.then_inc(s_zf, 1)

                def chunk_products(r):
                    ht, dr = r // 2, r % 2
                    pe.wait_ge(s_qd, r + 1)
                    fill_free()
                    for t in range(TT):
                        m = pe.transpose(psG[:, t // 4, P * (t % 4):P * (t % 4) + P], df[:, P * t:P * t + P], ident[:])
                    m.then_inc(s_gf, 1)
                    if dr == 0:
                        pe.wait_ge(s_vg, 32 * (ht + 1))
                    for batch in range(2):
                        fill_free()
                        for i in range(8):
                            n = 8 * batch + i
                            rows = slice(CH * (n % 2), CH * (n % 2) + CH)
                            for hd in range(2):
                                m = pe.matmul(psG[CH * hd:CH * hd + CH, n % 2, DV * (i // 2):DV * (i // 2) + DV],
                                              kT[rows, n // 2, CH * hd:CH * hd + CH], v[rows, n // 2, DV * hd:DV * hd + DV],
                                              start=True, stop=True)
                        m.then_inc(s_gf, 1)

                def scores(ht, t):
                    n = TT * ht + t
                    if n:
                        pe.wait_ge(s_sm, n)
                    for hd in range(2):
                        rows = slice(DK * hd, DK * hd + DK)
                        for dr in range(2):
                            m = pe.matmul(psS[:, hd, P * dr:P * dr + P], ki[rows, dr, P * t:P * t + P], qd[rows, dr, P * t:P * t + P],
                                          start=True, stop=True)
                    m.then_inc(s_sf, 1)

                def heads_out(ht):
                    pe.wait_ge(s_S, 2 * ht + 2)
                    scores(ht, 0)
                    for t in range(TT):
                        if t + 1 < TT:
                            scores(ht, t + 1)
                        pe.wait_ge(s_sm, TT * ht + t + 1)
                        fill_free()
                        for hd in range(2):
                            rows = slice(DK * hd, DK * hd + DK)
                            for dr in range(2):
                                m = pe.matmul(psG[:, hd, 0:DV], sc[:, t % 2, hd, dr, :], v[:, t, DV * hd:DV * hd + DV],
                                              start=(dr == 0), stop=False, skip_group_check=True)
                            for c in range(2):
                                n = 2 * t + c
                                for dr, before in ((0, n - 1), (1, n + 1)):
                                    if 0 <= before < NCH:
                                        m = pe.matmul(psG[CH * c:CH * c + CH, hd, 0:DV], qd[rows, dr, CH * n:CH * n + CH],
                                                      S[rows, dr, before, :], start=False, stop=False, skip_group_check=True)
                        m.then_inc(s_gf, 1)

                pe.wait_ge(s_gl, 16 * 6)
                for r in range(R):
                    gate_logits(r)
                    if r == 0:
                        pe.wait_ge(s_tab, 32)
                        pe.wait_ge(s_inv, 16)
                    hyena(r)
                    chunk_products(r)
                    if r % 2:
                        heads_out(r // 2)

            @block.vector
            def _(dve):
                one, so_far = raise_counts()

                def products(r, before):
                    dve.wait_ge(s_K, 16 * (r + 1))
                    for i in range(GROUPS):
                        n = GROUPS * r + i
                        before.get(i, nothing)()
                        dve.wait_ge(s_u, n + 1)
                        U = psU[:, n % 2, :].rearrange("p (a c) -> p a c", a=2)
                        if so_far(s_tree):
                            dve.wait_ge(s_tree, so_far(s_tree))
                        if so_far(s_y):
                            dve.wait_ge(s_y, so_far(s_y))
                        dve.tensor_tensor(M[:, 0], U, K[:, i], ALU.mult).then_inc(own_dve, one(own_dve))
                        dve.tensor_tensor(M[:, 1], U, K[:, i, ::-1, :], ALU.mult).then_inc(s_mult, one(s_mult))
                        if n >= 2:
                            dve.wait_ge(s_zf, n - 1)
                        dve.wait_ge(s_mult, so_far(s_mult))
                        dve.tensor_tensor(Y[:, n % 2, 0, :], M[:, 0, 0, :], M[:, 0, 1, :], ALU.subtract).then_inc(own_dve, one(own_dve))
                        last = dve.tensor_tensor(Y[:, n % 2, 1, :], M[:, 1, 0, :], M[:, 1, 1, :], ALU.add)
                        if i == 0:
                            last.then_inc(own_dve, one(own_dve))
                            dve.wait_ge(own_dve, so_far(own_dve))
                            last = dve.tensor_copy(Y[0:1, n % 2], M[0:1, 0])
                        last.then_inc(s_y, one(s_y))

                def cumulate(r):
                    dr = r % 2
                    dve.wait_ge(s_gx, r + 1)
                    dve.scalar_tensor_tensor(out=gx, in0=gx, scalar=0.0, in1=ab, op0=ALU.min, op1=ALU.subtract).then_inc(own_dve, one(own_dve))
                    dve.wait_ge(own_dve, so_far(own_dve))
                    f = (lambda t: t) if dr == 0 else (lambda t: t[:, ::-1])
                    dve.tensor_tensor_scan(f(b), starts[:], f(gx), 0.0, ALU.mult, ALU.add).then_inc(s_b, one(s_b))
                    dve.wait_ge(s_b, so_far(s_b))
                    bc = b.rearrange("p (n c) -> p n c", c=CH)
                    end = bc[:, :, CH - 1:CH] if dr == 0 else bc[:, :, 0:1]
                    dve.tensor_tensor(df.rearrange("p (n c) -> p n c", c=CH), end.to_broadcast([P, NCH, CH]), bc, ALU.subtract).then_inc(s_df, one(s_df))

                def decayed(r):
                    dr = r % 2
                    dve.wait_ge(s_ex, r + 1)
                    dve.wait_ge(s_qk, 32 * (r // 2 + 1))
                    dve.tensor_tensor(qd[:, dr, :], q[:], gx, ALU.mult).then_inc(own_dve, one(own_dve))
                    dve.tensor_tensor(ki[:, dr, :], k[:], ab, ALU.mult).then_inc(own_dve, one(own_dve))
                    dve.tensor_tensor(df, k[:], df, ALU.mult).then_inc(s_qd, one(s_qd))

                def states(r):
                    ht, dr = r // 2, r % 2
                    dve.wait_ge(s_gt, psg_after(r))
                    order = range(1, NCH - 1) if dr == 0 else range(NCH - 2, 0, -1)
                    for i, n in enumerate(order):
                        if so_far(s_qd):
                            dve.wait_ge(s_qd, so_far(s_qd))
                        if so_far(own_dve):
                            dve.wait_ge(own_dve, so_far(own_dve))
                        prev = n - 1 if dr == 0 else n + 1
                        ins = dve.scalar_tensor_tensor(out=S[:, dr, n, :], in0=S[:, dr, prev, :], scalar=dec[:, dr, n:n + 1],
                                                       in1=S[:, dr, n, :], op0=ALU.mult, op1=ALU.add)
                        if i == NCH - 3:
                            ins.then_inc(s_S, one(s_S))
                        else:
                            ins.then_inc(own_dve, one(own_dve))

                def causal(ht, ts):
                    for t in ts:
                        dve.wait_ge(s_sf, TT * ht + t + 1)
                        if t >= 2:
                            dve.wait_ge(s_gf, fills_before_heads(ht) + t - 1)
                        elif t == 0:
                            dve.wait_ge(s_gl, 16 * 6)
                        m = mask[:].rearrange("p a c -> p (a c)").unsqueeze(1).to_broadcast([P, 2, 2 * P])
                        dve.copy_predicated(sc[:, t % 2].rearrange("p h d c -> p h (d c)"), m, psS[:, :, 0:2 * P]).then_inc(s_sm, one(s_sm))

                def heads_norm(ht):
                    dve.wait_ge(s_gt, fills_before_heads(ht) + TT)
                    dve.wait_ge(s_sm, so_far(s_sm))
                    dve.tensor_tensor(nt, osb, osb, ALU.mult).then_inc(own_dve, one(own_dve))
                    dve.wait_ge(own_dve, so_far(own_dve))
                    dve.tensor_reduce(rs[:, 3, :], nt, AX_X, ALU.add).then_inc(own_dve, one(own_dve))
                    dve.wait_ge(own_dve, so_far(own_dve))
                    dve.tensor_scalar(rs[:, 0, :], rs[:, 3, :], 1.0 / DV, EPS, ALU.mult, ALU.add).then_inc(s_ss, one(s_ss))
                    dve.wait_ge(s_rt, ht + 1)
                    dve.reciprocal(rs[:, 2, :], rs[:, 1, :]).then_inc(own_dve, one(own_dve))
                    newton(dve, own_dve, one, so_far, rs)
                    dve.tensor_tensor(osb, osb, rs[:, 2, :].unsqueeze(2).to_broadcast([P, 2 * TT, DV]), ALU.mult).then_inc(own_dve, one(own_dve))
                    dve.wait_ge(s_gn, ht + 1)
                    dve.wait_ge(own_dve, so_far(own_dve))
                    dve.tensor_tensor(osb, osb, g[:].rearrange("p a (x d) -> p (a x) d", d=DV), ALU.mult).then_inc(s_on, one(s_on))

                def forward(r, between):
                    if r < 2:
                        dve.wait_ge(s_z[r], 16)
                    else:
                        dve.wait_ge(s_gated, r - 1)
                    if r:
                        dve.wait_ge(s_gated, so_far(s_gated))
                    forward_tree(dve, own_dve, one, so_far, z[:, :, HALF * (r % 2):HALF * (r % 2) + HALF], V[:], T[:], s_tree, between)

                def inverse(r, between):
                    dve.wait_ge(s_zt, GROUPS * (r + 1))
                    dve.wait_ge(s_gate, 16 * (r + 1))
                    dve.wait_ge(s_tree, so_far(s_tree))
                    inverse_tree(dve, own_dve, one, so_far, V[:], z[:, :, HALF * (r % 2):HALF * (r % 2) + HALF], gate[:], T[:], s_gated, between)

                forward(0, {})
                dve.wait_ge(s_zero, 4)
                for ht in range(2):
                    r, s = 2 * ht, 2 * ht + 1
                    products(r, {6: lambda: cumulate(r)})
                    inverse(r, {2: lambda: decayed(r)})
                    forward(s, {0: lambda: states(r), 1: lambda: cumulate(s)})
                    products(s, {4: lambda: decayed(s)})
                    inverse(s, {5: lambda: states(s)})
                    if ht == 0:
                        forward(s + 1, {i: lambda i=i: causal(0, (2 * i, 2 * i + 1)) for i in range(3)})
                        causal(ht, (6, 7))
                    else:
                        causal(ht, range(TT))
                    heads_norm(ht)

            @block.scalar
            def _(act):
                one, so_far = raise_counts()
                taken = [0]
                act.wait_ge(s_gl, 16 * 6)

                def inverse(r, groups):
                    for i in groups:
                        n = GROUPS * r + i
                        act.wait_ge(s_zf, n + 1)
                        act.activation(V[:, 2 * i:2 * i + 2, :], psZ[:, n % 2, :].rearrange("p (a c) -> p a c", a=2), ACT.Identity).then_inc(s_zt, one(s_zt))

                def wait_fill():
                    taken[0] += 1
                    act.wait_ge(s_gf, taken[0])
                    return taken[0]

                def logs(r):
                    ht, dr = r // 2, r % 2
                    if r and dr == 0:
                        act.wait_ge(s_st, 16 * ht)
                    n = wait_fill()
                    if so_far(s_gt):
                        act.wait_ge(s_gt, so_far(s_gt))
                    if so_far(s_rt):
                        act.wait_ge(s_rt, so_far(s_rt))
                    act.activation(gx, psG[:], ACT.Identity, bias=ba[:, dr, ht:ht + 1]).then_inc(s_gt, one(s_gt))
                    act.wait_ge(s_gt, so_far(s_gt))
                    act.activation(ab, gx, ACT.Abs).then_inc(own_act, one(own_act))
                    act.wait_ge(own_act, so_far(own_act))
                    act.activation(ab, ab, ACT.Exp, scale=-1.0).then_inc(own_act, one(own_act))
                    act.wait_ge(own_act, so_far(own_act))
                    act.activation(ab, ab, ACT.Ln, bias=1.0).then_inc(s_gx, one(s_gx))

                def exps(r):
                    dr = r % 2
                    act.wait_ge(s_b, r + 1)
                    act.wait_ge(s_zt, so_far(s_zt))
                    end = b.rearrange("p (n c) -> p n c", c=CH)[:, :, (CH - 1) * (1 - dr)]
                    act.activation(dec[:, dr, :], end, ACT.Exp, scale=1.0 / TAU).then_inc(own_act, one(own_act))
                    act.activation(gx, b, ACT.Exp, scale=1.0 / TAU).then_inc(own_act, one(own_act))
                    act.activation(ab, b, ACT.Exp, scale=-1.0 / TAU).then_inc(own_act, one(own_act))
                    act.wait_ge(s_df, r + 1)
                    act.activation(df, df, ACT.Exp, scale=1.0 / TAU).then_inc(s_ex, one(s_ex))

                def take_products(r):
                    dr = r % 2
                    n = wait_fill()
                    act.activation(kT[:], psG[:].rearrange("p a (t c) -> p (a t) c", c=P), ACT.Identity).then_inc(s_gt, one(s_gt))
                    for batch in range(2):
                        n = wait_fill()
                        for par in range(2):
                            ins = act.activation(S[:, dr, 8 * batch + par:8 * batch + 8:2, :], psG[:, par, :].rearrange("p (i d) -> p i d", d=DV), ACT.Identity)
                            if par:
                                ins.then_inc(s_gt, one(s_gt))
                            else:
                                ins.then_inc(own_act, one(own_act))

                def take_heads(ht):
                    for t in range(TT):
                        n = wait_fill()
                        act.activation(osb[:, 2 * t:2 * t + 2, :], psG[:, :, 0:DV], ACT.Identity).then_inc(s_gt, one(s_gt))
                    act.wait_ge(s_gt, so_far(s_gt))
                    act.activation(g[:], g[:], ACT.Silu).then_inc(s_sg, one(s_sg))
                    act.wait_ge(s_ss, ht + 1)
                    act.activation(rs[:, 1, :], rs[:, 0, :], ACT.Sqrt).then_inc(s_rt, one(s_rt))

                for ht in range(2):
                    r, s = 2 * ht, 2 * ht + 1
                    inverse(r, range(0, 4))
                    logs(r)
                    inverse(r, range(4, GROUPS))
                    exps(r)
                    take_products(r)
                    logs(s)
                    exps(s)
                    inverse(s, range(GROUPS))
                    take_products(s)
                    take_heads(ht)


RING = 8
NGU, NDN = 16, 8


def load_piece(sp, dram, ring, piece_loaded, e, i):
    slot = ring[:, i % RING, :]
    if i < NGU:
        n, m, half = i // 4, (i // 2) % 2, i % 2
        w = dram[("w_gate_e", "w_up_e")[m]][0]
        src = w[bass.ds(e, 1), 512 * half:512 * half + 512, 512 * n:512 * n + 512].rearrange("o (k p) c -> (o p) k c", p=P)
        dst = slot.rearrange("p (k c) -> p k c", k=4)
    else:
        j = i - NGU
        src = dram["w_down_e"][0, bass.ds(e, 1), 2 * P * j:2 * P * j + 2 * P, :].rearrange("o (k p) c -> (o p) k c", p=P)
        dst = slot.rearrange("p (k c) -> p k c", k=2)
    sp.dma_start(dst, src).then_inc(piece_loaded[i % RING], 16)


def residual_stage(nc, dram, scratch, tile_loaded, loads_before, ring, piece_loaded):
    with ExitStack() as ctx:
        sb = lambda name, shape, dt=F32: ctx.enter_context(nc.sbuf_tensor(name, shape, dt))
        ps = lambda name, n: ctx.enter_context(nc.psum_tensor(name, [P, n, 512], F32))
        sem = lambda name: ctx.enter_context(nc.semaphore(name))
        mix = sb("o_mix", [P, TT, D])
        x = sb("o_x", [P, TT, D])
        w = sb("o_w", [P, DT, D])
        mixT = sb("o_mixT", [P, 2, DT, P])
        h = sb("o_h", [P, 2, D])
        hT = sb("o_hT", [P, 2, DT, P])
        sq = sb("o_sq", [P, D])
        wr = sb("o_wr", [P, DT, NE])
        lnw = sb("o_lnw", [P, DT])
        ident = sb("o_ident", [P, P])
        ssq = sb("o_ssq", [P, TT])
        rs = sb("o_rs", [P, 4, TT])
        lg = sb("o_lg", [P, TT, NE])
        ex = sb("o_ex", [P, TT, NE])
        st = sb("o_st", [P, 4, TT])
        pr = sb("o_pr", [P, TT, NE])
        prc = sb("o_prc", [P, NE, TT])
        pT = sb("o_pT", [NE, L])
        psT, psO, psH, psR = ps("o_psT", 2), ps("o_psO", 3), ps("o_psH", 2), ps("o_psR", 1)

        s_c, s_wr = sem("o_constants"), sem("o_router_loaded")
        s_w = [sem(f"o_w_loaded{c}") for c in range(2)]
        both_loaded = loads_before + 32
        own_dve, own_act = sem("o_own_dve"), sem("o_own_act")
        s_tf, s_tt = sem("o_mixT_filled"), sem("o_mixT_taken")
        s_of, s_ot = sem("o_product"), sem("o_residual_added")
        s_sq, s_var, s_rt = sem("o_squares"), sem("o_variance"), sem("o_root")
        s_h = sem("o_normed")
        s_hf, s_hT = sem("o_hT_filled"), sem("o_hT_taken")
        s_lg = sem("o_logits")
        s_sub, s_ex = sem("o_logits_less_max"), sem("o_exps")
        s_pr, s_pf, s_pT = sem("o_probs"), sem("o_probs_transposed"), sem("o_probs_by_row")
        s_sth = [sem(f"o_h_stored{i}") for i in range(2)]
        s_str = sem("o_stored")

        with nc.Block() as block:
            @block.sync
            def _(sp):
                sp.dma_start(ident[:], dram["c_ident"]).then_inc(s_c, 16)
                sp.dma_start(lnw[:], dram["l_ln_ffn"]).then_inc(s_c, 16)
                for t in range(TT):
                    sp.dma_start(mix[:, t, :], scratch["mix"][P * t:P * t + P, :]).then_inc(tile_loaded[t], 16)
                    if t < 2:
                        sp.dma_start(w[:, :, 512 * t:512 * t + 512],
                                     dram["w_out"][0, :, 512 * t:512 * t + 512].rearrange("(k p) n -> p k n", p=P)).then_inc(s_w[t], 16)
                    sp.dma_start(x[:, t, :], dram["x"][0, P * t:P * t + P, :]).then_inc(tile_loaded[t], 16)
                    if t == 0:
                        sp.dma_start(wr[:], dram["w_router"][0].rearrange("(k p) n -> p k n", p=P)).then_inc(s_wr, 16)
                for i in range(RING):
                    load_piece(sp, dram, ring, piece_loaded, 0, i)

            @block.gpsimd
            def _(pool):
                for t in range(TT):
                    pool.wait_ge(s_ot, 2 * t + 2)
                    pool.dma_start(scratch["r"][P * t:P * t + P, :], x[:, t, :]).then_inc(s_str, 16)
                    pool.wait_ge(s_h, t + 1)
                    pool.dma_start(scratch["h2"][P * t:P * t + P, :], h[:, t % 2, :]).then_inc(s_sth[t % 2], 16)
                pool.wait_ge(s_pr, 2)
                pool.dma_start(scratch["pcol"].rearrange("e p t -> p e t"), prc[:]).then_inc(s_str, 16)
                pool.wait_ge(s_pT, 1)
                pool.dma_start(scratch["prow"], pT[:]).then_inc(s_str, 16)
                pool.wait_ge(s_str, 16 * (TT + 2))
                for i in range(2):
                    pool.wait_ge(s_sth[i], 16 * TT // 2)

            @block.tensor
            def _(pe):
                pe.wait_ge(s_c, 32)
                fills = [0]

                def mix_transposes(t):
                    pe.wait_ge(tile_loaded[t], both_loaded)
                    for c in range(2):
                        if fills[0] >= 2:
                            pe.wait_ge(s_tt, fills[0] - 1)
                        for i in range(4):
                            k = 4 * c + i
                            m = pe.transpose(psT[:, c, P * i:P * i + P], mix[:, t, P * k:P * k + P], ident[:])
                        m.then_inc(s_tf, 1)
                        fills[0] += 1

                def product(t):
                    pe.wait_ge(s_tt, 2 * t + 2)
                    for c in range(2):
                        pe.wait_ge(s_w[c], 16)
                        n = 2 * t + c
                        if n >= 3:
                            pe.wait_ge(s_ot, n - 2)
                        for k in range(DT):
                            m = pe.matmul(psO[:, n % 3, :], mixT[:, t % 2, k, :], w[:, k, 512 * c:512 * c + 512],
                                          start=(k == 0), stop=(k == DT - 1))
                        m.then_inc(s_of, 1)

                def h_transposes(t):
                    pe.wait_ge(s_h, t + 1)
                    for c in range(2):
                        if t:
                            pe.wait_ge(s_hT, 2 * (t - 1) + c + 1)
                        for i in range(4):
                            k = 4 * c + i
                            m = pe.transpose(psH[:, c, P * i:P * i + P], h[:, t % 2, P * k:P * k + P], ident[:])
                        m.then_inc(s_hf, 1)

                def router(t):
                    pe.wait_ge(s_hT, 2 * t + 2)
                    if t == 0:
                        pe.wait_ge(s_wr, 16)
                    for k in range(DT):
                        m = pe.matmul(psR[:, 0, NE * t:NE * t + NE], hT[:, t % 2, k, :], wr[:, k, :], start=(k == 0), stop=(k == DT - 1))
                    m.then_inc(s_lg, 1)

                for i in range(TT + 3):
                    if i < TT:
                        mix_transposes(i)
                    if 1 <= i <= TT:
                        product(i - 1)
                    if 2 <= i <= TT + 1:
                        h_transposes(i - 2)
                    if i >= 3:
                        router(i - 3)
                pe.wait_ge(s_pr, 1)
                for t in range(TT):
                    m = pe.transpose(psT[0:NE, t // 4, P * (t % 4):P * (t % 4) + P], pr[:, t, :], ident[:])
                m.then_inc(s_pf, 1)

            @block.scalar
            def _(act):
                one, so_far = raise_counts()
                for i in range(TT + 1):
                    if i < TT:
                        if i >= 2:
                            act.wait_ge(s_of, 2 * (i - 2) + 2)
                        for c in range(2):
                            act.wait_ge(s_tf, 2 * i + c + 1)
                            act.activation(mixT[:, i % 2, 4 * c:4 * c + 4, :], psT[:, c, :].rearrange("p (k c) -> p k c", k=4), ACT.Identity).then_inc(s_tt, one(s_tt))
                    if i >= 1:
                        t = i - 1
                        act.wait_ge(s_ot, 2 * t + 2)
                        if so_far(s_tt):
                            act.wait_ge(s_tt, so_far(s_tt))
                        if so_far(s_rt):
                            act.wait_ge(s_rt, so_far(s_rt))
                        act.activation(sq[:], x[:, t, :], ACT.Square, accum_out=ssq[:, t:t + 1]).then_inc(s_sq, one(s_sq))
                        act.wait_ge(s_var, t + 1)
                        act.activation(rs[:, 1, t:t + 1], rs[:, 0, t:t + 1], ACT.Sqrt).then_inc(s_rt, one(s_rt))
                act.wait_ge(s_sub, 1)
                act.activation(ex[:], lg[:], ACT.Exp).then_inc(s_ex, one(s_ex))
                act.wait_ge(s_pf, 1)
                act.activation(pT[:], psT[0:NE].rearrange("p a c -> p (a c)"), ACT.Identity).then_inc(s_pT, one(s_pT))

            @block.vector
            def _(dve):
                one, so_far = raise_counts()
                dve.wait_ge(s_c, 32)
                for i in range(TT + 1):
                    if i < TT:
                        t = i
                        dve.wait_ge(tile_loaded[t], both_loaded)
                        for c in range(2):
                            n = 2 * t + c
                            dve.wait_ge(s_of, n + 1)
                            xs = x[:, t, 512 * c:512 * c + 512]
                            dve.tensor_tensor(xs, xs, psO[:, n % 3, :], ALU.add).then_inc(s_ot, one(s_ot))
                        dve.wait_ge(s_sq, t + 1)
                        dve.wait_ge(s_ot, so_far(s_ot))
                        dve.tensor_scalar(rs[:, 0, t:t + 1], ssq[:, t:t + 1], 1.0 / D, EPS, ALU.mult, ALU.add).then_inc(s_var, one(s_var))
                        dve.wait_ge(s_rt, t + 1)
                        dve.reciprocal(rs[:, 2, t:t + 1], rs[:, 1, t:t + 1]).then_inc(own_dve, one(own_dve))
                        newton(dve, own_dve, one, so_far, rs[:, :, t:t + 1])
                        if t >= 2:
                            dve.wait_ge(s_sth[t % 2], 16 * (t // 2))
                            dve.wait_ge(s_hf, 2 * (t - 2) + 2)
                        dve.tensor_scalar(h[:, t % 2, :], x[:, t, :], rs[:, 2, t:t + 1], None, ALU.mult).then_inc(s_h, one(s_h))
                    if i >= 1:
                        t = i - 1
                        if t >= 2:
                            dve.wait_ge(s_lg, t - 1)
                        for c in range(2):
                            dve.wait_ge(s_hf, 2 * t + c + 1)
                            lw = lnw[:, 4 * c:4 * c + 4].unsqueeze(2).to_broadcast([P, 4, P])
                            dve.tensor_tensor(hT[:, t % 2, 4 * c:4 * c + 4, :], psH[:, c, :].rearrange("p (k c) -> p k c", k=4), lw, ALU.mult).then_inc(s_hT, one(s_hT))
                dve.wait_ge(s_lg, TT)
                dve.tensor_copy(lg[:], psR[:, 0, 0:TT * NE].rearrange("p (t e) -> p t e", e=NE)).then_inc(own_dve, one(own_dve))
                dve.wait_ge(own_dve, so_far(own_dve))
                dve.tensor_reduce(st[:, 0, :], lg[:], AX_X, ALU.max).then_inc(own_dve, one(own_dve))
                dve.wait_ge(own_dve, so_far(own_dve))
                dve.tensor_tensor(lg[:], lg[:], st[:, 0, :].unsqueeze(2).to_broadcast([P, TT, NE]), ALU.subtract).then_inc(s_sub, one(s_sub))
                dve.wait_ge(s_ex, 1)
                dve.tensor_reduce(st[:, 1, :], ex[:], AX_X, ALU.add).then_inc(own_dve, one(own_dve))
                dve.wait_ge(own_dve, so_far(own_dve))
                dve.reciprocal(st[:, 2, :], st[:, 1, :]).then_inc(own_dve, one(own_dve))
                dve.wait_ge(own_dve, so_far(own_dve))
                dve.tensor_tensor(pr[:], ex[:], st[:, 2, :].unsqueeze(2).to_broadcast([P, TT, NE]), ALU.mult).then_inc(s_pr, one(s_pr))
                dve.wait_ge(s_pr, so_far(s_pr))
                dve.tensor_copy(prc[:].rearrange("p e t -> p t e"), pr[:]).then_inc(s_pr, one(s_pr))


def expert_stage(nc, dram, scratch, ring, piece_loaded, p, wp, p_loaded):
    SPLIT = 4
    PER = NGU + NDN
    with ExitStack() as ctx:
        sb = lambda name, shape, dt=F32: ctx.enter_context(nc.sbuf_tensor(name, shape, dt))
        ps = lambda name, n: ctx.enter_context(nc.psum_tensor(name, [P, n, 512], F32))
        sem = lambda name: ctx.enter_context(nc.semaphore(name))
        wh = sb("e_wh", [P, SPLIT, 4, 512], F32R)
        wl = sb("e_wl", [P, SPLIT, 4, 512], F32R)
        xg = sb("e_xg", [P, D])
        xT = sb("e_xT", [P, DT, P])
        xh = sb("e_xh", [P, 2, DT, P], F32R)
        xl = sb("e_xl", [P, 2, DT, P], F32R)
        sg = sb("e_sg", [P, 512])
        hid = sb("e_hid", [P, 2, 512])
        hidT = sb("e_hidT", [P, FF // P, P])
        y = sb("e_y", [P, D])
        ident = sb("e_ident", [P, P])
        lnw = sb("e_lnw", [P, DT])
        prow = sb("e_prow", [P, L])
        pcol = sb("e_pcol", [P, TT])
        cmp = sb("e_cmp", [P, L])
        lower = sb("e_lower", [P, P])
        iota = sb("e_iota", [P, P])
        cnt = sb("e_cnt", [P, TT, 3])
        rank = sb("e_rank", [P, TT])
        hot = sb("e_hot", [P, TT, P])
        vals = sb("e_vals", [P, TT, 2])
        idx = sb("e_idx", [P, 2, 1], I32)
        gate = sb("e_gate", [P, 2])
        psG, psU, psT, psY = ps("e_psG", 2), ps("e_psU", 2), ps("e_psT", 2), ps("e_psY", 2)

        s_c = sem("e_constants")
        s_ld = piece_loaded
        own_dve, own_act = sem("e_own_dve"), sem("e_own_act")
        s_p = sem("e_probs_loaded")
        s_rank = sem("e_ranked")
        s_hot = sem("e_slots_ready")
        s_rf, s_rt = sem("e_route_filled"), sem("e_route_taken")
        s_g = sem("e_gathered")
        s_xf, s_xt = sem("e_x_transposed"), sem("e_x_taken")
        s_xh, s_xl = sem("e_xh_ready"), sem("e_xl_ready")
        s_hi, s_lo = sem("e_hi_ready"), sem("e_lo_ready")
        s_gu = sem("e_piece_multiplied")
        s_sg, s_hid = sem("e_silu_ready"), sem("e_hidden_ready")
        s_hf, s_ht = sem("e_hid_transposed"), sem("e_hidT_ready")
        s_dn = sem("e_down_multiplied")
        s_y = sem("e_y_ready")
        s_sc = sem("e_scattered")

        with nc.Block() as block:
            @block.sync
            def _(sp):
                sp.dma_start(lnw[:], dram["l_ln_ffn"]).then_inc(s_c, 16)
                sp.dma_start(ident[:], dram["c_ident"]).then_inc(s_c, 16)
                sp.dma_start(lower[:], dram["c_lower"]).then_inc(s_c, 16)
                sp.dma_start(iota[:], dram["c_iota"]).then_inc(s_c, 16)
                sp.dma_start(vals[:, :, 0:1], dram["c_tok"].unsqueeze(2), allow_slow_non_contiguous=True).then_inc(s_c, 16)

                def probs(e):
                    sp.dma_start(prow[:], scratch["prow"][bass.ds(e, 1), :].to_broadcast([P, L])).then_inc(s_p, 16)
                    sp.dma_start(pcol[:], scratch["pcol"][bass.ds(e, 1)].rearrange("o p t -> (o p) t")).then_inc(s_p, 16)

                def body(e, par, last, first=False):
                    for i in range(PER):
                        if first and i < RING:
                            continue
                        if i < RING:
                            sp.wait_ge(s_dn, NDN * e + i + 1 - NDN)
                        else:
                            sp.wait_ge(s_lo, NGU * e + i - RING + 1)
                        load_piece(sp, dram, ring, piece_loaded, e, i)
                        if i == RING and not last:
                            sp.wait_ge(s_rank, e + 1)
                            probs(e + 1)

                probs(0)
                body(0, 0, False, first=True)
                body(1, 1, False)
                with sp.Fori(2, NE - 2, 2) as e:
                    body(e, 0, False)
                    body(e + 1, 1, False)
                body(NE - 2, 0, False)
                body(NE - 1, 1, True)
                sp.dma_start(p[:], dram["p"][0, 0].rearrange("(t p) c -> p t c", p=P)).then_inc(p_loaded, 16)
                sp.dma_start(wp[:], dram["w_ple_proj"][0].rearrange("(k p) c -> p k c", p=P)).then_inc(p_loaded, 16)

            @block.gpsimd
            def _(pool):
                def gather(e, par):
                    pool.wait_ge(s_rt, e + 1)
                    pool.indirect_dma_start(xg[:], None, scratch["h2"], bass.IndirectOffsetOnAxis(ap=idx[:, par, :], axis=0)).then_inc(s_g, 16)

                def body(e, par, last):
                    if not last:
                        pool.wait_ge(s_xf, e + 1)
                        gather(e + 1, 1 - par)
                    pool.wait_ge(s_y, e + 1)
                    pool.indirect_dma_start(scratch["r"], bass.IndirectOffsetOnAxis(ap=idx[:, par, :], axis=0), y[:], None,
                                            compute_op=ALU.add).then_inc(s_sc, 16)
                    pool.wait_ge(s_sc, 16 * e + 16)

                gather(0, 0)
                for e in range(NE):
                    body(e, e % 2, e == NE - 1)

            @block.tensor
            def _(pe):
                def route(e):
                    pe.wait_ge(s_hot, e + 1)
                    for t in range(TT):
                        m = pe.matmul(psT[:, 0, 0:2], hot[:, t, :], vals[:, t, :], start=(t == 0), stop=(t == TT - 1))
                    m.then_inc(s_rf, 1)

                def x_transposes(e):
                    pe.wait_ge(s_rt, e + 1)
                    pe.wait_ge(s_g, 16 * e + 16)
                    for k in range(DT):
                        m = pe.transpose(psT[:, k // 4, P * (k % 4):P * (k % 4) + P], xg[:, P * k:P * k + P], ident[:])
                    m.then_inc(s_xf, 1)

                def hid_transposes(e, n):
                    pe.wait_ge(s_hid, 4 * e + n + 1)
                    if n >= 2:
                        pe.wait_ge(s_ht, 4 * e + n - 1)
                    for i in range(4):
                        m = pe.transpose(psT[:, n % 2, P * i:P * i + P], hid[:, n % 2, P * i:P * i + P], ident[:])
                    m.then_inc(s_hf, 1)

                def body(e, par, last):
                    pe.wait_ge(s_xh, e + 1)
                    pe.wait_ge(s_xl, e + 1)
                    for n in range(4):
                        for m_, bank in ((0, psG), (1, psU)):
                            if n < 2:
                                pe.wait_ge(s_hid, 4 * e + n - 2 + 1) if not (isinstance(e, int) and e == 0) else None
                            else:
                                pe.wait_ge(s_hid, 4 * e + n - 2 + 1)
                            for half in range(2):
                                i = 4 * n + 2 * m_ + half
                                pe.wait_ge(s_lo, NGU * e + i + 1)
                                for k in range(4):
                                    kk = 4 * half + k
                                    for j, (a, b) in enumerate(((xh, wh), (xl, wh), (xh, wl))):
                                        mm = pe.matmul(bank[:, n % 2, :], a[:, par, kk, :], b[:, i % SPLIT, k, :],
                                                       start=(kk == 0 and j == 0), stop=(kk == DT - 1 and j == 2))
                                mm.then_inc(s_gu, 1)
                        if n >= 1:
                            hid_transposes(e, n - 1)
                    for j in range(NDN):
                        i = NGU + j
                        pe.wait_ge(s_ld[i % RING], 48 * e + 16 * (i // RING + 1))
                        if j == 0:
                            if not (isinstance(e, int) and e == 0):
                                pe.wait_ge(s_y, e)
                        if j % 2 == 0:
                            pe.wait_ge(s_ht, 4 * e + j // 2 + 1)
                        wdn = ring[:, i % RING, :].rearrange("p (k c) -> p k c", k=2)
                        for k in range(2):
                            for c in range(2):
                                mm = pe.matmul(psY[:, c, :], hidT[:, 2 * j + k, :], wdn[:, k, 512 * c:512 * c + 512],
                                               start=(j == 0 and k == 0), stop=(j == NDN - 1 and k == 1))
                        mm.then_inc(s_dn, 1)
                        if j == 1:
                            hid_transposes(e, 3)
                        if j == 5 and not last:
                            pe.wait_ge(s_ht, 4 * e + 4)
                            route(e + 1)
                    if not last:
                        x_transposes(e + 1)

                pe.wait_ge(s_c, 80)
                route(0)
                x_transposes(0)
                body(0, 0, False)
                body(1, 1, False)
                with pe.Fori(2, NE - 2, 2) as e:
                    body(e, 0, False)
                    body(e + 1, 1, False)
                body(NE - 2, 0, False)
                body(NE - 1, 1, True)

            @block.scalar
            def _(act):
                one, so_far = raise_counts()

                def hi(e, i):
                    act.wait_ge(s_ld[i % RING], 48 * e + 16 * (i // RING + 1))
                    if not (isinstance(e, int) and e == 0 and i < SPLIT):
                        act.wait_ge(s_gu, NGU * e + i - SPLIT + 1)
                    act.activation(wh[:, i % SPLIT], ring[:, i % RING, :].rearrange("p (k c) -> p k c", k=4), ACT.Identity).then_inc(s_hi, 1)

                def silu(e, n):
                    act.wait_ge(s_gu, NGU * e + 4 * n + 2)
                    if n or not (isinstance(e, int) and e == 0):
                        act.wait_ge(s_hid, 4 * e + n)
                    act.activation(sg[:], psG[:, n % 2, :], ACT.Silu).then_inc(s_sg, 1)

                def take_hid(e, n):
                    act.wait_ge(s_hf, 4 * e + n + 1)
                    act.activation(hidT[:, 4 * n:4 * n + 4, :], psT[:, n % 2, :].rearrange("p (k c) -> p k c", k=4), ACT.Identity).then_inc(s_ht, 1)

                def x_high(e, par):
                    act.wait_ge(s_xt, e + 1)
                    act.activation(xh[:, par], xT[:], ACT.Identity).then_inc(s_xh, 1)

                def body(e, par, last):
                    for i in range(SPLIT, NGU):
                        hi(e, i)
                        if i in (5, 9, 13):
                            silu(e, (i - 5) // 4)
                        if i == 11 or i == 15:
                            take_hid(e, (i - 11) // 4)
                    silu(e, 3)
                    take_hid(e, 2)
                    take_hid(e, 3)
                    if not last:
                        for i in range(SPLIT):
                            hi(e + 1, i)
                        x_high(e + 1, 1 - par)
                    act.wait_ge(s_dn, NDN * e + NDN)
                    if not (isinstance(e, int) and e == 0):
                        act.wait_ge(s_sc, 16 * e)
                    act.activation(y[:].rearrange("p (a c) -> p a c", a=2), psY[:], ACT.Identity, scale=gate[:, par:par + 1]).then_inc(s_y, 1)

                for i in range(SPLIT):
                    hi(0, i)
                x_high(0, 0)
                body(0, 0, False)
                body(1, 1, False)
                with act.Fori(2, NE - 2, 2) as e:
                    body(e, 0, False)
                    body(e + 1, 1, False)
                body(NE - 2, 0, False)
                body(NE - 1, 1, True)

            @block.vector
            def _(dve):
                own_before = [0]
                one, so_far = raise_counts()

                def ranks(e, ts):
                    if ts[0] == 0:
                        dve.wait_ge(s_p, 32 * e + 32)
                        dve.memset(cnt[:, 0, 0:1], 0.0).then_inc(own_dve, one(own_dve))
                    for t in ts:
                        own_p = pcol[:, t:t + 1]
                        a = P * t
                        dve.wait_ge(own_dve, own_before[0] + so_far(own_dve))
                        if t:
                            dve.tensor_scalar(cmp[:, 0:a], prow[:, 0:a], own_p, None, ALU.is_ge, ALU.add,
                                              accum_out=cnt[:, t, 0:1]).then_inc(own_dve, one(own_dve))
                        dve.tensor_scalar(cmp[:, a:L], prow[:, a:L], own_p, None, ALU.is_gt, ALU.add,
                                          accum_out=cnt[:, t, 1:2]).then_inc(own_dve, one(own_dve))
                        dve.scalar_tensor_tensor(out=hot[:, t, :], in0=prow[:, a:a + P], scalar=own_p, in1=lower[:],
                                                 op0=ALU.is_equal, op1=ALU.mult, accum_out=cnt[:, t, 2:3]).then_inc(own_dve, one(own_dve))

                def slots(e):
                    dve.wait_ge(own_dve, own_before[0] + so_far(own_dve))
                    dve.tensor_reduce(rank[:], cnt[:], AX_X, ALU.add).then_inc(own_dve, one(own_dve))
                    dve.tensor_copy(vals[:, :, 1:2], pcol[:].unsqueeze(2)).then_inc(s_rank, 1)
                    dve.wait_ge(own_dve, own_before[0] + so_far(own_dve))
                    for t in range(TT - 1):
                        dve.tensor_scalar(hot[:, t, :], iota[:], rank[:, t:t + 1], None, ALU.is_equal).then_inc(own_dve, one(own_dve))
                    dve.tensor_scalar(hot[:, TT - 1, :], iota[:], rank[:, TT - 1:TT], None, ALU.is_equal).then_inc(s_hot, 1)

                def take_route(e, par):
                    dve.wait_ge(s_rf, e + 1)
                    if not (isinstance(e, int) and e < 2):
                        dve.wait_ge(s_sc, 16 * (e - 1))
                    dve.tensor_copy(gate[:, par:par + 1], psT[:, 0, 1:2]).then_inc(own_dve, one(own_dve))
                    dve.tensor_copy(idx[:, par, :], psT[:, 0, 0:1]).then_inc(s_rt, 1)

                def take_x(e, par):
                    dve.wait_ge(s_xf, e + 1)
                    dve.tensor_tensor(xT[:], psT[:].rearrange("p a (k c) -> p (a k) c", c=P),
                                      lnw[:].unsqueeze(2).to_broadcast([P, DT, P]), ALU.mult).then_inc(s_xt, 1)
                    dve.wait_ge(s_xh, e + 1)
                    dve.tensor_tensor(xl[:, par], xT[:], xh[:, par], ALU.subtract).then_inc(s_xl, 1)

                def lo(e, i):
                    dve.wait_ge(s_hi, NGU * e + i + 1)
                    dve.tensor_tensor(wl[:, i % SPLIT], ring[:, i % RING, :].rearrange("p (k c) -> p k c", k=4), wh[:, i % SPLIT],
                                      ALU.subtract).then_inc(s_lo, 1)

                def hidden(e, n):
                    dve.wait_ge(s_sg, 4 * e + n + 1)
                    dve.wait_ge(s_gu, NGU * e + 4 * n + 4)
                    if n >= 2:
                        dve.wait_ge(s_hf, 4 * e + n - 1)
                    dve.tensor_tensor(hid[:, n % 2, :], sg[:], psU[:, n % 2, :], ALU.mult).then_inc(s_hid, 1)

                def body(e, par, last):
                    for i in range(SPLIT, NGU):
                        lo(e, i)
                        if i in (7, 11, 15):
                            hidden(e, (i - 7) // 4)
                        if i in (5, 8, 10, 13) and not last:
                            ranks(e + 1, [(5, 8, 10, 13).index(i)])
                    hidden(e, 3)
                    if not last:
                        ranks(e + 1, [4, 5, 6, 7])
                        slots(e + 1)
                        take_route(e + 1, 1 - par)
                        lo(e + 1, 0)
                        lo(e + 1, 1)
                        take_x(e + 1, 1 - par)
                        lo(e + 1, 2)
                        lo(e + 1, 3)

                dve.wait_ge(s_c, 80)
                ranks(0, range(TT))
                slots(0)
                take_route(0, 0)
                for i in range(SPLIT):
                    lo(0, i)
                take_x(0, 0)
                before = so_far(own_dve)
                body(0, 0, False)
                per_expert = so_far(own_dve) - before
                body(1, 1, False)
                with dve.Fori(2, NE - 2, 2) as e:
                    one, so_far = raise_counts()
                    own_before[0] = before + per_expert * e
                    body(e, 0, False)
                    body(e + 1, 1, False)
                one, so_far = raise_counts()
                own_before[0] = before + per_expert * (NE - 2)
                body(NE - 2, 0, False)
                body(NE - 1, 1, True)


def embed_stage(nc, dram, scratch, out, tile_loaded, loads_before, ring, piece_loaded, p, wp, s_p):
    SHARED = (((0, 2), (2, 5), (5, 8)), ((0, 4), (4, 7), (7, 8)))
    with ExitStack() as ctx:
        sb = lambda name, shape, dt=F32: ctx.enter_context(nc.sbuf_tensor(name, shape, dt))
        ps = lambda name, n: ctx.enter_context(nc.psum_tensor(name, [P, n, 512], F32))
        sem = lambda name: ctx.enter_context(nc.semaphore(name))
        r, emb = (ring[:, RING // 2 * i:RING // 2 * (i + 1), :].rearrange("p a (b c) -> p (a b) c", c=D) for i in range(2))
        pT = sb("f_pT", [P, 2, 2, P])
        w = sb("f_w", [P, 2, 2, D])
        wh = sb("f_wh", [P, DT, D], F32R)
        wl = sb("f_wl", [P, DT, D], F32R)
        h = sb("f_h", [P, 2, D])
        hT = sb("f_hT", [P, DT, P])
        hh = sb("f_hh", [P, 2, DT, P], F32R)
        hl = sb("f_hl", [P, 2, DT, P], F32R)
        sg = sb("f_sg", [P, D])
        sq = sb("f_sq", [P, D])
        lnw = sb("f_lnw", [P, DT])
        fin = sb("f_fin", [P, D])
        ident = sb("f_ident", [P, P])
        ssq = sb("f_ssq", [P, 2, TT])
        rs = sb("f_rs", [P, 2, 4, TT])
        psT, psP, psG = ps("f_psT", 2), ps("f_psP", 2), ps("f_psG", 4)

        s_c, s_fin = sem("f_constants"), sem("f_final_w_loaded")
        pieces_before = 16 * (NGU + NDN) // RING * NE
        own_dve, own_act = sem("f_own_dve"), sem("f_own_act")
        s_pt, s_pT = sem("f_p_transposed"), sem("f_pT_taken")
        s_pp, s_emb = sem("f_embedding_product"), sem("f_embedding_taken")
        s_wh, s_wl = sem("f_wh_ready"), sem("f_wl_ready")
        s_sq, s_var, s_rt = sem("f_squares"), sem("f_variance"), sem("f_root")
        s_h, s_hf = sem("f_normed"), sem("f_h_transposed")
        s_hT, s_hh, s_hl = sem("f_hT_ready"), sem("f_hh_ready"), sem("f_hl_ready")
        s_g, s_sg, s_r2 = sem("f_gate_product"), sem("f_gate_ready"), sem("f_embedding_added")
        s_out, s_st = sem("f_out_ready"), sem("f_stored")

        with nc.Block() as block:
            @block.sync
            def _(sp):
                sp.dma_start(ident[:], dram["c_ident"]).then_inc(s_c, 16)
                sp.dma_start(lnw[:], dram["l_ln_ple"]).then_inc(s_c, 16)
                for i in range(4):
                    if i >= 2:
                        sp.wait_ge(s_wl, i - 1)
                    sp.dma_start(w[:, i % 2], dram["w_ple_gate"][0, 2 * P * i:2 * P * i + 2 * P, :].rearrange("(k p) c -> p k c", p=P)).then_inc(piece_loaded[i % 2], 16)
                    for t in (2 * i, 2 * i + 1):
                        sp.dma_start(r[:, t, :], scratch["r"][P * t:P * t + P, :]).then_inc(tile_loaded[t], 16)
                sp.dma_start(fin[:], dram["final_norm_w"].unsqueeze(0).to_broadcast([P, D])).then_inc(s_fin, 16)
                for t in range(TT):
                    sp.wait_ge(s_out, t + 1)
                    sp.dma_start(out[0, P * t:P * t + P, :], r[:, t, :]).then_inc(s_st, 16)
                sp.wait_ge(s_st, 16 * TT)

            @block.tensor
            def _(pe):
                pe.wait_ge(s_c, 32)
                pe.wait_ge(s_p, 32)
                for i in range(TT + 1):
                    if i < TT:
                        if i >= 2:
                            pe.wait_ge(s_pT, i - 1)
                        for k in range(2):
                            m = pe.transpose(psT[:, i % 2, P * k:P * k + P], p[:, i, P * k:P * k + P], ident[:])
                        m.then_inc(s_pt, 1)
                    if i >= 1:
                        t = i - 1
                        pe.wait_ge(s_pT, t + 1)
                        for c in range(2):
                            if t:
                                pe.wait_ge(s_emb, 2 * t + c - 1)
                            for k in range(2):
                                m = pe.matmul(psP[:, c, :], pT[:, t % 2, k, :], wp[:, k, 512 * c:512 * c + 512], start=(k == 0), stop=(k == 1))
                            m.then_inc(s_pp, 1)
                pe.wait_ge(s_pT, TT)
                for i in range(TT + 1):
                    if i < TT:
                        pe.wait_ge(s_h, i + 1)
                        if i:
                            pe.wait_ge(s_hT, i)
                        for k in range(DT):
                            m = pe.transpose(psT[:, k // 4, P * (k % 4):P * (k % 4) + P], h[:, i % 2, P * k:P * k + P], ident[:])
                        m.then_inc(s_hf, 1)
                    if i >= 1:
                        t = i - 1
                        pe.wait_ge(s_hh, t + 1)
                        pe.wait_ge(s_hl, t + 1)
                        pe.wait_ge(s_wl, 4)
                        for c in range(2):
                            n = 2 * t + c
                            if n >= 4:
                                pe.wait_ge(s_sg, n - 3)
                            for k in range(DT):
                                for j, (a, b) in enumerate(((hh, wh), (hl, wh), (hh, wl))):
                                    m = pe.matmul(psG[:, n % 4, :], a[:, t % 2, k, :], b[:, k, 512 * c:512 * c + 512],
                                                  start=(k == 0 and j == 0), stop=(k == DT - 1 and j == 2))
                            m.then_inc(s_g, 1)

            @block.scalar
            def _(act):
                one, so_far = raise_counts()

                def embedding(t):
                    act.wait_ge(s_pt, t + 1)
                    if t >= 2:
                        act.wait_ge(s_pp, 2 * (t - 2) + 2)
                    act.activation(pT[:, t % 2], psT[:, t % 2, 0:2 * P].rearrange("p (k c) -> p k c", k=2), ACT.Identity).then_inc(s_pT, one(s_pT))

                def take_embedding(t):
                    for c in range(2):
                        act.wait_ge(s_pp, 2 * t + c + 1)
                        act.activation(emb[:, t, 512 * c:512 * c + 512], psP[:, c, :], ACT.Identity).then_inc(s_emb, one(s_emb))

                def square(phase, t):
                    if so_far(s_pT):
                        act.wait_ge(s_pT, so_far(s_pT))
                    if so_far(s_emb):
                        act.wait_ge(s_emb, so_far(s_emb))
                    if so_far(s_sg):
                        act.wait_ge(s_sg, so_far(s_sg))
                    act.activation(sq[:], r[:, t, :], ACT.Square, accum_out=ssq[:, phase, t:t + 1]).then_inc(s_sq, one(s_sq))

                def root(phase, t):
                    for n, (a, b) in enumerate(SHARED[phase]):
                        if b == t + 1:
                            act.wait_ge(s_var, n + 1 + phase * len(SHARED[0]))
                            act.activation(rs[:, phase, 1, a:b], rs[:, phase, 0, a:b], ACT.Sqrt).then_inc(s_rt, 1)

                for t in range(TT):
                    embedding(t)
                    if t:
                        take_embedding(t - 1)
                    if t % 2 == 0:
                        i = t // 2
                        act.wait_ge(piece_loaded[i % 2], pieces_before + 16 * (i // 2 + 1))
                        act.activation(wh[:, 2 * i:2 * i + 2, :], w[:, i % 2], ACT.Identity).then_inc(s_wh, 1)
                    act.wait_ge(tile_loaded[t], loads_before + 16)
                    square(0, t)
                    root(0, t)
                take_embedding(TT - 1)
                for i in range(TT + 1):
                    if i < TT:
                        act.wait_ge(s_hT, i + 1)
                        if i >= 2:
                            act.wait_ge(s_g, 2 * (i - 2) + 2)
                        act.activation(hh[:, i % 2], hT[:], ACT.Identity).then_inc(s_hh, 1)
                    if i >= 1:
                        t = i - 1
                        if t:
                            act.wait_ge(s_r2, t)
                        for c in range(2):
                            act.wait_ge(s_g, 2 * t + c + 1)
                            act.activation(sg[:, 512 * c:512 * c + 512], psG[:, (2 * t + c) % 4, :], ACT.Sigmoid).then_inc(s_sg, one(s_sg))
                        act.wait_ge(s_r2, t + 1)
                        square(1, t)
                        root(1, t)

            @block.vector
            def _(dve):
                one, so_far = raise_counts()

                def inverse_root(phase, a, b, n):
                    dve.wait_ge(s_sq, phase * TT + b)
                    if so_far(s_r2):
                        dve.wait_ge(s_r2, so_far(s_r2))
                    dve.tensor_scalar(rs[:, phase, 0, a:b], ssq[:, phase, a:b], 1.0 / D, EPS, ALU.mult, ALU.add).then_inc(s_var, one(s_var))
                    dve.wait_ge(s_rt, n + 1)
                    dve.reciprocal(rs[:, phase, 2, a:b], rs[:, phase, 1, a:b]).then_inc(own_dve, one(own_dve))
                    newton(dve, own_dve, one, so_far, rs[:, phase, :, a:b])

                def low_halves(i):
                    dve.wait_ge(s_wh, i + 1)
                    dve.tensor_tensor(wl[:, 2 * i:2 * i + 2, :], w[:, i % 2], wh[:, 2 * i:2 * i + 2, :], ALU.subtract).then_inc(s_wl, 1)

                low_halves(0)
                inverse_root(0, *SHARED[0][0], 0)
                low_halves(1)
                inverse_root(0, *SHARED[0][1], 1)
                low_halves(2)
                low_halves(3)
                inverse_root(0, *SHARED[0][2], 2)
                dve.wait_ge(s_c, 32)
                dve.wait_ge(s_fin, 16)

                def normed(t):
                    if t >= 2:
                        dve.wait_ge(s_hf, t - 1)
                    dve.tensor_scalar(h[:, t % 2, :], r[:, t, :], rs[:, 0, 2, t:t + 1], None, ALU.mult).then_inc(s_h, one(s_h))

                normed(0)
                for i in range(TT + 1):
                    if i < TT:
                        if i + 1 < TT:
                            normed(i + 1)
                        dve.wait_ge(s_hf, i + 1)
                        if so_far(s_h):
                            dve.wait_ge(s_h, so_far(s_h))
                        if so_far(s_r2):
                            dve.wait_ge(s_r2, so_far(s_r2))
                        dve.tensor_tensor(hT[:], psT[:].rearrange("p a (k c) -> p (a k) c", c=P),
                                                     lnw[:].unsqueeze(2).to_broadcast([P, DT, P]), ALU.mult).then_inc(s_hT, one(s_hT))
                        dve.wait_ge(s_hh, i + 1)
                        dve.wait_ge(s_hT, so_far(s_hT))
                        dve.tensor_tensor(hl[:, i % 2], hT[:], hh[:, i % 2], ALU.subtract).then_inc(s_hl, one(s_hl))
                    if i >= 1:
                        t = i - 1
                        dve.wait_ge(s_sg, 2 * t + 2)
                        dve.wait_ge(s_emb, 2 * t + 2)
                        dve.tensor_tensor(emb[:, t, :], emb[:, t, :], sg[:], ALU.mult).then_inc(own_dve, one(own_dve))
                        dve.wait_ge(own_dve, so_far(own_dve))
                        dve.tensor_tensor(r[:, t, :], r[:, t, :], emb[:, t, :], ALU.add).then_inc(s_r2, one(s_r2))
                        for n, (a, b) in enumerate(SHARED[1]):
                            if b == t + 1:
                                inverse_root(1, a, b, len(SHARED[0]) + n)
                                for u in range(a, b):
                                    dve.scalar_tensor_tensor(out=r[:, u, :], in0=r[:, u, :], scalar=rs[:, 1, 2, u:u + 1], in1=fin[:],
                                                                        op0=ALU.mult, op1=ALU.mult).then_inc(s_out, one(s_out))


def program(nc, dram, out):
    scratch = {name: nc.dram_tensor("s_" + name, shape, F32, kind="Internal").ap() for name, shape in {
        "hy": (3, L, HW), "code": (2 * RANK, L), "qk": (2 * QK // P, P, L), "vg": (2, L, GW),
        "spec": (ORDER, 2, P, GROUPS, 2, HALF), "mix": (L, D), "r": (L, D), "h2": (L, D),
        "prow": (NE, L), "pcol": (NE, P, TT)}.items()}
    tile_loaded = [nc.alloc_semaphore(f"tile_loaded{t}") for t in range(TT)]
    project_stage(nc, dram, scratch, tile_loaded)
    mix_stage(nc, dram, scratch)
    with nc.sbuf_tensor("ring", [P, RING, 4 * 512], F32) as ring:
        piece_loaded = [nc.alloc_semaphore(f"piece_loaded{i}") for i in range(RING)]
        residual_stage(nc, dram, scratch, tile_loaded, 16, ring, piece_loaded)
        with nc.sbuf_tensor("ple", [P, TT, PLE], F32) as p, nc.sbuf_tensor("ple_proj", [P, 2, D], F32) as wp:
            p_loaded = nc.alloc_semaphore("ple_loaded")
            expert_stage(nc, dram, scratch, ring, piece_loaded, p, wp, p_loaded)
            embed_stage(nc, dram, scratch, out, tile_loaded, 48, ring, piece_loaded, p, wp, p_loaded)


INPUTS = ["x", "p", "w_in", "gla_wa_f", "gla_wa_b", "gla_norm_w", "hy_f_w1", "hy_f_w2", "hy_f_w3", "hy_bias", "w_out", "ln_ffn_w",
          "w_router", "w_gate_e", "w_up_e", "w_down_e", "w_ple_gate", "w_ple_proj", "final_norm_w"]


def by_partition(a):
    a = np.asarray(a)
    return np.ascontiguousarray(np.moveaxis(a.reshape(*a.shape[:-1], -1, P), -1, 0))


def kernel(**inputs):
    import concourse.bacc as bacc
    from concourse.bass_utils import run_bass_kernel_spmd as run
    nc = bacc.Bacc("TRN2", target_bir_lowering=False, num_devices=1)
    arrays = {name: np.ascontiguousarray(inputs[name]) for name in INPUTS}
    arrays.update(shape_constants())
    arrays["l_ln_mix"] = by_partition(inputs["ln_mix_w"][0])
    arrays["l_ln_ffn"] = by_partition(inputs["ln_ffn_w"][0])
    arrays["l_ln_ple"] = by_partition(inputs["ln_ple_w"][0])
    arrays["l_conv_w"] = by_partition(inputs["hy_conv_w"][0])
    arrays["l_conv_b"] = by_partition(inputs["hy_conv_b"][0])
    arrays["l_gate_b"] = by_partition(np.stack([inputs["gla_ba_f"][0], inputs["gla_ba_b"][0]]))
    arrays["l_filter"] = np.ascontiguousarray(np.stack([inputs[n][0] for n in ("hy_f_b1", "hy_f_freq1", "hy_f_b2", "hy_f_freq2")], 1))
    dram = {name: nc.dram_tensor("in_" + name, a.shape, mybir.dt.from_np(a.dtype), kind="ExternalInput").ap() for name, a in arrays.items()}
    out = nc.dram_tensor("out", (1, L, D), F32, kind="ExternalOutput").ap()
    program(nc, dram, out)
    r = run(nc, [{"in_" + name: a for name, a in arrays.items()}], core_ids=[0])
    return r.results[0]["out"]
```

```python
from contextlib import ExitStack
import math

import numpy as np
import concourse.bass as bass
from concourse import mybir

ALU = mybir.AluOpType
ACT = mybir.ActivationFunctionType
AX_X = mybir.AxisListType.X
F32 = mybir.dt.float32
F32R = mybir.dt.float32r
I32 = mybir.dt.int32

P = 128
D = 1024
L = 1024
DT = D // P
TT = L // P
EPS = 1e-6
HEADS, DK, DV = 4, D // 16, D // 8
QK, GW, RANK = HEADS * DK, HEADS * DV, 16
TAU = 16.0
HW = D - GW
ORDER, FFN, BANDS = 2, 64, 8
EMB = 1 + 2 * BANDS
NE = 16
CAP = 2 * L // NE
FF = 2 * D
PLE = 256
Q0, K0, V0, G0 = 0, QK, 2 * QK, 2 * QK + GW
C0 = G0 + GW
H0 = C0 + 2 * RANK
IN_COLS = H0 + 3 * HW

NFFT = 2 * L
HALF = HW // 2
GROUPS = 8
RESIDUES = [(0, 0), (4, -1), (2, -1), (6, 1), (1, -1), (9, -1), (5, -1), (13, -1)]
C45 = math.cos(math.pi / 4)
C22 = math.cos(math.pi / 8)
T22 = math.tan(math.pi / 8)


def shape_constants():
    p = np.arange(P, dtype=np.float64)[:, None]
    j = np.arange(P, dtype=np.float64)[None, :]
    fwd = np.zeros((GROUPS, 4, P, P))
    weight = np.full((GROUPS, 2, P), 2.0 / NFFT)
    for g, (r, s) in enumerate(RESIDUES):
        if g == 0:
            for part, r0 in ((0, 0), (1, 8)):
                th = 2 * np.pi * p * (r0 + 16 * j[:, :64]) / NFFT
                fwd[0, part, :, 64 * part:64 * part + 64] = np.cos(th)
                fwd[0, 2 + part, :, 64 * part:64 * part + 64] = -np.sin(th)
            fwd[0, 2, :, 0] = (-1.0) ** np.arange(P)
            weight[0, :, 0] = 1.0 / NFFT
        else:
            th = 2 * np.pi * p * (r + 16 * j) / NFFT
            mr, mi = np.cos(th), -np.sin(th)
            fwd[g, 0], fwd[g, 1] = mr, -mi * s
            fwd[g, 2], fwd[g, 3] = mi, mr * s
    inv = np.zeros((GROUPS, 4, P, P))
    for g in range(GROUPS):
        for q in range(4):
            inv[g, q] = fwd[g, q].T * weight[g, q // 2][:, None]
    f32 = np.float32
    t = np.linspace(0.0, 1.0, L, dtype=f32)[:, None]
    w_pos = (f32(2.0 * math.pi) * np.arange(L, dtype=f32)[:, None] / f32(L)).astype(f32)
    f = np.linspace(1e-4, BANDS - 1, BANDS, dtype=f32)[None]
    z = np.concatenate([t, np.cos(f * w_pos), -np.sin(f * w_pos)], axis=-1).astype(f32)
    lo, hi = math.log(1e-2) / 1.5, math.log(1e-2) / 0.3
    deltas = np.abs(np.linspace(lo, hi, HW, dtype=f32))
    decay = np.exp(-t * deltas[None]).astype(f32)
    s_idx, t_idx = np.arange(P)[:, None], np.arange(P)[None, :]
    same = (s_idx // 64) == (t_idx // 64)
    masks = np.stack([same & (s_idx <= t_idx), same & (s_idx > t_idx)], 1).astype(np.int32)
    return {
        "c_fwd": np.ascontiguousarray(fwd.transpose(2, 0, 1, 3).reshape(P, -1).astype(f32)),
        "c_inv": np.ascontiguousarray(inv.transpose(2, 0, 1, 3).reshape(P, -1).astype(f32)),
        "c_z": np.ascontiguousarray(z.T),
        "c_decay": decay,
        "c_ident": np.eye(P, dtype=f32),
        "c_mask": np.ascontiguousarray(masks),
        "c_iota": np.tile(np.arange(P, dtype=f32)[None], (P, 1)),
        "c_tok": np.ascontiguousarray(np.arange(L, dtype=f32).reshape(TT, P).T),
        "c_lower": (s_idx > t_idx).astype(f32),
        "c_sel": np.ascontiguousarray(np.repeat(np.eye(NE, dtype=f32)[:, :, None], P, 2).reshape(NE, NE * P)),
    }


def raise_counts():
    raised = {}

    def one(sem):
        raised[sem] = raised.get(sem, 0) + 1
        return 1

    def so_far(sem):
        return raised.get(sem, 0)

    return one, so_far


def forward_tree(dve, own, one, so_far, U, V, T, tree_done):
    s, d, pp, m, A, B, x1, x3 = (T[:, a:b, :] for a, b in
                                 ((0, 4), (4, 8), (8, 10), (10, 12), (12, 14), (14, 16), (16, 18), (18, 20)))
    add, sub, mul = ALU.add, ALU.subtract, ALU.mult
    dve.tensor_tensor(s, U[:, 0:4, :], U[:, 4:8, :], add).then_inc(own, one(own))
    dve.tensor_tensor(d, U[:, 0:4, :], U[:, 4:8, :], sub).then_inc(own, one(own))
    dve.scalar_tensor_tensor(out=x1[:, 0, :], in0=U[:, 5, :], scalar=-T22, in1=U[:, 1, :], op0=mul, op1=add).then_inc(own, one(own))
    dve.scalar_tensor_tensor(out=x1[:, 1, :], in0=U[:, 1, :], scalar=T22, in1=U[:, 5, :], op0=mul, op1=add).then_inc(own, one(own))
    dve.scalar_tensor_tensor(out=x3[:, 0, :], in0=U[:, 3, :], scalar=T22, in1=U[:, 7, :], op0=mul, op1=sub).then_inc(own, one(own))
    dve.scalar_tensor_tensor(out=x3[:, 1, :], in0=U[:, 7, :], scalar=T22, in1=U[:, 3, :], op0=mul, op1=add).then_inc(own, one(own))
    dve.wait_ge(own, so_far(own))
    dve.tensor_tensor(pp, s[:, 0:2, :], s[:, 2:4, :], add).then_inc(own, one(own))
    dve.tensor_tensor(V[:, 2:4, :], s[:, 0:2, :], s[:, 2:4, :], sub).then_inc(own, one(own))
    dve.tensor_tensor(m[:, 0, :], d[:, 1, :], d[:, 3, :], sub).then_inc(own, one(own))
    dve.tensor_tensor(m[:, 1, :], d[:, 1, :], d[:, 3, :], add).then_inc(own, one(own))
    ds = T[:, 6:1:-4, :]
    u04 = U[:, 0:5:4, :]
    dve.scalar_tensor_tensor(out=A, in0=ds, scalar=C45, in1=u04, op0=mul, op1=add).then_inc(own, one(own))
    dve.scalar_tensor_tensor(out=B, in0=ds, scalar=-C45, in1=u04, op0=mul, op1=add).then_inc(own, one(own))
    dve.wait_ge(own, so_far(own))
    dve.tensor_tensor(V[:, 0, :], pp[:, 0, :], pp[:, 1, :], add).then_inc(own, one(own))
    dve.tensor_tensor(V[:, 1, :], pp[:, 0, :], pp[:, 1, :], sub).then_inc(own, one(own))
    d02 = T[:, 4:7:2, :]
    dve.scalar_tensor_tensor(out=V[:, 4:6, :], in0=m, scalar=C45, in1=d02, op0=mul, op1=add).then_inc(own, one(own))
    dve.scalar_tensor_tensor(out=V[:, 6:8, :], in0=m, scalar=-C45, in1=d02, op0=mul, op1=add).then_inc(own, one(own))
    Cc, Dd = T[:, 0:2, :], T[:, 2:4, :]
    dve.tensor_tensor(Cc, x1, x3, add).then_inc(own, one(own))
    dve.tensor_tensor(Dd, x1, x3, sub).then_inc(own, one(own))
    dve.wait_ge(own, so_far(own))
    dve.scalar_tensor_tensor(out=V[:, 8:10, :], in0=Cc, scalar=C22, in1=A, op0=mul, op1=add).then_inc(own, one(own))
    dve.scalar_tensor_tensor(out=V[:, 10:12, :], in0=Cc, scalar=-C22, in1=A, op0=mul, op1=add).then_inc(own, one(own))
    Dnr, Bnr = T[:, 3:1:-1, :], T[:, 15:13:-1, :]
    dve.scalar_tensor_tensor(out=V[:, 13:15, :], in0=Dd, scalar=C22, in1=Bnr, op0=mul, op1=add).then_inc(own, one(own))
    dve.scalar_tensor_tensor(out=V[:, 12:16:3, :], in0=Dnr, scalar=-C22, in1=B, op0=mul, op1=add).then_inc(tree_done, one(tree_done))


def newton(dve, own, one, so_far, rs):
    v, r, u = rs[:, 0, :], rs[:, 2, :], rs[:, 3, :]
    dve.wait_ge(own, so_far(own))
    dve.tensor_tensor(u, r, r, ALU.mult).then_inc(own, one(own))
    dve.wait_ge(own, so_far(own))
    dve.tensor_tensor(u, u, v, ALU.mult).then_inc(own, one(own))
    dve.wait_ge(own, so_far(own))
    dve.tensor_scalar(u, u, -0.5, 1.5, ALU.mult, ALU.add).then_inc(own, one(own))
    dve.wait_ge(own, so_far(own))
    dve.tensor_tensor(r, r, u, ALU.mult).then_inc(own, one(own))
    dve.wait_ge(own, so_far(own))


def filter_stage(nc, dram, scratch, own, tile_loaded, hT):
    own_dve, own_act, one, so_far = own
    WC = 256
    WB = 2
    with ExitStack() as ctx:
        sb = lambda name, shape, dt=F32: ctx.enter_context(nc.sbuf_tensor(name, shape, dt))
        sem = lambda name: ctx.enter_context(nc.semaphore(name))
        x_sb = sb("x_sb", [P, TT, D])
        V = x_sb[:].rearrange("p t (a c) -> p (t a) c", c=HALF).rearrange("p (b s) c -> p b s c", b=2)
        w_sb = sb("w_sb", [P, WB, DT, WC])
        fwd = sb("fwd", [P, GROUPS, 4, P])
        ident = sb("ident", [P, P])
        lnw = sb("lnw", [P, DT])
        ssq = sb("ssq", [P, TT])
        rstd = sb("rstd", [P, 4, TT])
        cw = sb("cw", [P, 3, 12])
        cb = sb("cb", [P, 12])
        tap = sb("tap", [P, 2, L])
        zT = sb("zT", [EMB, L])
        fw1 = sb("fw1", [EMB, FFN])
        fw2 = sb("fw2", [FFN, FFN])
        fcol = sb("fcol", [FFN, 4])
        w3 = sb("w3", [FFN, ORDER, 2, HW])
        w3eo = sb("w3eo", [FFN, 2, ORDER, HW])
        arg = sb("arg", [FFN, L])
        red = sb("red", [FFN, L])
        hdn1 = red
        hdn2 = sb("hdn2", [FFN, L])
        hbias = sb("hbias", [1, ORDER, HW])
        row0 = hbias
        decay = sb("decay", [P, TT, HALF])
        eo = sb("eo", [P, TT, HALF])
        T = sb("T", [P, 20, HALF])
        spec = sb("spec", [P, GROUPS, 2, HALF])
        nyq = sb("nyq", [1, HALF])
        stage = sb("stage", [P, 2, L])
        acc = ctx.enter_context(nc.psum_tensor("acc", [P, 2, L], F32))
        psA = ctx.enter_context(nc.psum_tensor("psA", [P, 2, 512], F32))
        psB = ctx.enter_context(nc.psum_tensor("psB", [P, 2, 512], F32))

        s_x = tile_loaded
        s_small = sem("small_loaded")
        s_tab = sem("tables_loaded")
        s_filt = sem("filter_weights_loaded")
        s_decay = sem("decay_loaded")
        s_w = [sem(f"w_loaded{i}") for i in range(WB)]
        s_ssq = sem("squares_summed")
        s_var = sem("variance_ready")
        s_root = sem("root_ready")
        s_xs = sem("x_scaled")
        s_pt = sem("h_transposed")
        s_ht = sem("hT_ready")
        s_pre = sem("filter_preact")
        s_arg = sem("filter_arg_reduced")
        s_hdn = sem("filter_hidden")
        s_w3 = sem("w3_combined")
        s_row = sem("row0_product")
        s_row0 = sem("row0_ready")
        s_acc = sem("acc_done")
        s_gen = sem("filter_product")
        s_genu = sem("filter_taken")
        s_tree = sem("kernel_tree_done")
        s_spec = sem("spectrum_product")
        s_specw = sem("spectrum_staged")
        s_specs = sem("spectrum_stored")
        s_tap0 = sem("centre_tap")
        s_conv = sem("conv_done")
        s_store = [sem(f"stage_stored{i}") for i in range(2)]

        HY = 3 * HW // P
        PERW = WC // P
        rounds = [(h, o, eopart) for h in range(2) for o in range(ORDER) for eopart in range(2)]
        halves = [range(2 * len(rounds) * i // HY, 2 * len(rounds) * (i + 1) // HY) for i in range(HY)]

        def spectra_after(i):
            return (halves[i][-1]) // 2

        def taken(i):
            m = spectra_after(i)
            return 2 * DT + 2 * (i + 1) + 4 * m + (m + 1) // 2

        with nc.Block() as block:
            @block.sync
            def _(sp):
                sp.dma_start(ident[:], dram["c_ident"]).then_inc(s_small, 16)
                sp.dma_start(lnw[:], dram["l_ln_mix"]).then_inc(s_small, 16)
                for t in range(TT):
                    sp.dma_start(x_sb[:, t, :], dram["x"][0, P * t:P * t + P, :]).then_inc(s_x[t], 16)
                sp.dma_start(zT[:], dram["c_z"]).then_inc(s_filt, 16)
                sp.dma_start(fw1[:], dram["hy_f_w1"][0]).then_inc(s_filt, 16)
                sp.dma_start(fw2[:], dram["hy_f_w2"][0]).then_inc(s_filt, 16)
                sp.dma_start(fcol[:], dram["l_filter"]).then_inc(s_filt, 16)
                sp.dma_start(w3[:], dram["hy_f_w3"][0].rearrange("k (o d c) -> k o d c", o=ORDER, d=2)).then_inc(s_filt, 16)
                sp.dma_start(hbias[:], dram["hy_bias"]).then_inc(s_filt, 16)
                for i in range(HY // PERW):
                    if i >= WB:
                        sp.wait_ge(s_acc, PERW * (i - WB + 1))
                    c = H0 + WC * i
                    sp.dma_start(w_sb[:, i % WB], dram["w_in"][0, :, c:c + WC].rearrange("(k p) n -> p k n", p=P)).then_inc(s_w[i % WB], 16)
                    if i == 0:
                        sp.dma_start(cw[:], dram["l_conv_w"]).then_inc(s_tab, 16)
                        sp.dma_start(cb[:], dram["l_conv_b"]).then_inc(s_tab, 16)
                        sp.dma_start(fwd[:], dram["c_fwd"].rearrange("p (g q c) -> p g q c", g=GROUPS, q=4)).then_inc(s_tab, 16)
                        sp.dma_start(decay[:], dram["c_decay"][:, 0:HALF].rearrange("(a p) c -> p a c", p=P)).then_inc(s_decay, 16)
                    if i == HY // PERW - 2:
                        sp.wait_ge(s_genu, 4 * 4)
                        sp.dma_start(decay[:], dram["c_decay"][:, HALF:HW].rearrange("(a p) c -> p a c", p=P)).then_inc(s_decay, 16)

            @block.gpsimd
            def _(pool):
                for i in range(HY):
                    pool.wait_ge(s_ht, taken(i))
                    dst = scratch["hy"][i * P // HW, :, (i * P) % HW:(i * P) % HW + P].rearrange("(a p) c -> p a c", p=P)
                    pool.dma_start(dst, stage[:, i % 2, :].rearrange("p (a c) -> p a c", c=P)).then_inc(s_store[i % 2], 16)
                    if i % 3 == 2:
                        h, o, _ = rounds[2 * (i // 3)]
                        pool.wait_ge(s_specw, i // 3 + 1)
                        pool.dma_start(scratch["spec"][o, h], spec[:]).then_inc(s_specs, 16)
                pool.wait_ge(s_store[0], 16 * (HY // 2))
                pool.wait_ge(s_store[1], 16 * (HY // 2))
                pool.wait_ge(s_specs, 16 * (HY // 3))

            @block.tensor
            def _(pe):
                pe.wait_ge(s_filt, 16 * 6)
                for c in range(2):
                    pe.matmul(psB[0:FFN, c, :], fw1[:], zT[:, 512 * c:512 * c + 512], start=True, stop=True).then_inc(s_pre, 1)
                pe.wait_ge(s_small, 32)
                for b in range(2 * DT):
                    dt, th = b % DT, b // DT
                    if dt == 0:
                        pe.wait_ge(s_xs, 4 * th + 4)
                    if b >= 2:
                        pe.wait_ge(s_ht, b - 1)
                    for t in range(4):
                        m = pe.transpose(psA[:, b % 2, P * t:P * t + P], x_sb[:, 4 * th + t, P * dt:P * dt + P], ident[:])
                    m.then_inc(s_pt, 1)
                pe.wait_ge(s_hdn, 1)
                for c in range(2):
                    pe.matmul(psB[0:FFN, c, :], fw2[:], hdn1[:, 512 * c:512 * c + 512], start=True, stop=True).then_inc(s_pre, 1)
                pe.wait_ge(s_hdn, 2)
                for o in range(ORDER):
                    pe.matmul(psB[0:1, o, :], hdn2[:, 0:1], w3[:, o, 0, :], start=True, stop=True).then_inc(s_row, 1)
                pe.wait_ge(s_w3, 2)
                pe.wait_ge(s_row0, 1)

                def gen(r, chunks):
                    h, o, part = rounds[r]
                    for c in chunks:
                        n = 4 * r + c
                        if n >= 2:
                            pe.wait_ge(s_genu, n - 1)
                        for a in (2 * c, 2 * c + 1):
                            m = pe.matmul(psB[:, n % 2, HALF * (a % 2):HALF * (a % 2) + HALF], hdn2[:, P * a:P * a + P],
                                          w3eo[:, part, o, HALF * h:HALF * h + HALF], start=True, stop=True)
                        m.then_inc(s_gen, 1)

                used = [2 * DT]

                def spectrum(r):
                    h, o, part = rounds[r]
                    pe.wait_ge(s_tree, r + 1)
                    Vr = V[:, r % 2]
                    for c in range(4):
                        pe.wait_ge(s_ht, used[0] - 1)
                        for g in (2 * c, 2 * c + 1):
                            dst = psA[:, used[0] % 2, HALF * (g % 2):HALF * (g % 2) + HALF]
                            for q in range(2):
                                m = pe.matmul(dst, fwd[:, g, 2 * part + q, :], Vr[:, 2 * g + q, :], start=(q == 0), stop=(q == 1))
                        m.then_inc(s_pt, 1)
                        used[0] += 1
                    if part == 0:
                        pe.wait_ge(s_ht, used[0] - 1)
                        pe.matmul(psA[0:1, used[0] % 2, 0:HALF], fwd[:, 0, 2, 0:1], Vr[:, 0, :], start=True, stop=True).then_inc(s_pt, 1)
                        used[0] += 1

                def transposes(i):
                    pe.wait_ge(s_conv, i + 1)
                    for c in range(2):
                        pe.wait_ge(s_ht, used[0] - 1)
                        for a in range(4):
                            t = 4 * c + a
                            m = pe.transpose(psA[:, used[0] % 2, P * a:P * a + P], tap[:, i % 2, P * t:P * t + P], ident[:])
                        m.then_inc(s_pt, 1)
                        used[0] += 1

                pe.wait_ge(s_ht, 2 * DT)
                for i in range(HY):
                    pe.wait_ge(s_w[i // PERW % WB], 16 * (i // PERW // WB + 1))
                    if i >= 2:
                        pe.wait_ge(s_conv, i - 1)
                    off = P * (i % PERW)
                    for c in range(2):
                        for k in range(DT):
                            m = pe.matmul(acc[:, i % 2, 512 * c:512 * c + 512], w_sb[:, i // PERW % WB, k, off:off + P],
                                          hT[:, k, 512 * c:512 * c + 512], start=(k == 0), stop=(k == DT - 1))
                    m.then_inc(s_acc, 1)
                    if i == 0:
                        pe.wait_ge(s_tab, 16 * 3)
                    else:
                        transposes(i - 1)
                    for q in halves[i]:
                        if q % 2 == 0 and q:
                            spectrum(q // 2 - 1)
                        gen(q // 2, (0, 1) if q % 2 == 0 else (2, 3))
                transposes(HY - 1)
                spectrum(len(rounds) - 1)

            @block.vector
            def _(dve):

                def reduce_arg(layer):
                    for c in range(2):
                        dve.wait_ge(s_pre, 2 * layer + c + 1)
                        dve.tensor_scalar(arg[:, 512 * c:512 * c + 512], psB[0:FFN, c, :], fcol[:, 2 * layer:2 * layer + 1],
                                                   fcol[:, 2 * layer + 1:2 * layer + 2], ALU.add, ALU.mult).then_inc(own_dve, one(own_dve))
                    dve.wait_ge(own_dve, so_far(own_dve))
                    big = 1.5 * 2.0 ** 23
                    dve.tensor_scalar(red[:], arg[:], 1.0 / (2 * math.pi), big, ALU.mult, ALU.add).then_inc(own_dve, one(own_dve))
                    dve.wait_ge(own_dve, so_far(own_dve))
                    dve.tensor_scalar(red[:], red[:], big, None, ALU.subtract).then_inc(own_dve, one(own_dve))
                    dve.wait_ge(own_dve, so_far(own_dve))
                    two_pi_hi = 6.28125
                    for part in (two_pi_hi, 2 * math.pi - two_pi_hi):
                        dve.scalar_tensor_tensor(out=arg[:], in0=red[:], scalar=-part, in1=arg[:], op0=ALU.mult, op1=ALU.add).then_inc(own_dve, one(own_dve))
                        dve.wait_ge(own_dve, so_far(own_dve))
                    edge = float(np.nextafter(np.float32(math.pi), np.float32(0)))
                    dve.tensor_scalar(arg[:], arg[:], edge, -edge, ALU.min, ALU.max).then_inc(s_arg, one(s_arg))

                dve.wait_ge(s_filt, 16 * 6)
                reduce_arg(0)
                for part, op in ((0, ALU.add), (1, ALU.subtract)):
                    dve.tensor_tensor(w3eo[:, part], w3[:, :, 0, :], w3[:, :, 1, :], op).then_inc(s_w3, one(s_w3))
                dve.wait_ge(s_ssq, TT)
                dve.wait_ge(s_w3, so_far(s_w3))
                dve.tensor_scalar(rstd[:, 0, :], ssq[:], 1.0 / D, EPS, ALU.mult, ALU.add).then_inc(s_var, one(s_var))
                dve.wait_ge(s_root, 1)
                dve.reciprocal(rstd[:, 2, :], rstd[:, 1, :]).then_inc(own_dve, one(own_dve))
                dve.wait_ge(own_dve, so_far(own_dve))
                newton(dve, own_dve, one, so_far, rstd)
                for t in range(TT):
                    dve.tensor_scalar(x_sb[:, t, :], x_sb[:, t, :], rstd[:, 2, t:t + 1], None, ALU.mult).then_inc(s_xs, one(s_xs))
                dve.wait_ge(s_hdn, 1)
                reduce_arg(1)
                dve.wait_ge(s_row, 2)
                dve.wait_ge(s_arg, so_far(s_arg))
                dve.tensor_tensor(row0[:], psB[0:1, :, :], hbias[:], ALU.add).then_inc(s_row0, one(s_row0))

                def conv(i):
                    dve.wait_ge(s_tap0, i + 1)
                    t, a = tap[:, i % 2, :], acc[:, i % 2, :]
                    dve.scalar_tensor_tensor(out=t[:, 1:L], in0=a[:, 0:L - 1], scalar=cw[:, 0, i:i + 1], in1=t[:, 1:L],
                                                      op0=ALU.mult, op1=ALU.add).then_inc(own_dve, one(own_dve))
                    dve.wait_ge(own_dve, so_far(own_dve))
                    dve.scalar_tensor_tensor(out=t[:, 0:L - 1], in0=a[:, 1:L], scalar=cw[:, 2, i:i + 1], in1=t[:, 0:L - 1],
                                                        op0=ALU.mult, op1=ALU.add).then_inc(s_conv, one(s_conv))

                def take(r, chunks):
                    h, o, part = rounds[r]
                    dve.wait_ge(s_decay, 16 * (h + 1))
                    if so_far(s_conv):
                        dve.wait_ge(s_conv, so_far(s_conv))
                    if so_far(s_tree):
                        dve.wait_ge(s_tree, so_far(s_tree))
                    if so_far(s_genu):
                        dve.wait_ge(s_genu, so_far(s_genu))
                    for c in chunks:
                        dve.wait_ge(s_gen, 4 * r + c + 1)
                        dve.tensor_tensor(eo[:, 2 * c:2 * c + 2, :], psB[:, (4 * r + c) % 2, :].rearrange("p (a c) -> p a c", a=2),
                                                     decay[:, 2 * c:2 * c + 2, :], ALU.mult).then_inc(s_genu, one(s_genu))

                for i in range(HY):
                    conv(i)
                    for q in halves[i]:
                        r = q // 2
                        h, o, part = rounds[r]
                        if q % 2 == 0:
                            take(r, (0, 1))
                            continue
                        take(r, (2, 3))
                        dve.wait_ge(s_genu, so_far(s_genu))
                        if part == 0:
                            dve.tensor_copy(eo[0:1, 0, :], row0[0:1, o, HALF * h:HALF * h + HALF]).then_inc(own_dve, one(own_dve))
                            dve.wait_ge(own_dve, so_far(own_dve))
                        forward_tree(dve, own_dve, one, so_far, eo[:], V[:, r % 2], T[:], s_tree)

            @block.scalar
            def _(act):
                for t in range(TT):
                    act.wait_ge(s_x[t], 16)
                    if so_far(s_ssq):
                        act.wait_ge(s_ssq, so_far(s_ssq))
                    act.activation(acc[:, 0, :], x_sb[:, t, :], ACT.Square, accum_out=ssq[:, t:t + 1]).then_inc(s_ssq, one(s_ssq))
                act.wait_ge(s_var, 1)
                act.activation(rstd[:, 1, :], rstd[:, 0, :], ACT.Sqrt).then_inc(s_root, 1)
                act.wait_ge(s_arg, 1)
                act.activation(hdn1[:], arg[:], ACT.Sin).then_inc(s_hdn, 1)
                used = [0]

                def take(dst, src, **kw):
                    act.wait_ge(s_pt, used[0] + 1)
                    used[0] += 1
                    act.activation(dst, src, ACT.Identity, **kw).then_inc(s_ht, one(s_ht))

                act.wait_ge(s_small, 32)
                for b in range(2 * DT):
                    dt, th = b % DT, b // DT
                    take(hT[:, dt, 512 * th:512 * th + 512], psA[:, b % 2, :], scale=lnw[:, dt:dt + 1])
                act.wait_ge(s_arg, 2)
                act.activation(hdn2[:], arg[:], ACT.Sin).then_inc(s_hdn, 1)
                act.wait_ge(s_tab, 16 * 3)

                def spectrum(r):
                    h, o, part = rounds[r]
                    if part == 0 and r >= 2:
                        act.wait_ge(s_specs, 16 * (r // 2))
                    for c in range(4):
                        take(spec[:, 2 * c:2 * c + 2, part, :], psA[:, used[0] % 2, :].rearrange("p (g c) -> p g c", g=2))
                    if part == 0:
                        take(nyq[:], psA[0:1, used[0] % 2, 0:HALF])
                    else:
                        act.wait_ge(s_ht, so_far(s_ht))
                        act.activation(spec[0:1, 0, 1, :], nyq[:], ACT.Identity).then_inc(s_specw, one(s_specw))

                def stage_free(i):
                    if i >= 2:
                        act.wait_ge(s_store[i % 2], 16 * (i // 2))

                def stage_tile(i):
                    stage_free(i)
                    for c in range(2):
                        take(stage[:, i % 2, 512 * c:512 * c + 512], psA[:, used[0] % 2, :])

                for i in range(HY):
                    act.wait_ge(s_acc, i + 1)
                    act.activation(tap[:, i % 2, :], acc[:, i % 2, :], ACT.Identity, scale=cw[:, 1, i:i + 1],
                                   bias=cb[:, i:i + 1]).then_inc(s_tap0, one(s_tap0))
                    if i:
                        stage_tile(i - 1)
                    for q in halves[i]:
                        if q % 2 == 0 and q:
                            spectrum(q // 2 - 1)
                stage_tile(HY - 1)
                spectrum(len(rounds) - 1)


def inverse_tree(dve, own, one, so_far, Z, Y, X, T, done):
    add, sub, mul = ALU.add, ALU.subtract, ALU.mult
    tt, stt = dve.tensor_tensor, dve.scalar_tensor_tensor
    G, Cc, Bh, Dd, dq, m, pp, x1, x3, w = (T[:, 2 * i:2 * i + 2, :] for i in range(10))
    tt(G, Z[:, 8:10, :], Z[:, 10:12, :], add).then_inc(own, one(own))
    tt(Cc, Z[:, 8:10, :], Z[:, 10:12, :], sub).then_inc(own, one(own))
    tt(Bh, Z[:, 12:14, :], Z[:, 14:16, :], add).then_inc(own, one(own))
    tt(Dd, Z[:, 13:15, :], Z[:, 15:11:-3, :], sub).then_inc(own, one(own))
    tt(dq, Z[:, 4:6, :], Z[:, 6:8, :], add).then_inc(own, one(own))
    tt(m, Z[:, 4:6, :], Z[:, 6:8, :], sub).then_inc(own, one(own))
    tt(pp[:, 0, :], Z[:, 0, :], Z[:, 1, :], add).then_inc(own, one(own))
    tt(pp[:, 1, :], Z[:, 0, :], Z[:, 1, :], sub).then_inc(own, one(own))
    dve.wait_ge(own, so_far(own))
    tt(x1, Cc, Dd, add).then_inc(own, one(own))
    tt(x3, Cc, Dd, sub).then_inc(own, one(own))
    tt(w, G, Bh, add).then_inc(own, one(own))
    tt(Y[:, 0:3:2, :], pp, Z[:, 2:4, :], add).then_inc(own, one(own))
    tt(Y[:, 4:7:2, :], pp, Z[:, 2:4, :], sub).then_inc(own, one(own))
    dve.wait_ge(own, so_far(own))
    tt(Cc, G, Bh, sub).then_inc(own, one(own))
    tt(Dd[:, 0, :], m[:, 0, :], m[:, 1, :], add).then_inc(own, one(own))
    tt(Dd[:, 1, :], m[:, 1, :], m[:, 0, :], sub).then_inc(own, one(own))
    stt(out=Y[:, 1, :], in0=x1[:, 1, :], scalar=T22, in1=x1[:, 0, :], op0=mul, op1=add).then_inc(own, one(own))
    stt(out=Y[:, 5, :], in0=x1[:, 0, :], scalar=-T22, in1=x1[:, 1, :], op0=mul, op1=add).then_inc(own, one(own))
    stt(out=Y[:, 3, :], in0=x3[:, 0, :], scalar=T22, in1=x3[:, 1, :], op0=mul, op1=add).then_inc(own, one(own))
    stt(out=Y[:, 7, :], in0=x3[:, 1, :], scalar=T22, in1=x3[:, 0, :], op0=mul, op1=sub).then_inc(own, one(own))
    dve.wait_ge(own, so_far(own))
    stt(out=dq[:, 1, :], in0=Cc[:, 0, :], scalar=C45, in1=dq[:, 1, :], op0=mul, op1=add).then_inc(own, one(own))
    stt(out=Y[:, 4, :], in0=Cc[:, 1, :], scalar=C45, in1=Y[:, 4, :], op0=mul, op1=add).then_inc(own, one(own))
    s13 = Y[:, 2:7:4, :]
    stt(out=G, in0=Dd, scalar=C45, in1=s13, op0=mul, op1=add).then_inc(own, one(own))
    stt(out=Bh, in0=Dd, scalar=-C45, in1=s13, op0=mul, op1=add).then_inc(own, one(own))
    dve.wait_ge(own, so_far(own))
    s02 = Y[:, 0:5:4, :]
    tt(m, s02, dq, add).then_inc(own, one(own))
    tt(pp, s02, dq, sub).then_inc(own, one(own))
    stt(out=Y[:, 1:4:2, :], in0=Y[:, 1:4:2, :], scalar=C22, in1=G, op0=mul, op1=add).then_inc(own, one(own))
    stt(out=Y[:, 5:8:2, :], in0=Y[:, 5:8:2, :], scalar=C22, in1=Bh, op0=mul, op1=add).then_inc(own, one(own))
    dve.wait_ge(own, so_far(own))
    tt(Y[:, 0:5:4, :], T[:, 10:13:2, :], w, add).then_inc(own, one(own))
    tt(Y[:, 2:7:4, :], T[:, 11:14:2, :], X[:, 2:7:4, :], mul).then_inc(own, one(own))
    tt(Y[:, 1:8:2, :], Y[:, 1:8:2, :], X[:, 1:8:2, :], mul).then_inc(own, one(own))
    dve.wait_ge(own, so_far(own))
    tt(Y[:, 0:5:4, :], Y[:, 0:5:4, :], X[:, 0:5:4, :], mul).then_inc(done, one(done))


def hyena_stage(nc, dram, scratch, own, hT, mix):
    own_dve, own_act, one, so_far = own
    R = 2 * ORDER
    WC = 256
    tiles = [("code", 0, C0, 2 * RANK)] + [("qk", j, Q0 + P * j, P) for j in range(2 * QK // P)]
    tiles += [("vg", (c, th), V0 + WC * c, WC) for c in range(2 * GW // WC) for th in range(2)]
    loads = [(C0, 2 * RANK)] + [(Q0 + WC * c, WC) for c in range((C0 - Q0) // WC)]
    load_of = [next(i for i, (c, n) in enumerate(loads) if c <= t[2] < c + n) for t in tiles]
    after_round = [2, 5, 8, 11, len(tiles)]
    with ExitStack() as ctx:
        sb = lambda name, shape, dt=F32: ctx.enter_context(nc.sbuf_tensor(name, shape, dt))
        sem = lambda name: ctx.enter_context(nc.semaphore(name))
        fwd = sb("m_fwd", [P, GROUPS, 4, P])
        inv = sb("m_inv", [P, GROUPS, 4, P])
        z = mix[:, :, GW:D]
        V = sb("m_V", [P, 2 * GROUPS, HALF])
        T = sb("m_T", [P, 20, HALF])
        K = sb("m_K", [P, GROUPS, 2, HALF])
        gate = sb("m_gate", [P, TT, HALF])
        M = sb("m_M", [P, 2, 2, HALF])
        Y = sb("m_Y", [P, 2, 2, HALF])
        w_sb = sb("m_w", [P, 2, DT, WC])
        stage = sb("m_stage", [P, 2, L])
        psU = ctx.enter_context(nc.psum_tensor("psU", [P, 2, 512], F32))
        psZ = ctx.enter_context(nc.psum_tensor("psZ", [P, 2, 512], F32))
        acc = ctx.enter_context(nc.psum_tensor("m_acc", [P, 2, L], F32))

        s_tab, s_inv = sem("m_forward_table"), sem("m_inverse_table")
        s_z = [sem(f"m_z_loaded{h}") for h in range(2)]
        s_K = sem("m_K_loaded")
        s_gate = sem("m_gate_loaded")
        s_w = [sem(f"m_w_loaded{i}") for i in range(2)]
        s_tree = sem("m_tree_done")
        s_u = sem("m_data_spectrum")
        s_mult = sem("m_spectrum_taken")
        s_y = sem("m_product_ready")
        s_zf = sem("m_inverse_product")
        s_zt = sem("m_inverse_taken")
        s_gated = sem("m_round_done")
        s_acc, s_stage = sem("m_tile_product"), sem("m_tile_staged")
        s_store = [sem(f"m_tile_stored{i}") for i in range(2)]

        with nc.Block() as block:
            @block.sync
            def _(sp):
                def half_load(h):
                    sp.dma_start(mix[:, :, GW + HALF * h:GW + HALF * h + HALF],
                                 scratch["hy"][0, :, HALF * h:HALF * h + HALF].rearrange("(a p) c -> p a c", p=P)).then_inc(s_z[h], 16)

                half_load(0)
                sp.dma_start(fwd[:], dram["c_fwd"].rearrange("p (g q c) -> p g q c", g=GROUPS, q=4)).then_inc(s_tab, 16)
                for r in range(R):
                    o, h = r // 2, r % 2
                    if r:
                        sp.wait_ge(s_y, 8 * r)
                    sp.dma_start(K[:], scratch["spec"][o, h]).then_inc(s_K, 16)
                    if r == 0:
                        sp.dma_start(inv[:], dram["c_inv"].rearrange("p (g q c) -> p g q c", g=GROUPS, q=4)).then_inc(s_inv, 16)
                    else:
                        sp.wait_ge(s_gated, r)
                    sp.dma_start(gate[:], scratch["hy"][1 + o, :, HALF * h:HALF * h + HALF].rearrange("(a p) c -> p a c", p=P)).then_inc(s_gate, 16)
                    if r == 0:
                        half_load(1)

            @block.gpsimd
            def _(pool):
                def load(i):
                    c, n = loads[i]
                    pool.dma_start(w_sb[:, i % 2, :, 0:n], dram["w_in"][0, :, c:c + n].rearrange("(k p) n -> p k n", p=P)).then_inc(s_w[i % 2], 16)

                load(0)
                load(1)
                for i, (kind, j, col, n) in enumerate(tiles):
                    pool.wait_ge(s_stage, i + 1)
                    src = stage[:, i % 2, :]
                    if kind == "code":
                        dst, src = scratch["code"][:], stage[0:2 * RANK, i % 2, :]
                    elif kind == "qk":
                        dst = scratch["qk"][j]
                    else:
                        c, th = j
                        dst = scratch["vg"][c // 2, 512 * th:512 * th + 512, WC * (c % 2):WC * (c % 2) + WC].rearrange("(a p) c -> p a c", p=P)
                        src = src.rearrange("p (a c) -> p a c", c=WC)
                    if i + 1 < len(tiles) and load_of[i + 1] != load_of[i] and load_of[i] + 2 < len(loads):
                        load(load_of[i] + 2)
                    pool.dma_start(dst, src).then_inc(s_store[i % 2], 16)
                pool.wait_ge(s_store[0], 16 * ((len(tiles) + 1) // 2))
                pool.wait_ge(s_store[1], 16 * (len(tiles) // 2))

            @block.tensor
            def _(pe):
                def product(i):
                    kind, j, col, n = tiles[i]
                    g = load_of[i]
                    w, off = w_sb[:, g % 2], col - loads[g][0]
                    pe.wait_ge(s_w[g % 2], 16 * (g // 2 + 1))
                    if i >= 2:
                        pe.wait_ge(s_stage, i - 1)
                    if kind == "vg":
                        for tt in range(4):
                            tok = 4 * j[1] + tt
                            for k in range(DT):
                                m = pe.matmul(acc[:, i % 2, WC * tt:WC * tt + WC], hT[:, k, P * tok:P * tok + P], w[:, k, :],
                                              start=(k == 0), stop=(k == DT - 1))
                    else:
                        for c in range(2):
                            for k in range(DT):
                                m = pe.matmul(acc[0:n, i % 2, 512 * c:512 * c + 512], w[:, k, off:off + n],
                                              hT[:, k, 512 * c:512 * c + 512], start=(k == 0), stop=(k == DT - 1))
                    m.then_inc(s_acc, 1)

                def hyena(r):
                    pe.wait_ge(s_tree, r + 1)
                    for i in range(GROUPS + 2):
                        if i < GROUPS:
                            n = GROUPS * r + i
                            if n >= 2:
                                pe.wait_ge(s_mult, n - 1)
                            for part in range(2):
                                for slot in range(2):
                                    mm = pe.matmul(psU[:, n % 2, HALF * part:HALF * part + HALF], fwd[:, i, 2 * part + slot, :],
                                                   V[:, 2 * i + slot, :], start=(slot == 0), stop=(slot == 1))
                            mm.then_inc(s_u, 1)
                        if i >= 2:
                            gi, n = i - 2, GROUPS * r + i - 2
                            pe.wait_ge(s_y, n + 1)
                            if n >= 2:
                                pe.wait_ge(s_zt, n - 1)
                            for slot in range(2):
                                for part in range(2):
                                    mm = pe.matmul(psZ[:, n % 2, HALF * slot:HALF * slot + HALF], inv[:, gi, 2 * part + slot, :],
                                                   Y[:, n % 2, part, :], start=(part == 0), stop=(part == 1))
                            mm.then_inc(s_zf, 1)

                for i in range(after_round[0]):
                    product(i)
                pe.wait_ge(s_tab, 16)
                pe.wait_ge(s_inv, 16)
                for r in range(R):
                    hyena(r)
                    for i in range(after_round[r], after_round[r + 1]):
                        product(i)

            @block.vector
            def _(dve):
                def products(r):
                    dve.wait_ge(s_K, 16 * (r + 1))
                    for i in range(GROUPS):
                        n = GROUPS * r + i
                        dve.wait_ge(s_u, n + 1)
                        U = psU[:, n % 2, :].rearrange("p (a c) -> p a c", a=2)
                        if so_far(s_tree):
                            dve.wait_ge(s_tree, so_far(s_tree))
                        if so_far(s_y):
                            dve.wait_ge(s_y, so_far(s_y))
                        dve.tensor_tensor(M[:, 0], U, K[:, i], ALU.mult).then_inc(own_dve, one(own_dve))
                        dve.tensor_tensor(M[:, 1], U, K[:, i, ::-1, :], ALU.mult).then_inc(s_mult, one(s_mult))
                        if n >= 2:
                            dve.wait_ge(s_zf, n - 1)
                        dve.wait_ge(s_mult, so_far(s_mult))
                        dve.tensor_tensor(Y[:, n % 2, 0, :], M[:, 0, 0, :], M[:, 0, 1, :], ALU.subtract).then_inc(own_dve, one(own_dve))
                        last = dve.tensor_tensor(Y[:, n % 2, 1, :], M[:, 1, 0, :], M[:, 1, 1, :], ALU.add)
                        if i == 0:
                            last.then_inc(own_dve, one(own_dve))
                            dve.wait_ge(own_dve, so_far(own_dve))
                            last = dve.tensor_copy(Y[0:1, n % 2], M[0:1, 0])
                        last.then_inc(s_y, one(s_y))

                def forward(r):
                    if r < 2:
                        dve.wait_ge(s_z[r], 16)
                    else:
                        dve.wait_ge(s_gated, r - 1)
                    if r:
                        dve.wait_ge(s_gated, so_far(s_gated))
                    forward_tree(dve, own_dve, one, so_far, z[:, :, HALF * (r % 2):HALF * (r % 2) + HALF], V[:], T[:], s_tree)

                def inverse(r):
                    dve.wait_ge(s_zt, GROUPS * (r + 1))
                    dve.wait_ge(s_gate, 16 * (r + 1))
                    dve.wait_ge(s_tree, so_far(s_tree))
                    inverse_tree(dve, own_dve, one, so_far, V[:], z[:, :, HALF * (r % 2):HALF * (r % 2) + HALF], gate[:], T[:], s_gated)

                forward(0)
                for r in range(R):
                    products(r)
                    inverse(r)
                    if r + 1 < R:
                        forward(r + 1)

            @block.scalar
            def _(act):
                def inverse(r):
                    for i in range(GROUPS):
                        n = GROUPS * r + i
                        act.wait_ge(s_zf, n + 1)
                        act.activation(V[:, 2 * i:2 * i + 2, :], psZ[:, n % 2, :].rearrange("p (a c) -> p a c", a=2), ACT.Identity).then_inc(s_zt, one(s_zt))

                def take_tile(i):
                    kind, _, col, n = tiles[i]
                    act.wait_ge(s_acc, i + 1)
                    if i >= 2:
                        act.wait_ge(s_store[i % 2], 16 * (i // 2))
                    scale = DK ** -0.5 if kind == "qk" and col < K0 else 1.0
                    rows = min(n, P)
                    act.activation(stage[0:rows, i % 2, :], acc[0:rows, i % 2, :], ACT.Identity, scale=scale).then_inc(s_stage, one(s_stage))

                for i in range(after_round[0]):
                    take_tile(i)
                for r in range(R):
                    inverse(r)
                    for i in range(after_round[r], after_round[r + 1]):
                        take_tile(i)


def attention_stage(nc, dram, scratch, own, mix, w_out, w_out_loaded):
    own_dve, own_act, one, so_far = own
    CH = 64
    NCH = L // CH
    R = 4
    with ExitStack() as ctx:
        sb = lambda name, shape, dt=F32: ctx.enter_context(nc.sbuf_tensor(name, shape, dt))
        ps = lambda name: ctx.enter_context(nc.psum_tensor(name, [P, 4, 512], F32))
        sem = lambda name: ctx.enter_context(nc.semaphore(name))
        ident = sb("m_ident", [P, P])
        q = sb("m_q", [P, 2, L])
        k = sb("m_k", [P, 2, L])
        v = sb("m_v", [P, 2, TT, 2 * DV])
        g = sb("m_g", [P, 2, TT, 2 * DV])
        code = sb("m_code", [2 * RANK, L])
        wa = sb("m_wa", [2 * RANK, 2, QK])
        ba = sb("m_ba", [P, 2, 2])
        pre = [[sb(f"m_{name}{i}", [P, L])[:] for name in ("gx", "ab", "b", "df")] for i in range(2)]
        osb = sb("m_o", [P, 2 * TT, DV])
        starts = sb("m_starts", [P, L], mybir.dt.uint8)
        qd = sb("m_qd", [P, 2, L])
        ki = sb("m_ki", [P, 2, L])
        dec = sb("m_dec", [P, 2, NCH])
        kT = sb("m_kT", [P, TT, P])
        S = sb("m_S", [P, 2, NCH, DV])
        mask = sb("m_mask", [P, 2, P], I32)
        sc = sb("m_sc", [P, 2, 2, 2, P])
        nw = sb("m_nw", [P, DV])
        rs = sb("m_rs", [P, 4, 2 * TT])
        psG, psS = ps("psG"), ps("psS")

        s_id = sem("m_identity")
        s_gl = sem("m_gla_constants")
        s_qk = sem("m_qk_loaded")
        s_vg = sem("m_vg_loaded")
        s_gf = sem("m_psG_filled")
        s_gt = sem("m_psG_taken")
        s_gx = sem("m_logs_ready")
        s_b = sem("m_cumsum_ready")
        s_df = sem("m_chunk_rest_ready")
        s_ex = sem("m_exps_ready")
        s_qd = sem("m_decayed_ready")
        s_S = sem("m_states_ready")
        s_sf = sem("m_scores_filled")
        s_sm = sem("m_scores_masked")
        s_zero = sem("m_scores_zeroed")
        s_ss = sem("m_head_variance")
        s_rt = sem("m_head_root")
        s_sg = sem("m_silu_ready")
        s_gn = sem("m_silu_times_norm")
        s_on = sem("m_heads_done")
        chunk_fills = [2, 6, 10 + TT, 13 + TT]
        head_fills = [10, 16 + TT]

        with nc.Block() as block:
            @block.sync
            def _(sp):
                sp.dma_start(code[:], scratch["code"]).then_inc(s_gl, 16)
                sp.wait_ge(s_zero, 1)
                sp.dma_start(wa[0:RANK, 0, :], dram["gla_wa_f"][0]).then_inc(s_gl, 16)
                sp.dma_start(wa[RANK:2 * RANK, 1, :], dram["gla_wa_b"][0]).then_inc(s_gl, 16)
                sp.dma_start(ba[:], dram["l_gate_b"]).then_inc(s_gl, 16)
                sp.dma_start(mask[:], dram["c_mask"]).then_inc(s_gl, 16)
                sp.dma_start(nw[:], dram["gla_norm_w"][0].partition_broadcast(P)).then_inc(s_gl, 16)
                sp.dma_start(ident[:], dram["c_ident"]).then_inc(s_id, 16)
                for t, i in ((q, 0), (k, 2)):
                    sp.dma_start(t[:], scratch["qk"][i:i + 2].rearrange("h p l -> p h l")).then_inc(s_qk, 16)
                for i, t in enumerate((v, g)):
                    for ht in range(2):
                        sp.dma_start(t[:, ht], scratch["vg"][i, :, 2 * DV * ht:2 * DV * ht + 2 * DV].rearrange("(a p) c -> p a c", p=P)).then_inc(s_vg, 16)
                for c in range(2):
                    sp.dma_start(w_out[:, :, 512 * c:512 * c + 512],
                                 dram["w_out"][0, :, 512 * c:512 * c + 512].rearrange("(k p) n -> p k n", p=P)).then_inc(w_out_loaded[c], 16)

            @block.gpsimd
            def _(pool):
                pool.memset(wa[:], 0.0).then_inc(s_zero, 1)
                pool.memset(sc[:], 0.0).then_inc(s_zero, 1)
                pool.memset(starts[:], 1).then_inc(s_zero, 1)
                pool.wait_ge(s_zero, 3)
                pool.memset(starts[:].rearrange("p (n c) -> p n c", c=CH)[:, :, 0:1], 0).then_inc(s_zero, 1)
                pool.wait_ge(s_gl, 16 * 6)
                for ht in range(2):
                    pool.wait_ge(s_sg, ht + 1)
                    gv = g[:, ht].rearrange("p a (x d) -> p (a x) d", d=DV)
                    pool.tensor_tensor(gv, gv, nw[:].unsqueeze(1).to_broadcast([P, 2 * TT, DV]), ALU.mult).then_inc(s_gn, 1)

            @block.tensor
            def _(pe):
                fills = [0]

                def next_fill():
                    if fills[0] >= 2:
                        pe.wait_ge(s_gt, fills[0] - 1)
                    fills[0] += 1
                    half = (fills[0] - 1) % 2
                    return psG[:, 2 * half:2 * half + 2, :]

                def gate_logits(r):
                    ht, dr = r // 2, r % 2
                    bank = next_fill()
                    for c in range(2):
                        m = pe.matmul(bank[:, c, :], wa[:, dr, P * ht:P * ht + P], code[:, 512 * c:512 * c + 512], start=True, stop=True)
                    m.then_inc(s_gf, 1)

                def chunk_products(r):
                    ht, dr = r // 2, r % 2
                    df = pre[dr][3]
                    pe.wait_ge(s_qd, r + 1)
                    bank = next_fill()
                    for t in range(TT):
                        m = pe.transpose(bank[:, t // 4, P * (t % 4):P * (t % 4) + P], df[:, P * t:P * t + P], ident[:])
                    m.then_inc(s_gf, 1)
                    if dr == 0:
                        pe.wait_ge(s_vg, 64)
                    for batch in range(2):
                        bank = next_fill()
                        if batch == 0:
                            pe.wait_ge(s_gt, chunk_fills[r] + 1)
                        for i in range(8):
                            n = 8 * batch + i
                            rows = slice(CH * (n % 2), CH * (n % 2) + CH)
                            for hd in range(2):
                                m = pe.matmul(bank[CH * hd:CH * hd + CH, n % 2, DV * (i // 2):DV * (i // 2) + DV],
                                              kT[rows, n // 2, CH * hd:CH * hd + CH], v[rows, ht, n // 2, DV * hd:DV * hd + DV],
                                              start=True, stop=True)
                        m.then_inc(s_gf, 1)

                def scores(ht, t):
                    n = TT * ht + t
                    if n >= 2:
                        pe.wait_ge(s_sm, n - 1)
                    for hd in range(2):
                        rows = slice(DK * hd, DK * hd + DK)
                        for dr in range(2):
                            m = pe.matmul(psS[:, 2 * (t % 2) + hd, P * dr:P * dr + P], ki[rows, dr, P * t:P * t + P], qd[rows, dr, P * t:P * t + P],
                                          start=True, stop=True)
                    m.then_inc(s_sf, 1)

                def heads_out(ht):
                    pe.wait_ge(s_S, 2 * ht + 2)
                    scores(ht, 0)
                    for t in range(TT):
                        if t + 1 < TT:
                            scores(ht, t + 1)
                        pe.wait_ge(s_sm, TT * ht + t + 1)
                        bank = next_fill()
                        for hd in range(2):
                            rows = slice(DK * hd, DK * hd + DK)
                            for dr in range(2):
                                m = pe.matmul(bank[:, hd, 0:DV], sc[:, t % 2, hd, dr, :], v[:, ht, t, DV * hd:DV * hd + DV],
                                              start=(dr == 0), stop=False, skip_group_check=True)
                            for c in range(2):
                                n = 2 * t + c
                                for dr, before in ((0, n - 1), (1, n + 1)):
                                    if 0 <= before < NCH:
                                        m = pe.matmul(bank[CH * c:CH * c + CH, hd, 0:DV], qd[rows, dr, CH * n:CH * n + CH],
                                                      S[rows, dr, before, :], start=False, stop=False, skip_group_check=True)
                        m.then_inc(s_gf, 1)

                pe.wait_ge(s_gl, 16 * 6)
                gate_logits(0)
                gate_logits(1)
                pe.wait_ge(s_id, 16)
                chunk_products(0)
                gate_logits(2)
                chunk_products(1)
                gate_logits(3)
                heads_out(0)
                chunk_products(2)
                chunk_products(3)
                heads_out(1)

            @block.vector
            def _(dve):

                def cumulate(r):
                    dr = r % 2
                    gx, ab, b, df = pre[dr]
                    dve.wait_ge(s_gx, r + 1)
                    dve.scalar_tensor_tensor(out=gx, in0=gx, scalar=0.0, in1=ab, op0=ALU.min, op1=ALU.subtract).then_inc(own_dve, one(own_dve))
                    dve.wait_ge(own_dve, so_far(own_dve))
                    f = (lambda t: t) if dr == 0 else (lambda t: t[:, ::-1])
                    dve.tensor_tensor_scan(f(b), starts[:], f(gx), 0.0, ALU.mult, ALU.add).then_inc(s_b, one(s_b))
                    dve.wait_ge(s_b, so_far(s_b))
                    bc = b.rearrange("p (n c) -> p n c", c=CH)
                    end = bc[:, :, CH - 1:CH] if dr == 0 else bc[:, :, 0:1]
                    dve.tensor_tensor(df.rearrange("p (n c) -> p n c", c=CH), end.to_broadcast([P, NCH, CH]), bc, ALU.subtract).then_inc(s_df, one(s_df))

                def decayed(r):
                    dr = r % 2
                    gx, ab, b, df = pre[dr]
                    dve.wait_ge(s_ex, r + 1)
                    dve.wait_ge(s_qk, 32)
                    dve.tensor_tensor(qd[:, dr, :], q[:, r // 2], gx, ALU.mult).then_inc(own_dve, one(own_dve))
                    dve.tensor_tensor(ki[:, dr, :], k[:, r // 2], ab, ALU.mult).then_inc(own_dve, one(own_dve))
                    dve.tensor_tensor(df, k[:, r // 2], df, ALU.mult).then_inc(s_qd, one(s_qd))

                def states(r):
                    ht, dr = r // 2, r % 2
                    dve.wait_ge(s_gt, chunk_fills[r] + 3)
                    order = range(1, NCH - 1) if dr == 0 else range(NCH - 2, 0, -1)
                    for i, n in enumerate(order):
                        if so_far(s_qd):
                            dve.wait_ge(s_qd, so_far(s_qd))
                        if so_far(own_dve):
                            dve.wait_ge(own_dve, so_far(own_dve))
                        prev = n - 1 if dr == 0 else n + 1
                        ins = dve.scalar_tensor_tensor(out=S[:, dr, n, :], in0=S[:, dr, prev, :], scalar=dec[:, dr, n:n + 1],
                                                       in1=S[:, dr, n, :], op0=ALU.mult, op1=ALU.add)
                        if i == NCH - 3:
                            ins.then_inc(s_S, one(s_S))
                        else:
                            ins.then_inc(own_dve, one(own_dve))

                def causal(ht, ts):
                    for t in ts:
                        dve.wait_ge(s_sf, TT * ht + t + 1)
                        if t >= 2:
                            dve.wait_ge(s_gf, head_fills[ht] + t - 1)
                        elif t == 0:
                            dve.wait_ge(s_gl, 16 * 6)
                        m = mask[:].rearrange("p a c -> p (a c)").unsqueeze(1).to_broadcast([P, 2, 2 * P])
                        dve.copy_predicated(sc[:, t % 2].rearrange("p h d c -> p h (d c)"), m, psS[:, 2 * (t % 2):2 * (t % 2) + 2, 0:2 * P]).then_inc(s_sm, one(s_sm))

                def heads_norm(ht):
                    nt = v[:, ht].rearrange("p a (x d) -> p (a x) d", d=DV)
                    dve.wait_ge(s_gt, head_fills[ht] + TT)
                    dve.wait_ge(s_sm, so_far(s_sm))
                    dve.tensor_tensor(nt, osb[:], osb[:], ALU.mult).then_inc(own_dve, one(own_dve))
                    dve.wait_ge(own_dve, so_far(own_dve))
                    dve.tensor_reduce(rs[:, 3, :], nt, AX_X, ALU.add).then_inc(own_dve, one(own_dve))
                    dve.wait_ge(own_dve, so_far(own_dve))
                    dve.tensor_scalar(rs[:, 0, :], rs[:, 3, :], 1.0 / DV, EPS, ALU.mult, ALU.add).then_inc(s_ss, one(s_ss))
                    dve.wait_ge(s_rt, ht + 1)
                    dve.reciprocal(rs[:, 2, :], rs[:, 1, :]).then_inc(own_dve, one(own_dve))
                    newton(dve, own_dve, one, so_far, rs)
                    dve.tensor_tensor(osb[:], osb[:], rs[:, 2, :].unsqueeze(2).to_broadcast([P, 2 * TT, DV]), ALU.mult).then_inc(own_dve, one(own_dve))
                    dve.wait_ge(s_gn, ht + 1)
                    dve.wait_ge(own_dve, so_far(own_dve))
                    dve.tensor_tensor(mix[:, :, 2 * DV * ht:2 * DV * ht + 2 * DV], osb[:].rearrange("p (a x) d -> p a (x d)", x=2), g[:, ht], ALU.mult).then_inc(s_on, one(s_on))

                dve.wait_ge(s_zero, 4)
                cumulate(0)
                cumulate(1)
                decayed(0)
                decayed(1)
                states(0)
                cumulate(2)
                states(1)
                cumulate(3)
                causal(0, range(TT))
                dve.wait_ge(s_gt, head_fills[0] + TT)
                decayed(2)
                decayed(3)
                heads_norm(0)
                states(2)
                states(3)
                causal(1, range(TT))
                dve.wait_ge(s_gt, head_fills[1] + TT)
                heads_norm(1)

            @block.scalar
            def _(act):
                taken = [0]
                act.wait_ge(s_gl, 16 * 6)

                def wait_fill():
                    taken[0] += 1
                    act.wait_ge(s_gf, taken[0])
                    half = (taken[0] - 1) % 2
                    return psG[:, 2 * half:2 * half + 2, :]

                def logs(r):
                    ht, dr = r // 2, r % 2
                    gx, ab, b, df = pre[dr]
                    bank = wait_fill()
                    if so_far(s_gt):
                        act.wait_ge(s_gt, so_far(s_gt))
                    if so_far(s_rt):
                        act.wait_ge(s_rt, so_far(s_rt))
                    act.activation(gx, bank, ACT.Identity, bias=ba[:, dr, ht:ht + 1]).then_inc(s_gt, one(s_gt))
                    act.wait_ge(s_gt, so_far(s_gt))
                    act.activation(ab, gx, ACT.Abs).then_inc(own_act, one(own_act))
                    act.wait_ge(own_act, so_far(own_act))
                    act.activation(ab, ab, ACT.Exp, scale=-1.0).then_inc(own_act, one(own_act))
                    act.wait_ge(own_act, so_far(own_act))
                    act.activation(ab, ab, ACT.Ln, bias=1.0).then_inc(s_gx, one(s_gx))

                def exps(r):
                    dr = r % 2
                    gx, ab, b, df = pre[dr]
                    act.wait_ge(s_b, r + 1)
                    end = b.rearrange("p (n c) -> p n c", c=CH)[:, :, (CH - 1) * (1 - dr)]
                    act.activation(dec[:, dr, :], end, ACT.Exp, scale=1.0 / TAU).then_inc(own_act, one(own_act))
                    act.activation(gx, b, ACT.Exp, scale=1.0 / TAU).then_inc(own_act, one(own_act))
                    act.activation(ab, b, ACT.Exp, scale=-1.0 / TAU).then_inc(own_act, one(own_act))
                    act.wait_ge(s_df, r + 1)
                    act.activation(df, df, ACT.Exp, scale=1.0 / TAU).then_inc(s_ex, one(s_ex))

                def take_products(r):
                    dr = r % 2
                    bank = wait_fill()
                    act.activation(kT[:], bank.rearrange("p a (t c) -> p (a t) c", c=P), ACT.Identity).then_inc(s_gt, one(s_gt))
                    for batch in range(2):
                        bank = wait_fill()
                        for par in range(2):
                            ins = act.activation(S[:, dr, 8 * batch + par:8 * batch + 8:2, :], bank[:, par, :].rearrange("p (i d) -> p i d", d=DV), ACT.Identity)
                            if par:
                                ins.then_inc(s_gt, one(s_gt))
                            else:
                                ins.then_inc(own_act, one(own_act))

                def take_heads(ht):
                    for t in range(TT):
                        bank = wait_fill()
                        act.activation(osb[:, 2 * t:2 * t + 2, :], bank[:, :, 0:DV], ACT.Identity).then_inc(s_gt, one(s_gt))
                    act.wait_ge(s_gt, so_far(s_gt))
                    act.activation(g[:, ht], g[:, ht], ACT.Silu).then_inc(s_sg, one(s_sg))
                    act.wait_ge(s_ss, ht + 1)
                    act.activation(rs[:, 1, :], rs[:, 0, :], ACT.Sqrt).then_inc(s_rt, one(s_rt))

                logs(0)
                logs(1)
                exps(0)
                exps(1)
                take_products(0)
                logs(2)
                take_products(1)
                exps(2)
                logs(3)
                exps(3)
                take_heads(0)
                take_products(2)
                take_products(3)
                take_heads(1)


RING = 8
NGU, NDN = 16, 8


def load_piece(sp, dram, ring, piece_loaded, e, i):
    slot = ring[:, i % RING, :]
    if i < NGU:
        n, m, half = i // 4, (i // 2) % 2, i % 2
        w = dram[("w_gate_e", "w_up_e")[m]][0]
        src = w[bass.ds(e, 1), 512 * half:512 * half + 512, 512 * n:512 * n + 512].rearrange("o (k p) c -> (o p) k c", p=P)
        dst = slot.rearrange("p (k c) -> p k c", k=4)
    else:
        j = i - NGU
        src = dram["w_down_e"][0, bass.ds(e, 1), 2 * P * j:2 * P * j + 2 * P, :].rearrange("o (k p) c -> (o p) k c", p=P)
        dst = slot.rearrange("p (k c) -> p k c", k=2)
    sp.dma_start(dst, src).then_inc(piece_loaded[i % RING], 16)


def residual_stage(nc, dram, scratch, own, tile_loaded, loads_before, ring, piece_loaded, mix, w, s_w):
    own_dve, own_act, one, so_far = own
    with ExitStack() as ctx:
        sb = lambda name, shape, dt=F32: ctx.enter_context(nc.sbuf_tensor(name, shape, dt))
        ps = lambda name, n: ctx.enter_context(nc.psum_tensor(name, [P, n, 512], F32))
        sem = lambda name: ctx.enter_context(nc.semaphore(name))
        x = sb("o_x", [P, TT, D])
        mixT = sb("o_mixT", [P, 2, DT, P])
        h = sb("o_h", [P, 2, D])
        hT = sb("o_hT", [P, 2, DT, P])
        sq = sb("o_sq", [P, D])
        wr = sb("o_wr", [P, DT, NE])
        lnw = sb("o_lnw", [P, DT])
        ident = sb("o_ident", [P, P])
        ssq = sb("o_ssq", [P, TT])
        rs = sb("o_rs", [P, 4, TT])
        lg = sb("o_lg", [P, TT, NE])
        ex = sb("o_ex", [P, TT, NE])
        st = sb("o_st", [P, 4, TT])
        pr = sb("o_pr", [P, TT, NE])
        prc = sb("o_prc", [P, NE, TT])
        pT = sb("o_pT", [NE, L])
        psT, psO, psH, psR = ps("o_psT", 2), ps("o_psO", 3), ps("o_psH", 2), ps("o_psR", 1)

        s_c, s_wr = sem("o_constants"), sem("o_router_loaded")
        x_loaded = loads_before + 16
        s_tf, s_tt = sem("o_mixT_filled"), sem("o_mixT_taken")
        s_of, s_ot = sem("o_product"), sem("o_residual_added")
        s_sq, s_var, s_rt = sem("o_squares"), sem("o_variance"), sem("o_root")
        s_h = sem("o_normed")
        s_hf, s_hT = sem("o_hT_filled"), sem("o_hT_taken")
        s_lg = sem("o_logits")
        s_sub, s_ex = sem("o_logits_less_max"), sem("o_exps")
        s_pr, s_pf, s_pT = sem("o_probs"), sem("o_probs_transposed"), sem("o_probs_by_row")
        s_sth = [sem(f"o_h_stored{i}") for i in range(2)]
        s_str = sem("o_stored")

        with nc.Block() as block:
            @block.sync
            def _(sp):
                sp.dma_start(ident[:], dram["c_ident"]).then_inc(s_c, 16)
                sp.dma_start(lnw[:], dram["l_ln_ffn"]).then_inc(s_c, 16)
                for t in range(TT):
                    sp.dma_start(x[:, t, :], dram["x"][0, P * t:P * t + P, :]).then_inc(tile_loaded[t], 16)
                    if t == 0:
                        sp.dma_start(wr[:], dram["w_router"][0].rearrange("(k p) n -> p k n", p=P)).then_inc(s_wr, 16)
                for i in range(RING):
                    load_piece(sp, dram, ring, piece_loaded, 0, i)

            @block.gpsimd
            def _(pool):
                for t in range(TT):
                    pool.wait_ge(s_ot, 2 * t + 2)
                    pool.dma_start(scratch["r"][P * t:P * t + P, :], x[:, t, :]).then_inc(s_str, 16)
                    pool.wait_ge(s_h, t + 1)
                    pool.dma_start(scratch["h2"][P * t:P * t + P, :], h[:, t % 2, :]).then_inc(s_sth[t % 2], 16)
                pool.wait_ge(s_pr, 2)
                pool.dma_start(scratch["pcol"].rearrange("e p t -> p e t"), prc[:]).then_inc(s_str, 16)
                pool.wait_ge(s_pT, 1)
                pool.dma_start(scratch["prow"], pT[:]).then_inc(s_str, 16)
                pool.wait_ge(s_str, 16 * (TT + 2))
                for i in range(2):
                    pool.wait_ge(s_sth[i], 16 * TT // 2)

            @block.tensor
            def _(pe):
                pe.wait_ge(s_c, 32)
                fills = [0]

                def mix_transposes(t):
                    for c in range(2):
                        if fills[0] >= 2:
                            pe.wait_ge(s_tt, fills[0] - 1)
                        for i in range(4):
                            k = 4 * c + i
                            m = pe.transpose(psT[:, c, P * i:P * i + P], mix[:, t, P * k:P * k + P], ident[:])
                        m.then_inc(s_tf, 1)
                        fills[0] += 1

                def product(t):
                    pe.wait_ge(s_tt, 2 * t + 2)
                    for c in range(2):
                        pe.wait_ge(s_w[c], 16)
                        n = 2 * t + c
                        if n >= 3:
                            pe.wait_ge(s_ot, n - 2)
                        for k in range(DT):
                            m = pe.matmul(psO[:, n % 3, :], mixT[:, t % 2, k, :], w[:, k, 512 * c:512 * c + 512],
                                          start=(k == 0), stop=(k == DT - 1))
                        m.then_inc(s_of, 1)

                def h_transposes(t):
                    pe.wait_ge(s_h, t + 1)
                    for c in range(2):
                        if t:
                            pe.wait_ge(s_hT, 2 * (t - 1) + c + 1)
                        for i in range(4):
                            k = 4 * c + i
                            m = pe.transpose(psH[:, c, P * i:P * i + P], h[:, t % 2, P * k:P * k + P], ident[:])
                        m.then_inc(s_hf, 1)

                def router(t):
                    pe.wait_ge(s_hT, 2 * t + 2)
                    if t == 0:
                        pe.wait_ge(s_wr, 16)
                    for k in range(DT):
                        m = pe.matmul(psR[:, 0, NE * t:NE * t + NE], hT[:, t % 2, k, :], wr[:, k, :], start=(k == 0), stop=(k == DT - 1))
                    m.then_inc(s_lg, 1)

                for i in range(TT + 3):
                    if i < TT:
                        mix_transposes(i)
                    if 1 <= i <= TT:
                        product(i - 1)
                    if 2 <= i <= TT + 1:
                        h_transposes(i - 2)
                    if i >= 3:
                        router(i - 3)
                pe.wait_ge(s_pr, 1)
                for t in range(TT):
                    m = pe.transpose(psT[0:NE, t // 4, P * (t % 4):P * (t % 4) + P], pr[:, t, :], ident[:])
                m.then_inc(s_pf, 1)

            @block.scalar
            def _(act):
                for i in range(TT + 1):
                    if i < TT:
                        if i >= 2:
                            act.wait_ge(s_of, 2 * (i - 2) + 2)
                        for c in range(2):
                            act.wait_ge(s_tf, 2 * i + c + 1)
                            act.activation(mixT[:, i % 2, 4 * c:4 * c + 4, :], psT[:, c, :].rearrange("p (k c) -> p k c", k=4), ACT.Identity).then_inc(s_tt, one(s_tt))
                    if i >= 1:
                        t = i - 1
                        act.wait_ge(s_ot, 2 * t + 2)
                        if so_far(s_tt):
                            act.wait_ge(s_tt, so_far(s_tt))
                        if so_far(s_rt):
                            act.wait_ge(s_rt, so_far(s_rt))
                        act.activation(sq[:], x[:, t, :], ACT.Square, accum_out=ssq[:, t:t + 1]).then_inc(s_sq, one(s_sq))
                        act.wait_ge(s_var, t + 1)
                        act.activation(rs[:, 1, t:t + 1], rs[:, 0, t:t + 1], ACT.Sqrt).then_inc(s_rt, one(s_rt))
                act.wait_ge(s_sub, 1)
                act.activation(ex[:], lg[:], ACT.Exp).then_inc(s_ex, one(s_ex))
                act.wait_ge(s_pf, 1)
                act.activation(pT[:], psT[0:NE].rearrange("p a c -> p (a c)"), ACT.Identity).then_inc(s_pT, one(s_pT))

            @block.vector
            def _(dve):
                dve.wait_ge(s_c, 32)
                for i in range(TT + 1):
                    if i < TT:
                        t = i
                        dve.wait_ge(tile_loaded[t], x_loaded)
                        for c in range(2):
                            n = 2 * t + c
                            dve.wait_ge(s_of, n + 1)
                            xs = x[:, t, 512 * c:512 * c + 512]
                            dve.tensor_tensor(xs, xs, psO[:, n % 3, :], ALU.add).then_inc(s_ot, one(s_ot))
                        dve.wait_ge(s_sq, t + 1)
                        dve.wait_ge(s_ot, so_far(s_ot))
                        dve.tensor_scalar(rs[:, 0, t:t + 1], ssq[:, t:t + 1], 1.0 / D, EPS, ALU.mult, ALU.add).then_inc(s_var, one(s_var))
                        dve.wait_ge(s_rt, t + 1)
                        dve.reciprocal(rs[:, 2, t:t + 1], rs[:, 1, t:t + 1]).then_inc(own_dve, one(own_dve))
                        newton(dve, own_dve, one, so_far, rs[:, :, t:t + 1])
                        if t >= 2:
                            dve.wait_ge(s_sth[t % 2], 16 * (t // 2))
                            dve.wait_ge(s_hf, 2 * (t - 2) + 2)
                        dve.tensor_scalar(h[:, t % 2, :], x[:, t, :], rs[:, 2, t:t + 1], None, ALU.mult).then_inc(s_h, one(s_h))
                    if i >= 1:
                        t = i - 1
                        if t >= 2:
                            dve.wait_ge(s_lg, t - 1)
                        for c in range(2):
                            dve.wait_ge(s_hf, 2 * t + c + 1)
                            lw = lnw[:, 4 * c:4 * c + 4].unsqueeze(2).to_broadcast([P, 4, P])
                            dve.tensor_tensor(hT[:, t % 2, 4 * c:4 * c + 4, :], psH[:, c, :].rearrange("p (k c) -> p k c", k=4), lw, ALU.mult).then_inc(s_hT, one(s_hT))
                dve.wait_ge(s_lg, TT)
                dve.tensor_copy(lg[:], psR[:, 0, 0:TT * NE].rearrange("p (t e) -> p t e", e=NE)).then_inc(own_dve, one(own_dve))
                dve.wait_ge(own_dve, so_far(own_dve))
                dve.tensor_reduce(st[:, 0, :], lg[:], AX_X, ALU.max).then_inc(own_dve, one(own_dve))
                dve.wait_ge(own_dve, so_far(own_dve))
                dve.tensor_tensor(lg[:], lg[:], st[:, 0, :].unsqueeze(2).to_broadcast([P, TT, NE]), ALU.subtract).then_inc(s_sub, one(s_sub))
                dve.wait_ge(s_ex, 1)
                dve.tensor_reduce(st[:, 1, :], ex[:], AX_X, ALU.add).then_inc(own_dve, one(own_dve))
                dve.wait_ge(own_dve, so_far(own_dve))
                dve.reciprocal(st[:, 2, :], st[:, 1, :]).then_inc(own_dve, one(own_dve))
                dve.wait_ge(own_dve, so_far(own_dve))
                dve.tensor_tensor(pr[:], ex[:], st[:, 2, :].unsqueeze(2).to_broadcast([P, TT, NE]), ALU.mult).then_inc(s_pr, one(s_pr))
                dve.wait_ge(s_pr, so_far(s_pr))
                dve.tensor_copy(prc[:].rearrange("p e t -> p t e"), pr[:]).then_inc(s_pr, one(s_pr))


def expert_stage(nc, dram, scratch, ring, piece_loaded, p, wp, p_loaded):
    SPLIT = 4
    PER = NGU + NDN
    with ExitStack() as ctx:
        sb = lambda name, shape, dt=F32: ctx.enter_context(nc.sbuf_tensor(name, shape, dt))
        ps = lambda name, n: ctx.enter_context(nc.psum_tensor(name, [P, n, 512], F32))
        sem = lambda name: ctx.enter_context(nc.semaphore(name))
        wh = sb("e_wh", [P, SPLIT, 4, 512], F32R)
        wl = sb("e_wl", [P, SPLIT, 4, 512], F32R)
        xg = sb("e_xg", [P, D])
        xT = sb("e_xT", [P, DT, P])
        xh = sb("e_xh", [P, 2, DT, P], F32R)
        xl = sb("e_xl", [P, 2, DT, P], F32R)
        sg = sb("e_sg", [P, 512])
        hid = sb("e_hid", [P, 2, 512])
        hidT = sb("e_hidT", [P, FF // P, P])
        y = sb("e_y", [P, D])
        ident = sb("e_ident", [P, P])
        lnw = sb("e_lnw", [P, DT])
        prow = sb("e_prow", [P, L])
        pcol = sb("e_pcol", [P, TT])
        cmp = sb("e_cmp", [P, L])
        lower = sb("e_lower", [P, P])
        iota = sb("e_iota", [P, P])
        cnt = sb("e_cnt", [P, TT, 3])
        rank = sb("e_rank", [P, TT])
        hot = sb("e_hot", [P, TT, P])
        vals = sb("e_vals", [P, TT, 2])
        idx = sb("e_idx", [P, 2, 1], I32)
        gate = sb("e_gate", [P, 2])
        psG, psU, psT, psY = ps("e_psG", 2), ps("e_psU", 2), ps("e_psT", 2), ps("e_psY", 2)

        s_c = sem("e_constants")
        s_ld = piece_loaded
        own_dve = sem("e_own_dve")
        s_p = sem("e_probs_loaded")
        s_rank = sem("e_ranked")
        s_hot = sem("e_slots_ready")
        s_rf, s_rt = sem("e_route_filled"), sem("e_route_taken")
        s_g = sem("e_gathered")
        s_xf, s_xt = sem("e_x_transposed"), sem("e_x_taken")
        s_xh, s_xl = sem("e_xh_ready"), sem("e_xl_ready")
        s_hi, s_lo = sem("e_hi_ready"), sem("e_lo_ready")
        s_gu = sem("e_piece_multiplied")
        s_sg, s_hid = sem("e_silu_ready"), sem("e_hidden_ready")
        s_hf, s_ht = sem("e_hid_transposed"), sem("e_hidT_ready")
        s_dn = sem("e_down_multiplied")
        s_y = sem("e_y_ready")
        s_sc = sem("e_scattered")

        with nc.Block() as block:
            @block.sync
            def _(sp):
                sp.dma_start(lnw[:], dram["l_ln_ffn"]).then_inc(s_c, 16)
                sp.dma_start(ident[:], dram["c_ident"]).then_inc(s_c, 16)
                sp.dma_start(lower[:], dram["c_lower"]).then_inc(s_c, 16)
                sp.dma_start(iota[:], dram["c_iota"]).then_inc(s_c, 16)
                sp.dma_start(vals[:, :, 0:1], dram["c_tok"].unsqueeze(2), allow_slow_non_contiguous=True).then_inc(s_c, 16)

                def probs(e):
                    sp.dma_start(prow[:], scratch["prow"][bass.ds(e, 1), :].to_broadcast([P, L])).then_inc(s_p, 16)
                    sp.dma_start(pcol[:], scratch["pcol"][bass.ds(e, 1)].rearrange("o p t -> (o p) t")).then_inc(s_p, 16)

                def body(e, par, last, first=False):
                    for i in range(PER):
                        if first and i < RING:
                            continue
                        if i < RING:
                            sp.wait_ge(s_dn, NDN * e + i + 1 - NDN)
                        else:
                            sp.wait_ge(s_lo, NGU * e + i - RING + 1)
                        load_piece(sp, dram, ring, piece_loaded, e, i)
                        if i == RING and not last:
                            sp.wait_ge(s_rank, e + 1)
                            probs(e + 1)

                probs(0)
                body(0, 0, False, first=True)
                body(1, 1, False)
                with sp.Fori(2, NE - 2, 2) as e:
                    body(e, 0, False)
                    body(e + 1, 1, False)
                body(NE - 2, 0, False)
                body(NE - 1, 1, True)
                sp.dma_start(p[:], dram["p"][0, 0].rearrange("(t p) c -> p t c", p=P)).then_inc(p_loaded, 16)
                sp.dma_start(wp[:], dram["w_ple_proj"][0].rearrange("(k p) c -> p k c", p=P)).then_inc(p_loaded, 16)

            @block.gpsimd
            def _(pool):
                def gather(e, par):
                    pool.wait_ge(s_rt, e + 1)
                    pool.indirect_dma_start(xg[:], None, scratch["h2"], bass.IndirectOffsetOnAxis(ap=idx[:, par, :], axis=0)).then_inc(s_g, 16)

                def body(e, par, last):
                    if not last:
                        pool.wait_ge(s_xf, e + 1)
                        gather(e + 1, 1 - par)
                    pool.wait_ge(s_y, e + 1)
                    pool.indirect_dma_start(scratch["r"], bass.IndirectOffsetOnAxis(ap=idx[:, par, :], axis=0), y[:], None,
                                            compute_op=ALU.add).then_inc(s_sc, 16)
                    pool.wait_ge(s_sc, 16 * e + 16)

                gather(0, 0)
                for e in range(NE):
                    body(e, e % 2, e == NE - 1)

            @block.tensor
            def _(pe):
                def route(e):
                    pe.wait_ge(s_hot, e + 1)
                    for t in range(TT):
                        m = pe.matmul(psT[:, 0, 0:2], hot[:, t, :], vals[:, t, :], start=(t == 0), stop=(t == TT - 1))
                    m.then_inc(s_rf, 1)

                def x_transposes(e):
                    pe.wait_ge(s_rt, e + 1)
                    pe.wait_ge(s_g, 16 * e + 16)
                    for k in range(DT):
                        m = pe.transpose(psT[:, k // 4, P * (k % 4):P * (k % 4) + P], xg[:, P * k:P * k + P], ident[:])
                    m.then_inc(s_xf, 1)

                def hid_transposes(e, n):
                    pe.wait_ge(s_hid, 4 * e + n + 1)
                    if n >= 2:
                        pe.wait_ge(s_ht, 4 * e + n - 1)
                    for i in range(4):
                        m = pe.transpose(psT[:, n % 2, P * i:P * i + P], hid[:, n % 2, P * i:P * i + P], ident[:])
                    m.then_inc(s_hf, 1)

                def body(e, par, last):
                    pe.wait_ge(s_xh, e + 1)
                    pe.wait_ge(s_xl, e + 1)
                    for n in range(4):
                        for m_, bank in ((0, psG), (1, psU)):
                            if n < 2:
                                pe.wait_ge(s_hid, 4 * e + n - 2 + 1) if not (isinstance(e, int) and e == 0) else None
                            else:
                                pe.wait_ge(s_hid, 4 * e + n - 2 + 1)
                            for half in range(2):
                                i = 4 * n + 2 * m_ + half
                                pe.wait_ge(s_lo, NGU * e + i + 1)
                                for k in range(4):
                                    kk = 4 * half + k
                                    for j, (a, b) in enumerate(((xh, wh), (xl, wh), (xh, wl))):
                                        mm = pe.matmul(bank[:, n % 2, :], a[:, par, kk, :], b[:, i % SPLIT, k, :],
                                                       start=(kk == 0 and j == 0), stop=(kk == DT - 1 and j == 2))
                                mm.then_inc(s_gu, 1)
                        if n >= 1:
                            hid_transposes(e, n - 1)
                    for j in range(NDN):
                        i = NGU + j
                        pe.wait_ge(s_ld[i % RING], 48 * e + 16 * (i // RING + 1))
                        if j == 0:
                            if not (isinstance(e, int) and e == 0):
                                pe.wait_ge(s_y, e)
                        if j % 2 == 0:
                            pe.wait_ge(s_ht, 4 * e + j // 2 + 1)
                        wdn = ring[:, i % RING, :].rearrange("p (k c) -> p k c", k=2)
                        for k in range(2):
                            for c in range(2):
                                mm = pe.matmul(psY[:, c, :], hidT[:, 2 * j + k, :], wdn[:, k, 512 * c:512 * c + 512],
                                               start=(j == 0 and k == 0), stop=(j == NDN - 1 and k == 1))
                        mm.then_inc(s_dn, 1)
                        if j == 1:
                            hid_transposes(e, 3)
                        if j == 5 and not last:
                            pe.wait_ge(s_ht, 4 * e + 4)
                            route(e + 1)
                    if not last:
                        x_transposes(e + 1)

                pe.wait_ge(s_c, 80)
                route(0)
                x_transposes(0)
                body(0, 0, False)
                body(1, 1, False)
                with pe.Fori(2, NE - 2, 2) as e:
                    body(e, 0, False)
                    body(e + 1, 1, False)
                body(NE - 2, 0, False)
                body(NE - 1, 1, True)

            @block.scalar
            def _(act):
                def hi(e, i):
                    act.wait_ge(s_ld[i % RING], 48 * e + 16 * (i // RING + 1))
                    if not (isinstance(e, int) and e == 0 and i < SPLIT):
                        act.wait_ge(s_gu, NGU * e + i - SPLIT + 1)
                    act.activation(wh[:, i % SPLIT], ring[:, i % RING, :].rearrange("p (k c) -> p k c", k=4), ACT.Identity).then_inc(s_hi, 1)

                def silu(e, n):
                    act.wait_ge(s_gu, NGU * e + 4 * n + 2)
                    if n or not (isinstance(e, int) and e == 0):
                        act.wait_ge(s_hid, 4 * e + n)
                    act.activation(sg[:], psG[:, n % 2, :], ACT.Silu).then_inc(s_sg, 1)

                def take_hid(e, n):
                    act.wait_ge(s_hf, 4 * e + n + 1)
                    act.activation(hidT[:, 4 * n:4 * n + 4, :], psT[:, n % 2, :].rearrange("p (k c) -> p k c", k=4), ACT.Identity).then_inc(s_ht, 1)

                def x_high(e, par):
                    act.wait_ge(s_xt, e + 1)
                    act.activation(xh[:, par], xT[:], ACT.Identity).then_inc(s_xh, 1)

                def body(e, par, last):
                    for i in range(SPLIT, NGU):
                        hi(e, i)
                        if i in (5, 9, 13):
                            silu(e, (i - 5) // 4)
                        if i == 11 or i == 15:
                            take_hid(e, (i - 11) // 4)
                    silu(e, 3)
                    take_hid(e, 2)
                    take_hid(e, 3)
                    if not last:
                        for i in range(SPLIT):
                            hi(e + 1, i)
                        x_high(e + 1, 1 - par)
                    act.wait_ge(s_dn, NDN * e + NDN)
                    if not (isinstance(e, int) and e == 0):
                        act.wait_ge(s_sc, 16 * e)
                    act.activation(y[:].rearrange("p (a c) -> p a c", a=2), psY[:], ACT.Identity, scale=gate[:, par:par + 1]).then_inc(s_y, 1)

                for i in range(SPLIT):
                    hi(0, i)
                x_high(0, 0)
                body(0, 0, False)
                body(1, 1, False)
                with act.Fori(2, NE - 2, 2) as e:
                    body(e, 0, False)
                    body(e + 1, 1, False)
                body(NE - 2, 0, False)
                body(NE - 1, 1, True)

            @block.vector
            def _(dve):
                own_before = [0]
                one, so_far = raise_counts()

                def ranks(e, ts):
                    if ts[0] == 0:
                        dve.wait_ge(s_p, 32 * e + 32)
                        dve.memset(cnt[:, 0, 0:1], 0.0).then_inc(own_dve, one(own_dve))
                    for t in ts:
                        own_p = pcol[:, t:t + 1]
                        a = P * t
                        dve.wait_ge(own_dve, own_before[0] + so_far(own_dve))
                        if t:
                            dve.tensor_scalar(cmp[:, 0:a], prow[:, 0:a], own_p, None, ALU.is_ge, ALU.add,
                                              accum_out=cnt[:, t, 0:1]).then_inc(own_dve, one(own_dve))
                        dve.tensor_scalar(cmp[:, a:L], prow[:, a:L], own_p, None, ALU.is_gt, ALU.add,
                                          accum_out=cnt[:, t, 1:2]).then_inc(own_dve, one(own_dve))
                        dve.scalar_tensor_tensor(out=hot[:, t, :], in0=prow[:, a:a + P], scalar=own_p, in1=lower[:],
                                                 op0=ALU.is_equal, op1=ALU.mult, accum_out=cnt[:, t, 2:3]).then_inc(own_dve, one(own_dve))

                def slots(e):
                    dve.wait_ge(own_dve, own_before[0] + so_far(own_dve))
                    dve.tensor_reduce(rank[:], cnt[:], AX_X, ALU.add).then_inc(own_dve, one(own_dve))
                    dve.tensor_copy(vals[:, :, 1:2], pcol[:].unsqueeze(2)).then_inc(s_rank, 1)
                    dve.wait_ge(own_dve, own_before[0] + so_far(own_dve))
                    for t in range(TT - 1):
                        dve.tensor_scalar(hot[:, t, :], iota[:], rank[:, t:t + 1], None, ALU.is_equal).then_inc(own_dve, one(own_dve))
                    dve.tensor_scalar(hot[:, TT - 1, :], iota[:], rank[:, TT - 1:TT], None, ALU.is_equal).then_inc(s_hot, 1)

                def take_route(e, par):
                    dve.wait_ge(s_rf, e + 1)
                    if not (isinstance(e, int) and e < 2):
                        dve.wait_ge(s_sc, 16 * (e - 1))
                    dve.tensor_copy(gate[:, par:par + 1], psT[:, 0, 1:2]).then_inc(own_dve, one(own_dve))
                    dve.tensor_copy(idx[:, par, :], psT[:, 0, 0:1]).then_inc(s_rt, 1)

                def take_x(e, par):
                    dve.wait_ge(s_xf, e + 1)
                    dve.tensor_tensor(xT[:], psT[:].rearrange("p a (k c) -> p (a k) c", c=P),
                                      lnw[:].unsqueeze(2).to_broadcast([P, DT, P]), ALU.mult).then_inc(s_xt, 1)
                    dve.wait_ge(s_xh, e + 1)
                    dve.tensor_tensor(xl[:, par], xT[:], xh[:, par], ALU.subtract).then_inc(s_xl, 1)

                def lo(e, i):
                    dve.wait_ge(s_hi, NGU * e + i + 1)
                    dve.tensor_tensor(wl[:, i % SPLIT], ring[:, i % RING, :].rearrange("p (k c) -> p k c", k=4), wh[:, i % SPLIT],
                                      ALU.subtract).then_inc(s_lo, 1)

                def hidden(e, n):
                    dve.wait_ge(s_sg, 4 * e + n + 1)
                    dve.wait_ge(s_gu, NGU * e + 4 * n + 4)
                    if n >= 2:
                        dve.wait_ge(s_hf, 4 * e + n - 1)
                    dve.tensor_tensor(hid[:, n % 2, :], sg[:], psU[:, n % 2, :], ALU.mult).then_inc(s_hid, 1)

                def body(e, par, last):
                    for i in range(SPLIT, NGU):
                        lo(e, i)
                        if i in (7, 11, 15):
                            hidden(e, (i - 7) // 4)
                        if i in (5, 8, 10, 13) and not last:
                            ranks(e + 1, [(5, 8, 10, 13).index(i)])
                    hidden(e, 3)
                    if not last:
                        ranks(e + 1, [4, 5, 6, 7])
                        slots(e + 1)
                        take_route(e + 1, 1 - par)
                        lo(e + 1, 0)
                        lo(e + 1, 1)
                        take_x(e + 1, 1 - par)
                        lo(e + 1, 2)
                        lo(e + 1, 3)

                dve.wait_ge(s_c, 80)
                ranks(0, range(TT))
                slots(0)
                take_route(0, 0)
                for i in range(SPLIT):
                    lo(0, i)
                take_x(0, 0)
                before = so_far(own_dve)
                body(0, 0, False)
                per_expert = so_far(own_dve) - before
                body(1, 1, False)
                with dve.Fori(2, NE - 2, 2) as e:
                    one, so_far = raise_counts()
                    own_before[0] = before + per_expert * e
                    body(e, 0, False)
                    body(e + 1, 1, False)
                one, so_far = raise_counts()
                own_before[0] = before + per_expert * (NE - 2)
                body(NE - 2, 0, False)
                body(NE - 1, 1, True)


def embed_stage(nc, dram, scratch, own, out, tile_loaded, loads_before, ring, piece_loaded, p, wp, s_p):
    own_dve, own_act, one, so_far = own
    SHARED = (((0, 2), (2, 5), (5, 8)), ((0, 4), (4, 7), (7, 8)))
    with ExitStack() as ctx:
        sb = lambda name, shape, dt=F32: ctx.enter_context(nc.sbuf_tensor(name, shape, dt))
        ps = lambda name, n: ctx.enter_context(nc.psum_tensor(name, [P, n, 512], F32))
        sem = lambda name: ctx.enter_context(nc.semaphore(name))
        r, emb = (ring[:, RING // 2 * i:RING // 2 * (i + 1), :].rearrange("p a (b c) -> p (a b) c", c=D) for i in range(2))
        pT = sb("f_pT", [P, 2, 2, P])
        w = sb("f_w", [P, 2, 2, D])
        wh = sb("f_wh", [P, DT, D], F32R)
        wl = sb("f_wl", [P, DT, D], F32R)
        h = sb("f_h", [P, 2, D])
        hT = sb("f_hT", [P, DT, P])
        hh = sb("f_hh", [P, 2, DT, P], F32R)
        hl = sb("f_hl", [P, 2, DT, P], F32R)
        sg = sb("f_sg", [P, D])
        sq = sb("f_sq", [P, D])
        lnw = sb("f_lnw", [P, DT])
        fin = sb("f_fin", [P, D])
        ident = sb("f_ident", [P, P])
        ssq = sb("f_ssq", [P, 2, TT])
        rs = sb("f_rs", [P, 2, 4, TT])
        psT, psP, psG = ps("f_psT", 2), ps("f_psP", 2), ps("f_psG", 4)

        s_c, s_fin = sem("f_constants"), sem("f_final_w_loaded")
        pieces_before = 16 * (NGU + NDN) // RING * NE
        s_pt, s_pT = sem("f_p_transposed"), sem("f_pT_taken")
        s_pp, s_emb = sem("f_embedding_product"), sem("f_embedding_taken")
        s_wh, s_wl = sem("f_wh_ready"), sem("f_wl_ready")
        s_sq, s_var, s_rt = sem("f_squares"), sem("f_variance"), sem("f_root")
        s_h, s_hf = sem("f_normed"), sem("f_h_transposed")
        s_hT, s_hh, s_hl = sem("f_hT_ready"), sem("f_hh_ready"), sem("f_hl_ready")
        s_g, s_sg, s_r2 = sem("f_gate_product"), sem("f_gate_ready"), sem("f_embedding_added")
        s_out, s_st = sem("f_out_ready"), sem("f_stored")

        with nc.Block() as block:
            @block.sync
            def _(sp):
                sp.dma_start(ident[:], dram["c_ident"]).then_inc(s_c, 16)
                sp.dma_start(lnw[:], dram["l_ln_ple"]).then_inc(s_c, 16)
                for i in range(4):
                    if i >= 2:
                        sp.wait_ge(s_wl, i - 1)
                    sp.dma_start(w[:, i % 2], dram["w_ple_gate"][0, 2 * P * i:2 * P * i + 2 * P, :].rearrange("(k p) c -> p k c", p=P)).then_inc(piece_loaded[i % 2], 16)
                    for t in (2 * i, 2 * i + 1):
                        sp.dma_start(r[:, t, :], scratch["r"][P * t:P * t + P, :]).then_inc(tile_loaded[t], 16)
                sp.dma_start(fin[:], dram["final_norm_w"].unsqueeze(0).to_broadcast([P, D])).then_inc(s_fin, 16)
                for t in range(TT):
                    sp.wait_ge(s_out, t + 1)
                    sp.dma_start(out[0, P * t:P * t + P, :], r[:, t, :]).then_inc(s_st, 16)
                sp.wait_ge(s_st, 16 * TT)

            @block.tensor
            def _(pe):
                pe.wait_ge(s_c, 32)
                pe.wait_ge(s_p, 32)
                for i in range(TT + 1):
                    if i < TT:
                        if i >= 2:
                            pe.wait_ge(s_pT, i - 1)
                        for k in range(2):
                            m = pe.transpose(psT[:, i % 2, P * k:P * k + P], p[:, i, P * k:P * k + P], ident[:])
                        m.then_inc(s_pt, 1)
                    if i >= 1:
                        t = i - 1
                        pe.wait_ge(s_pT, t + 1)
                        for c in range(2):
                            if t:
                                pe.wait_ge(s_emb, 2 * t + c - 1)
                            for k in range(2):
                                m = pe.matmul(psP[:, c, :], pT[:, t % 2, k, :], wp[:, k, 512 * c:512 * c + 512], start=(k == 0), stop=(k == 1))
                            m.then_inc(s_pp, 1)
                pe.wait_ge(s_pT, TT)
                for i in range(TT + 1):
                    if i < TT:
                        pe.wait_ge(s_h, i + 1)
                        if i:
                            pe.wait_ge(s_hT, i)
                        for k in range(DT):
                            m = pe.transpose(psT[:, k // 4, P * (k % 4):P * (k % 4) + P], h[:, i % 2, P * k:P * k + P], ident[:])
                        m.then_inc(s_hf, 1)
                    if i >= 1:
                        t = i - 1
                        pe.wait_ge(s_hh, t + 1)
                        pe.wait_ge(s_hl, t + 1)
                        pe.wait_ge(s_wl, 4)
                        for c in range(2):
                            n = 2 * t + c
                            if n >= 4:
                                pe.wait_ge(s_sg, n - 3)
                            for k in range(DT):
                                for j, (a, b) in enumerate(((hh, wh), (hl, wh), (hh, wl))):
                                    m = pe.matmul(psG[:, n % 4, :], a[:, t % 2, k, :], b[:, k, 512 * c:512 * c + 512],
                                                  start=(k == 0 and j == 0), stop=(k == DT - 1 and j == 2))
                            m.then_inc(s_g, 1)

            @block.scalar
            def _(act):

                def embedding(t):
                    act.wait_ge(s_pt, t + 1)
                    if t >= 2:
                        act.wait_ge(s_pp, 2 * (t - 2) + 2)
                    act.activation(pT[:, t % 2], psT[:, t % 2, 0:2 * P].rearrange("p (k c) -> p k c", k=2), ACT.Identity).then_inc(s_pT, one(s_pT))

                def take_embedding(t):
                    for c in range(2):
                        act.wait_ge(s_pp, 2 * t + c + 1)
                        act.activation(emb[:, t, 512 * c:512 * c + 512], psP[:, c, :], ACT.Identity).then_inc(s_emb, one(s_emb))

                def square(phase, t):
                    if so_far(s_pT):
                        act.wait_ge(s_pT, so_far(s_pT))
                    if so_far(s_emb):
                        act.wait_ge(s_emb, so_far(s_emb))
                    if so_far(s_sg):
                        act.wait_ge(s_sg, so_far(s_sg))
                    act.activation(sq[:], r[:, t, :], ACT.Square, accum_out=ssq[:, phase, t:t + 1]).then_inc(s_sq, one(s_sq))

                def root(phase, t):
                    for n, (a, b) in enumerate(SHARED[phase]):
                        if b == t + 1:
                            act.wait_ge(s_var, n + 1 + phase * len(SHARED[0]))
                            act.activation(rs[:, phase, 1, a:b], rs[:, phase, 0, a:b], ACT.Sqrt).then_inc(s_rt, 1)

                for t in range(TT):
                    embedding(t)
                    if t:
                        take_embedding(t - 1)
                    if t < 4:
                        i = t
                        act.wait_ge(piece_loaded[i % 2], pieces_before + 16 * (i // 2 + 1))
                        act.activation(wh[:, 2 * i:2 * i + 2, :], w[:, i % 2], ACT.Identity).then_inc(s_wh, 1)
                    act.wait_ge(tile_loaded[t], loads_before + 16)
                    square(0, t)
                    root(0, t)
                take_embedding(TT - 1)
                for i in range(TT + 1):
                    if i < TT:
                        act.wait_ge(s_hT, i + 1)
                        if i >= 2:
                            act.wait_ge(s_g, 2 * (i - 2) + 2)
                        act.activation(hh[:, i % 2], hT[:], ACT.Identity).then_inc(s_hh, 1)
                    if i >= 1:
                        t = i - 1
                        if t:
                            act.wait_ge(s_r2, t)
                        for c in range(2):
                            act.wait_ge(s_g, 2 * t + c + 1)
                            act.activation(sg[:, 512 * c:512 * c + 512], psG[:, (2 * t + c) % 4, :], ACT.Sigmoid).then_inc(s_sg, one(s_sg))
                        act.wait_ge(s_r2, t + 1)
                        square(1, t)
                        root(1, t)

            @block.vector
            def _(dve):

                def inverse_root(phase, a, b, n):
                    dve.wait_ge(s_sq, phase * TT + b)
                    if so_far(s_r2):
                        dve.wait_ge(s_r2, so_far(s_r2))
                    dve.tensor_scalar(rs[:, phase, 0, a:b], ssq[:, phase, a:b], 1.0 / D, EPS, ALU.mult, ALU.add).then_inc(s_var, one(s_var))
                    dve.wait_ge(s_rt, n + 1)
                    dve.reciprocal(rs[:, phase, 2, a:b], rs[:, phase, 1, a:b]).then_inc(own_dve, one(own_dve))
                    newton(dve, own_dve, one, so_far, rs[:, phase, :, a:b])

                def low_halves(i):
                    dve.wait_ge(s_wh, i + 1)
                    dve.tensor_tensor(wl[:, 2 * i:2 * i + 2, :], w[:, i % 2], wh[:, 2 * i:2 * i + 2, :], ALU.subtract).then_inc(s_wl, 1)

                low_halves(0)
                low_halves(1)
                inverse_root(0, *SHARED[0][0], 0)
                low_halves(2)
                low_halves(3)
                inverse_root(0, *SHARED[0][1], 1)
                inverse_root(0, *SHARED[0][2], 2)
                dve.wait_ge(s_c, 32)
                dve.wait_ge(s_fin, 16)

                def normed(t):
                    if t >= 2:
                        dve.wait_ge(s_hf, t - 1)
                    dve.tensor_scalar(h[:, t % 2, :], r[:, t, :], rs[:, 0, 2, t:t + 1], None, ALU.mult).then_inc(s_h, one(s_h))

                normed(0)
                for i in range(TT + 1):
                    if i < TT:
                        if i + 1 < TT:
                            normed(i + 1)
                        dve.wait_ge(s_hf, i + 1)
                        if so_far(s_h):
                            dve.wait_ge(s_h, so_far(s_h))
                        if so_far(s_r2):
                            dve.wait_ge(s_r2, so_far(s_r2))
                        dve.tensor_tensor(hT[:], psT[:].rearrange("p a (k c) -> p (a k) c", c=P),
                                                     lnw[:].unsqueeze(2).to_broadcast([P, DT, P]), ALU.mult).then_inc(s_hT, one(s_hT))
                        dve.wait_ge(s_hh, i + 1)
                        dve.wait_ge(s_hT, so_far(s_hT))
                        dve.tensor_tensor(hl[:, i % 2], hT[:], hh[:, i % 2], ALU.subtract).then_inc(s_hl, one(s_hl))
                    if i >= 1:
                        t = i - 1
                        dve.wait_ge(s_sg, 2 * t + 2)
                        dve.wait_ge(s_emb, 2 * t + 2)
                        dve.tensor_tensor(emb[:, t, :], emb[:, t, :], sg[:], ALU.mult).then_inc(own_dve, one(own_dve))
                        dve.wait_ge(own_dve, so_far(own_dve))
                        dve.tensor_tensor(r[:, t, :], r[:, t, :], emb[:, t, :], ALU.add).then_inc(s_r2, one(s_r2))
                        for n, (a, b) in enumerate(SHARED[1]):
                            if b == t + 1:
                                inverse_root(1, a, b, len(SHARED[0]) + n)
                                for u in range(a, b):
                                    dve.scalar_tensor_tensor(out=r[:, u, :], in0=r[:, u, :], scalar=rs[:, 1, 2, u:u + 1], in1=fin[:],
                                                                        op0=ALU.mult, op1=ALU.mult).then_inc(s_out, one(s_out))


def program(nc, dram, out):
    scratch = {name: nc.dram_tensor("s_" + name, shape, F32, kind="Internal").ap() for name, shape in {
        "hy": (3, L, HW), "code": (2 * RANK, L), "qk": (2 * QK // P, P, L), "vg": (2, L, GW),
        "spec": (ORDER, 2, P, GROUPS, 2, HALF), "r": (L, D), "h2": (L, D), "prow": (NE, L), "pcol": (NE, P, TT)}.items()}
    sem = nc.alloc_semaphore
    own = (sem("own_dve"), sem("own_act"), *raise_counts())
    tile_loaded = [sem(f"tile_loaded{t}") for t in range(TT)]
    w_out_loaded = [sem(f"w_out_loaded{c}") for c in range(2)]
    piece_loaded = [sem(f"piece_loaded{i}") for i in range(RING)]
    p_loaded = sem("ple_loaded")
    with ExitStack() as upper:
        wide = upper.enter_context(nc.sbuf_tensor("hT_then_w_out", [P, DT, L], F32, side="right"))
        filter_stage(nc, dram, scratch, own, tile_loaded, wide)
        mix = upper.enter_context(nc.sbuf_tensor("mix", [P, TT, D], F32, side="right"))
        hyena_stage(nc, dram, scratch, own, wide, mix)
        attention_stage(nc, dram, scratch, own, mix, wide, w_out_loaded)
        ring_guard = nc.sbuf_tensor("ring", [P, RING, 4 * 512], F32)
        ring = ring_guard.__enter__()
        residual_stage(nc, dram, scratch, own, tile_loaded, 16, ring, piece_loaded, mix, wide, w_out_loaded)
    with nc.sbuf_tensor("ple", [P, TT, PLE], F32) as p, nc.sbuf_tensor("ple_proj", [P, 2, D], F32) as wp:
        expert_stage(nc, dram, scratch, ring, piece_loaded, p, wp, p_loaded)
        embed_stage(nc, dram, scratch, own, out, tile_loaded, 32, ring, piece_loaded, p, wp, p_loaded)
    ring_guard.__exit__(None, None, None)


INPUTS = ["x", "p", "w_in", "gla_wa_f", "gla_wa_b", "gla_norm_w", "hy_f_w1", "hy_f_w2", "hy_f_w3", "hy_bias", "w_out", "ln_ffn_w",
          "w_router", "w_gate_e", "w_up_e", "w_down_e", "w_ple_gate", "w_ple_proj", "final_norm_w"]


def by_partition(a):
    a = np.asarray(a)
    return np.ascontiguousarray(np.moveaxis(a.reshape(*a.shape[:-1], -1, P), -1, 0))


def kernel(**inputs):
    import concourse.bacc as bacc
    from concourse.bass_utils import run_bass_kernel_spmd as run
    nc = bacc.Bacc("TRN2", target_bir_lowering=False, num_devices=1)
    arrays = {name: np.ascontiguousarray(inputs[name]) for name in INPUTS}
    arrays.update(shape_constants())
    arrays["l_ln_mix"] = by_partition(inputs["ln_mix_w"][0])
    arrays["l_ln_ffn"] = by_partition(inputs["ln_ffn_w"][0])
    arrays["l_ln_ple"] = by_partition(inputs["ln_ple_w"][0])
    arrays["l_conv_w"] = by_partition(inputs["hy_conv_w"][0])
    arrays["l_conv_b"] = by_partition(inputs["hy_conv_b"][0])
    arrays["l_gate_b"] = by_partition(np.stack([inputs["gla_ba_f"][0], inputs["gla_ba_b"][0]]))
    arrays["l_filter"] = np.ascontiguousarray(np.stack([inputs[n][0] for n in ("hy_f_b1", "hy_f_freq1", "hy_f_b2", "hy_f_freq2")], 1))
    dram = {name: nc.dram_tensor("in_" + name, a.shape, mybir.dt.from_np(a.dtype), kind="ExternalInput").ap() for name, a in arrays.items()}
    out = nc.dram_tensor("out", (1, L, D), F32, kind="ExternalOutput").ap()
    program(nc, dram, out)
    r = run(nc, [{"in_" + name: a for name, a in arrays.items()}], core_ids=[0])
    return r.results[0]["out"]
```

```python
from contextlib import ExitStack
import math

import numpy as np
import concourse.bass as bass
from concourse import mybir

ALU = mybir.AluOpType
ACT = mybir.ActivationFunctionType
AX_X = mybir.AxisListType.X
F32 = mybir.dt.float32
F32R = mybir.dt.float32r
I32 = mybir.dt.int32

P = 128
D = 1024
L = 1024
DT = D // P
TT = L // P
EPS = 1e-6
HEADS, DK, DV = 4, D // 16, D // 8
QK, GW, RANK = HEADS * DK, HEADS * DV, 16
TAU = 16.0
HW = D - GW
ORDER, FFN, BANDS = 2, 64, 8
EMB = 1 + 2 * BANDS
NE = 16
CAP = 2 * L // NE
assert CAP == P
FF = 2 * D
PLE = 256
Q0, K0, V0, G0 = 0, QK, 2 * QK, 2 * QK + GW
C0 = G0 + GW
H0 = C0 + 2 * RANK

NFFT = 2 * L
HALF = HW // 2
GROUPS = 8
RESIDUES = [(0, 0), (4, -1), (2, -1), (6, 1), (1, -1), (9, -1), (5, -1), (13, -1)]
C45 = math.cos(math.pi / 4)
C22 = math.cos(math.pi / 8)
T22 = math.tan(math.pi / 8)


def shape_constants():
    p = np.arange(P, dtype=np.float64)[:, None]
    j = np.arange(P, dtype=np.float64)[None, :]
    fwd = np.zeros((GROUPS, 4, P, P))
    weight = np.full((GROUPS, 2, P), 2.0 / NFFT)
    for g, (r, s) in enumerate(RESIDUES):
        if g == 0:
            for part, r0 in ((0, 0), (1, 8)):
                th = 2 * np.pi * p * (r0 + 16 * j[:, :64]) / NFFT
                fwd[0, part, :, 64 * part:64 * part + 64] = np.cos(th)
                fwd[0, 2 + part, :, 64 * part:64 * part + 64] = -np.sin(th)
            fwd[0, 2, :, 0] = (-1.0) ** np.arange(P)
            weight[0, :, 0] = 1.0 / NFFT
        else:
            th = 2 * np.pi * p * (r + 16 * j) / NFFT
            mr, mi = np.cos(th), -np.sin(th)
            fwd[g, 0], fwd[g, 1] = mr, -mi * s
            fwd[g, 2], fwd[g, 3] = mi, mr * s
    inv = np.zeros((GROUPS, 4, P, P))
    for g in range(GROUPS):
        for q in range(4):
            inv[g, q] = fwd[g, q].T * weight[g, q // 2][:, None]
    f32 = np.float32
    t = np.linspace(0.0, 1.0, L, dtype=f32)[:, None]
    w_pos = (f32(2.0 * math.pi) * np.arange(L, dtype=f32)[:, None] / f32(L)).astype(f32)
    f = np.linspace(1e-4, BANDS - 1, BANDS, dtype=f32)[None]
    z = np.concatenate([t, np.cos(f * w_pos), -np.sin(f * w_pos)], axis=-1).astype(f32)
    lo, hi = math.log(1e-2) / 1.5, math.log(1e-2) / 0.3
    deltas = np.abs(np.linspace(lo, hi, HW, dtype=f32))
    decay = np.exp(-t * deltas[None]).astype(f32)
    s_idx, t_idx = np.arange(P)[:, None], np.arange(P)[None, :]
    same = (s_idx // 64) == (t_idx // 64)
    masks = np.stack([same & (s_idx <= t_idx), same & (s_idx > t_idx)], 1).astype(np.int32)
    return {
        "c_fwd": np.ascontiguousarray(fwd.transpose(2, 0, 1, 3).reshape(P, -1).astype(f32)),
        "c_inv": np.ascontiguousarray(inv.transpose(2, 0, 1, 3).reshape(P, -1).astype(f32)),
        "c_z": np.ascontiguousarray(z.T),
        "c_decay": decay,
        "c_ident": np.eye(P, dtype=f32),
        "c_mask": np.ascontiguousarray(masks),
        "c_iota": np.tile(np.arange(P, dtype=f32)[None], (P, 1)),
        "c_tok": np.ascontiguousarray(np.arange(L, dtype=f32).reshape(TT, P).T),
        "c_lower": (s_idx > t_idx).astype(f32),
        "c_sel": np.ascontiguousarray(np.repeat(np.eye(NE, dtype=f32)[:, :, None], P, 2).reshape(NE, NE * P)),
    }


def raise_counts():
    raised = {}

    def one(sem):
        raised[sem] = raised.get(sem, 0) + 1
        return 1

    def so_far(sem):
        return raised.get(sem, 0)

    return one, so_far


def forward_tree(dve, own, one, so_far, U, V, T, tree_done):
    s, d, pp, m, A, B, x1, x3 = (T[:, a:b, :] for a, b in
                                 ((0, 4), (4, 8), (8, 10), (10, 12), (12, 14), (14, 16), (16, 18), (18, 20)))
    add, sub, mul = ALU.add, ALU.subtract, ALU.mult
    dve.tensor_tensor(s, U[:, 0:4, :], U[:, 4:8, :], add).then_inc(own, one(own))
    dve.tensor_tensor(d, U[:, 0:4, :], U[:, 4:8, :], sub).then_inc(own, one(own))
    dve.scalar_tensor_tensor(out=x1[:, 0, :], in0=U[:, 5, :], scalar=-T22, in1=U[:, 1, :], op0=mul, op1=add).then_inc(own, one(own))
    dve.scalar_tensor_tensor(out=x1[:, 1, :], in0=U[:, 1, :], scalar=T22, in1=U[:, 5, :], op0=mul, op1=add).then_inc(own, one(own))
    dve.scalar_tensor_tensor(out=x3[:, 0, :], in0=U[:, 3, :], scalar=T22, in1=U[:, 7, :], op0=mul, op1=sub).then_inc(own, one(own))
    dve.scalar_tensor_tensor(out=x3[:, 1, :], in0=U[:, 7, :], scalar=T22, in1=U[:, 3, :], op0=mul, op1=add).then_inc(own, one(own))
    dve.wait_ge(own, so_far(own))
    dve.tensor_tensor(pp, s[:, 0:2, :], s[:, 2:4, :], add).then_inc(own, one(own))
    dve.tensor_tensor(V[:, 2:4, :], s[:, 0:2, :], s[:, 2:4, :], sub).then_inc(own, one(own))
    dve.tensor_tensor(m[:, 0, :], d[:, 1, :], d[:, 3, :], sub).then_inc(own, one(own))
    dve.tensor_tensor(m[:, 1, :], d[:, 1, :], d[:, 3, :], add).then_inc(own, one(own))
    ds = T[:, 6:1:-4, :]
    u04 = U[:, 0:5:4, :]
    dve.scalar_tensor_tensor(out=A, in0=ds, scalar=C45, in1=u04, op0=mul, op1=add).then_inc(own, one(own))
    dve.scalar_tensor_tensor(out=B, in0=ds, scalar=-C45, in1=u04, op0=mul, op1=add).then_inc(own, one(own))
    dve.wait_ge(own, so_far(own))
    dve.tensor_tensor(V[:, 0, :], pp[:, 0, :], pp[:, 1, :], add).then_inc(own, one(own))
    dve.tensor_tensor(V[:, 1, :], pp[:, 0, :], pp[:, 1, :], sub).then_inc(own, one(own))
    d02 = T[:, 4:7:2, :]
    dve.scalar_tensor_tensor(out=V[:, 4:6, :], in0=m, scalar=C45, in1=d02, op0=mul, op1=add).then_inc(own, one(own))
    dve.scalar_tensor_tensor(out=V[:, 6:8, :], in0=m, scalar=-C45, in1=d02, op0=mul, op1=add).then_inc(own, one(own))
    Cc, Dd = T[:, 0:2, :], T[:, 2:4, :]
    dve.tensor_tensor(Cc, x1, x3, add).then_inc(own, one(own))
    dve.tensor_tensor(Dd, x1, x3, sub).then_inc(own, one(own))
    dve.wait_ge(own, so_far(own))
    dve.scalar_tensor_tensor(out=V[:, 8:10, :], in0=Cc, scalar=C22, in1=A, op0=mul, op1=add).then_inc(own, one(own))
    dve.scalar_tensor_tensor(out=V[:, 10:12, :], in0=Cc, scalar=-C22, in1=A, op0=mul, op1=add).then_inc(own, one(own))
    Dnr, Bnr = T[:, 3:1:-1, :], T[:, 15:13:-1, :]
    dve.scalar_tensor_tensor(out=V[:, 13:15, :], in0=Dd, scalar=C22, in1=Bnr, op0=mul, op1=add).then_inc(own, one(own))
    dve.scalar_tensor_tensor(out=V[:, 12:16:3, :], in0=Dnr, scalar=-C22, in1=B, op0=mul, op1=add).then_inc(tree_done, one(tree_done))


def newton(dve, own, one, so_far, rs):
    v, r, u = rs[:, 0, :], rs[:, 2, :], rs[:, 3, :]
    dve.wait_ge(own, so_far(own))
    dve.tensor_tensor(u, r, r, ALU.mult).then_inc(own, one(own))
    dve.wait_ge(own, so_far(own))
    dve.tensor_tensor(u, u, v, ALU.mult).then_inc(own, one(own))
    dve.wait_ge(own, so_far(own))
    dve.tensor_scalar(u, u, -0.5, 1.5, ALU.mult, ALU.add).then_inc(own, one(own))
    dve.wait_ge(own, so_far(own))
    dve.tensor_tensor(r, r, u, ALU.mult).then_inc(own, one(own))
    dve.wait_ge(own, so_far(own))


WC = 256
WB = 2
HY_LOADS = 3 * HW // WC
ATT_LOADS = [(C0, 2 * RANK)] + [(Q0 + WC * c, WC) for c in range((C0 - Q0) // WC)]


def filter_stage(nc, dram, scratch, own, tile_loaded, hT, x_sb, w_sb, w_loaded):
    own_dve, own_act, one, so_far = own
    with ExitStack() as ctx:
        sb = lambda name, shape, dt=F32: ctx.enter_context(nc.sbuf_tensor(name, shape, dt))
        sem = lambda name: ctx.enter_context(nc.semaphore(name))
        V = x_sb[:].rearrange("p t (a c) -> p (t a) c", c=HALF).rearrange("p (b s) c -> p b s c", b=2)
        fwd = sb("fwd", [P, GROUPS, 4, P])
        ident = sb("ident", [P, P])
        lnw = sb("lnw", [P, DT])
        ssq = sb("ssq", [P, TT])
        rstd = sb("rstd", [P, 4, TT])
        cw = sb("cw", [P, 3, 12])
        cb = sb("cb", [P, 12])
        tap = sb("tap", [P, 2, L])
        zT_hdn2 = sb("zT_hdn2", [FFN, L])
        zT, hdn2 = zT_hdn2[0:EMB, :], zT_hdn2
        fw1 = sb("fw1", [EMB, FFN])
        fw2 = sb("fw2", [FFN, FFN])
        fcol = sb("fcol", [FFN, 4])
        w3 = sb("w3", [FFN, ORDER, 2, HW])
        w3eo = sb("w3eo", [FFN, 2, ORDER, HW])
        arg = sb("arg", [FFN, L])
        red = sb("red", [FFN, L])
        hdn1 = red
        hbias = sb("hbias", [1, ORDER, HW])
        row0 = hbias
        decay = sb("decay", [P, TT, HW])
        eo = sb("eo", [P, TT, HALF])
        T = sb("T", [P, 20, HALF])
        spec = sb("spec", [P, GROUPS, 2, HALF])
        nyq = sb("nyq", [1, HALF])
        stage = sb("stage", [P, 2, L])
        acc = ctx.enter_context(nc.psum_tensor("acc", [P, 2, L], F32))
        psA = ctx.enter_context(nc.psum_tensor("psA", [P, 2, 512], F32))
        psB = ctx.enter_context(nc.psum_tensor("psB", [P, 2, 512], F32))

        s_x = tile_loaded
        s_small = sem("small_loaded")
        s_tab = sem("tables_loaded")
        s_filt = sem("filter_weights_loaded")
        s_decay = sem("decay_loaded")
        s_w = w_loaded
        s_ssq = sem("squares_summed")
        s_var = sem("variance_ready")
        s_root = sem("root_ready")
        s_xs = sem("x_scaled")
        s_pt = sem("h_transposed")
        s_ht = sem("hT_ready")
        s_pre = sem("filter_preact")
        s_arg = sem("filter_arg_reduced")
        s_hdn = sem("filter_hidden")
        s_w3 = sem("w3_combined")
        s_row = sem("row0_product")
        s_row0 = sem("row0_ready")
        s_acc = sem("acc_done")
        s_gen = sem("filter_product")
        s_genu = sem("filter_taken")
        s_tree = sem("kernel_tree_done")
        s_specw = sem("spectrum_staged")
        s_specs = sem("spectrum_stored")
        s_tap0 = sem("centre_tap")
        s_conv = sem("conv_done")
        s_store = [sem(f"stage_stored{i}") for i in range(2)]

        HY = 3 * HW // P
        PERW = WC // P
        rounds = [(h, o, eopart) for h in range(2) for o in range(ORDER) for eopart in range(2)]
        HALVES = 2 * len(rounds)
        halves = [[], [], [0], [1]] + [[2 * r, 2 * r + 1] for r in range(1, len(rounds))] + [[HALVES]]
        stored_after = [next(i for i in range(HY) if 4 * n + 4 in halves[i]) - 1 for n in range(len(rounds) // 2)]

        def spectra_after(i):
            return halves[i][-1] // 2 if halves[i] else 0

        def taken(i):
            m = spectra_after(i)
            return 2 * DT + 2 * (i + 1) + 4 * m + (m + 1) // 2

        with nc.Block() as block:
            @block.sync
            def _(sp):
                sp.dma_start(ident[:], dram["c_ident"]).then_inc(s_small, 16)
                sp.dma_start(lnw[:], dram["l_ln_mix"]).then_inc(s_small, 16)
                for t in range(TT):
                    sp.dma_start(x_sb[:, t, :], dram["x"][0, P * t:P * t + P, :]).then_inc(s_x[t], 16)
                sp.dma_start(zT, dram["c_z"]).then_inc(s_filt, 16)
                sp.dma_start(fw1[:], dram["hy_f_w1"][0]).then_inc(s_filt, 16)
                sp.dma_start(fw2[:], dram["hy_f_w2"][0]).then_inc(s_filt, 16)
                sp.dma_start(fcol[:], dram["l_filter"]).then_inc(s_filt, 16)
                sp.dma_start(w3[:], dram["hy_f_w3"][0].rearrange("k (o d c) -> k o d c", o=ORDER, d=2)).then_inc(s_filt, 16)
                sp.dma_start(hbias[:], dram["hy_bias"]).then_inc(s_filt, 16)
                for i in range(HY_LOADS + WB):
                    if i >= WB:
                        sp.wait_ge(s_acc, PERW * (i - WB + 1))
                    c, n = (H0 + WC * i, WC) if i < HY_LOADS else ATT_LOADS[i - HY_LOADS]
                    sp.dma_start(w_sb[:, i % WB, :, 0:n], dram["w_in"][0, :, c:c + n].rearrange("(k p) n -> p k n", p=P)).then_inc(s_w[i % WB], 16)
                    if i == 0:
                        sp.dma_start(cw[:], dram["l_conv_w"]).then_inc(s_tab, 16)
                        sp.dma_start(cb[:], dram["l_conv_b"]).then_inc(s_tab, 16)
                        sp.dma_start(fwd[:], dram["c_fwd"].rearrange("p (g q c) -> p g q c", g=GROUPS, q=4)).then_inc(s_tab, 16)
                        sp.dma_start(decay[:], dram["c_decay"].rearrange("(a p) c -> p a c", p=P)).then_inc(s_decay, 16)

            @block.gpsimd
            def _(pool):
                for i in range(HY):
                    pool.wait_ge(s_ht, taken(i))
                    dst = scratch["hy"][i * P // HW, :, (i * P) % HW:(i * P) % HW + P].rearrange("(a p) c -> p a c", p=P)
                    pool.dma_start(dst, stage[:, i % 2, :].rearrange("p (a c) -> p a c", c=P)).then_inc(s_store[i % 2], 16)
                    if i in stored_after:
                        n = stored_after.index(i)
                        h, o, _ = rounds[2 * n]
                        pool.wait_ge(s_specw, n + 1)
                        pool.dma_start(scratch["spec"][o, h], spec[:]).then_inc(s_specs, 16)
                pool.wait_ge(s_store[0], 16 * (HY // 2))
                pool.wait_ge(s_store[1], 16 * (HY // 2))
                pool.wait_ge(s_specs, 16 * len(stored_after))

            @block.tensor
            def _(pe):
                pe.wait_ge(s_small, 32)
                for b in range(2 * DT):
                    dt, th = b % DT, b // DT
                    if b == DT:
                        pe.wait_ge(s_filt, 16 * 6)
                        for c in range(2):
                            pe.matmul(psB[0:FFN, c, :], fw1[:], zT[:, 512 * c:512 * c + 512], start=True, stop=True).then_inc(s_pre, 1)
                    if dt == 0:
                        pe.wait_ge(s_xs, 4 * th + 4)
                    if b >= 2:
                        pe.wait_ge(s_ht, b - 1)
                    for t in range(4):
                        m = pe.transpose(psA[:, b % 2, P * t:P * t + P], x_sb[:, 4 * th + t, P * dt:P * dt + P], ident[:])
                    m.then_inc(s_pt, 1)
                def gen(r, chunks):
                    h, o, part = rounds[r]
                    for c in chunks:
                        n = 4 * r + c
                        if n >= 2:
                            pe.wait_ge(s_genu, n - 1)
                        for a in (2 * c, 2 * c + 1):
                            m = pe.matmul(psB[:, n % 2, HALF * (a % 2):HALF * (a % 2) + HALF], hdn2[:, P * a:P * a + P],
                                          w3eo[:, part, o, HALF * h:HALF * h + HALF], start=True, stop=True)
                        m.then_inc(s_gen, 1)

                used = [2 * DT]

                def spectrum(r):
                    h, o, part = rounds[r]
                    pe.wait_ge(s_tree, r + 1)
                    Vr = V[:, r % 2]
                    for c in range(4):
                        pe.wait_ge(s_ht, used[0] - 1)
                        for g in (2 * c, 2 * c + 1):
                            dst = psA[:, used[0] % 2, HALF * (g % 2):HALF * (g % 2) + HALF]
                            for q in range(2):
                                m = pe.matmul(dst, fwd[:, g, 2 * part + q, :], Vr[:, 2 * g + q, :], start=(q == 0), stop=(q == 1))
                        m.then_inc(s_pt, 1)
                        used[0] += 1
                    if part == 0:
                        pe.wait_ge(s_ht, used[0] - 1)
                        pe.matmul(psA[0:1, used[0] % 2, 0:HALF], fwd[:, 0, 2, 0:1], Vr[:, 0, :], start=True, stop=True).then_inc(s_pt, 1)
                        used[0] += 1

                def transposes(i):
                    pe.wait_ge(s_conv, i + 1)
                    for c in range(2):
                        pe.wait_ge(s_ht, used[0] - 1)
                        for a in range(4):
                            t = 4 * c + a
                            m = pe.transpose(psA[:, used[0] % 2, P * a:P * a + P], tap[:, i % 2, P * t:P * t + P], ident[:])
                        m.then_inc(s_pt, 1)
                        used[0] += 1

                def second_layer():
                    pe.wait_ge(s_hdn, 1)
                    for c in range(2):
                        pe.matmul(psB[0:FFN, c, :], fw2[:], hdn1[:, 512 * c:512 * c + 512], start=True, stop=True).then_inc(s_pre, 1)

                def filter_rows():
                    pe.wait_ge(s_hdn, 2)
                    for o in range(ORDER):
                        pe.matmul(psB[0:1, o, :], hdn2[:, 0:1], w3[:, o, 0, :], start=True, stop=True).then_inc(s_row, 1)
                    pe.wait_ge(s_w3, 2)
                    pe.wait_ge(s_row0, 1)

                pe.wait_ge(s_ht, 2 * DT)
                for i in range(HY):
                    pe.wait_ge(s_w[i // PERW % WB], 16 * (i // PERW // WB + 1))
                    if i >= 2:
                        pe.wait_ge(s_conv, i - 1)
                    off = P * (i % PERW)
                    for c in range(2):
                        for k in range(DT):
                            m = pe.matmul(acc[:, i % 2, 512 * c:512 * c + 512], w_sb[:, i // PERW % WB, k, off:off + P],
                                          hT[:, k, 512 * c:512 * c + 512], start=(k == 0), stop=(k == DT - 1))
                    m.then_inc(s_acc, 1)
                    if i == 0:
                        second_layer()
                        pe.wait_ge(s_tab, 16 * 3)
                    else:
                        transposes(i - 1)
                    if i == 1:
                        filter_rows()
                    for q in halves[i]:
                        if q % 2 == 0 and q:
                            spectrum(q // 2 - 1)
                        if q < HALVES:
                            gen(q // 2, (0, 1) if q % 2 == 0 else (2, 3))
                transposes(HY - 1)

            @block.vector
            def _(dve):

                def reduce_arg(layer):
                    for c in range(2):
                        dve.wait_ge(s_pre, 2 * layer + c + 1)
                        dve.tensor_scalar(arg[:, 512 * c:512 * c + 512], psB[0:FFN, c, :], fcol[:, 2 * layer:2 * layer + 1],
                                                   fcol[:, 2 * layer + 1:2 * layer + 2], ALU.add, ALU.mult).then_inc(own_dve, one(own_dve))
                    dve.wait_ge(own_dve, so_far(own_dve))
                    big = 1.5 * 2.0 ** 23
                    dve.tensor_scalar(red[:], arg[:], 1.0 / (2 * math.pi), big, ALU.mult, ALU.add).then_inc(own_dve, one(own_dve))
                    dve.wait_ge(own_dve, so_far(own_dve))
                    dve.tensor_scalar(red[:], red[:], big, None, ALU.subtract).then_inc(own_dve, one(own_dve))
                    dve.wait_ge(own_dve, so_far(own_dve))
                    two_pi_hi = 6.28125
                    for part in (two_pi_hi, 2 * math.pi - two_pi_hi):
                        dve.scalar_tensor_tensor(out=arg[:], in0=red[:], scalar=-part, in1=arg[:], op0=ALU.mult, op1=ALU.add).then_inc(own_dve, one(own_dve))
                        dve.wait_ge(own_dve, so_far(own_dve))
                    edge = float(np.nextafter(np.float32(math.pi), np.float32(0)))
                    dve.tensor_scalar(arg[:], arg[:], edge, -edge, ALU.min, ALU.max).then_inc(s_arg, one(s_arg))

                for half in range(2):
                    a, b = TT // 2 * half, TT // 2 * (half + 1)
                    dve.wait_ge(s_ssq, b)
                    dve.tensor_scalar(rstd[:, 0, a:b], ssq[:, a:b], 1.0 / D, EPS, ALU.mult, ALU.add).then_inc(s_var, one(s_var))
                    dve.wait_ge(s_root, half + 1)
                    dve.reciprocal(rstd[:, 2, a:b], rstd[:, 1, a:b]).then_inc(own_dve, one(own_dve))
                    newton(dve, own_dve, one, so_far, rstd[:, :, a:b])
                    for t in range(a, b):
                        dve.tensor_scalar(x_sb[:, t, :], x_sb[:, t, :], rstd[:, 2, t:t + 1], None, ALU.mult).then_inc(s_xs, one(s_xs))
                dve.wait_ge(s_filt, 16 * 6)
                reduce_arg(0)
                for part, op in ((0, ALU.add), (1, ALU.subtract)):
                    dve.tensor_tensor(w3eo[:, part], w3[:, :, 0, :], w3[:, :, 1, :], op).then_inc(s_w3, one(s_w3))

                def conv(i):
                    dve.wait_ge(s_tap0, i + 1)
                    t, a = tap[:, i % 2, :], acc[:, i % 2, :]
                    dve.scalar_tensor_tensor(out=t[:, 1:L], in0=a[:, 0:L - 1], scalar=cw[:, 0, i:i + 1], in1=t[:, 1:L],
                                                      op0=ALU.mult, op1=ALU.add).then_inc(own_dve, one(own_dve))
                    dve.wait_ge(own_dve, so_far(own_dve))
                    dve.scalar_tensor_tensor(out=t[:, 0:L - 1], in0=a[:, 1:L], scalar=cw[:, 2, i:i + 1], in1=t[:, 0:L - 1],
                                                        op0=ALU.mult, op1=ALU.add).then_inc(s_conv, one(s_conv))

                def take(r, chunks):
                    h, o, part = rounds[r]
                    dve.wait_ge(s_decay, 16)
                    if so_far(s_conv):
                        dve.wait_ge(s_conv, so_far(s_conv))
                    if so_far(s_tree):
                        dve.wait_ge(s_tree, so_far(s_tree))
                    if so_far(s_genu):
                        dve.wait_ge(s_genu, so_far(s_genu))
                    for c in chunks:
                        dve.wait_ge(s_gen, 4 * r + c + 1)
                        dve.tensor_tensor(eo[:, 2 * c:2 * c + 2, :], psB[:, (4 * r + c) % 2, :].rearrange("p (a c) -> p a c", a=2),
                                                     decay[:, 2 * c:2 * c + 2, HALF * h:HALF * h + HALF], ALU.mult).then_inc(s_genu, one(s_genu))

                for i in range(HY):
                    conv(i)
                    if i == 0:
                        reduce_arg(1)
                    if i == 1:
                        dve.wait_ge(s_row, 2)
                        dve.tensor_tensor(row0[:], psB[0:1, :, :], hbias[:], ALU.add).then_inc(s_row0, one(s_row0))
                    for q in halves[i]:
                        if q == HALVES:
                            break
                        r = q // 2
                        h, o, part = rounds[r]
                        if q % 2 == 0:
                            take(r, (0, 1))
                            continue
                        take(r, (2, 3))
                        dve.wait_ge(s_genu, so_far(s_genu))
                        if part == 0:
                            dve.tensor_copy(eo[0:1, 0, :], row0[0:1, o, HALF * h:HALF * h + HALF]).then_inc(own_dve, one(own_dve))
                            dve.wait_ge(own_dve, so_far(own_dve))
                        forward_tree(dve, own_dve, one, so_far, eo[:], V[:, r % 2], T[:], s_tree)

            @block.scalar
            def _(act):
                for t in range(TT):
                    act.wait_ge(s_x[t], 16)
                    if so_far(s_ssq):
                        act.wait_ge(s_ssq, so_far(s_ssq))
                    act.activation(acc[:, 0, :], x_sb[:, t, :], ACT.Square, accum_out=ssq[:, t:t + 1]).then_inc(s_ssq, one(s_ssq))
                    if (t + 1) % (TT // 2) == 0:
                        act.wait_ge(s_var, (t + 1) // (TT // 2))
                        act.activation(rstd[:, 1, t + 1 - TT // 2:t + 1], rstd[:, 0, t + 1 - TT // 2:t + 1], ACT.Sqrt).then_inc(s_root, 1)
                used = [0]

                def take(dst, src, **kw):
                    act.wait_ge(s_pt, used[0] + 1)
                    used[0] += 1
                    act.activation(dst, src, ACT.Identity, **kw).then_inc(s_ht, one(s_ht))

                act.wait_ge(s_small, 32)
                for b in range(2 * DT):
                    dt, th = b % DT, b // DT
                    take(hT[:, dt, 512 * th:512 * th + 512], psA[:, b % 2, :], scale=lnw[:, dt:dt + 1])
                act.wait_ge(s_arg, 1)
                act.activation(hdn1[:], arg[:], ACT.Sin).then_inc(s_hdn, 1)
                act.wait_ge(s_tab, 16 * 3)

                def spectrum(r):
                    h, o, part = rounds[r]
                    if part == 0 and r >= 2:
                        act.wait_ge(s_specs, 16 * (r // 2))
                    for c in range(4):
                        take(spec[:, 2 * c:2 * c + 2, part, :], psA[:, used[0] % 2, :].rearrange("p (g c) -> p g c", g=2))
                    if part == 0:
                        take(nyq[:], psA[0:1, used[0] % 2, 0:HALF])
                    else:
                        act.wait_ge(s_ht, so_far(s_ht))
                        act.activation(spec[0:1, 0, 1, :], nyq[:], ACT.Identity).then_inc(s_specw, one(s_specw))

                def stage_free(i):
                    if i >= 2:
                        act.wait_ge(s_store[i % 2], 16 * (i // 2))

                def stage_tile(i):
                    stage_free(i)
                    for c in range(2):
                        take(stage[:, i % 2, 512 * c:512 * c + 512], psA[:, used[0] % 2, :])

                for i in range(HY):
                    act.wait_ge(s_acc, i + 1)
                    act.activation(tap[:, i % 2, :], acc[:, i % 2, :], ACT.Identity, scale=cw[:, 1, i:i + 1],
                                   bias=cb[:, i:i + 1]).then_inc(s_tap0, one(s_tap0))
                    if i == 0:
                        act.wait_ge(s_arg, 2)
                        act.activation(hdn2[:], arg[:], ACT.Sin).then_inc(s_hdn, 1)
                    else:
                        stage_tile(i - 1)
                    for q in halves[i]:
                        if q % 2 == 0 and q:
                            spectrum(q // 2 - 1)
                stage_tile(HY - 1)


def inverse_tree(dve, own, one, so_far, Z, Y, X, T, done):
    add, sub, mul = ALU.add, ALU.subtract, ALU.mult
    tt, stt = dve.tensor_tensor, dve.scalar_tensor_tensor
    G, Cc, Bh, Dd, dq, m, pp, x1, x3, w = (T[:, 2 * i:2 * i + 2, :] for i in range(10))
    tt(G, Z[:, 8:10, :], Z[:, 10:12, :], add).then_inc(own, one(own))
    tt(Cc, Z[:, 8:10, :], Z[:, 10:12, :], sub).then_inc(own, one(own))
    tt(Bh, Z[:, 12:14, :], Z[:, 14:16, :], add).then_inc(own, one(own))
    tt(Dd, Z[:, 13:15, :], Z[:, 15:11:-3, :], sub).then_inc(own, one(own))
    tt(dq, Z[:, 4:6, :], Z[:, 6:8, :], add).then_inc(own, one(own))
    tt(m, Z[:, 4:6, :], Z[:, 6:8, :], sub).then_inc(own, one(own))
    tt(pp[:, 0, :], Z[:, 0, :], Z[:, 1, :], add).then_inc(own, one(own))
    tt(pp[:, 1, :], Z[:, 0, :], Z[:, 1, :], sub).then_inc(own, one(own))
    dve.wait_ge(own, so_far(own))
    tt(x1, Cc, Dd, add).then_inc(own, one(own))
    tt(x3, Cc, Dd, sub).then_inc(own, one(own))
    tt(w, G, Bh, add).then_inc(own, one(own))
    tt(Y[:, 0:3:2, :], pp, Z[:, 2:4, :], add).then_inc(own, one(own))
    tt(Y[:, 4:7:2, :], pp, Z[:, 2:4, :], sub).then_inc(own, one(own))
    dve.wait_ge(own, so_far(own))
    tt(Cc, G, Bh, sub).then_inc(own, one(own))
    tt(Dd[:, 0, :], m[:, 0, :], m[:, 1, :], add).then_inc(own, one(own))
    tt(Dd[:, 1, :], m[:, 1, :], m[:, 0, :], sub).then_inc(own, one(own))
    stt(out=Y[:, 1, :], in0=x1[:, 1, :], scalar=T22, in1=x1[:, 0, :], op0=mul, op1=add).then_inc(own, one(own))
    stt(out=Y[:, 5, :], in0=x1[:, 0, :], scalar=-T22, in1=x1[:, 1, :], op0=mul, op1=add).then_inc(own, one(own))
    stt(out=Y[:, 3, :], in0=x3[:, 0, :], scalar=T22, in1=x3[:, 1, :], op0=mul, op1=add).then_inc(own, one(own))
    stt(out=Y[:, 7, :], in0=x3[:, 1, :], scalar=T22, in1=x3[:, 0, :], op0=mul, op1=sub).then_inc(own, one(own))
    dve.wait_ge(own, so_far(own))
    stt(out=dq[:, 1, :], in0=Cc[:, 0, :], scalar=C45, in1=dq[:, 1, :], op0=mul, op1=add).then_inc(own, one(own))
    stt(out=Y[:, 4, :], in0=Cc[:, 1, :], scalar=C45, in1=Y[:, 4, :], op0=mul, op1=add).then_inc(own, one(own))
    s13 = Y[:, 2:7:4, :]
    stt(out=G, in0=Dd, scalar=C45, in1=s13, op0=mul, op1=add).then_inc(own, one(own))
    stt(out=Bh, in0=Dd, scalar=-C45, in1=s13, op0=mul, op1=add).then_inc(own, one(own))
    dve.wait_ge(own, so_far(own))
    s02 = Y[:, 0:5:4, :]
    tt(m, s02, dq, add).then_inc(own, one(own))
    tt(pp, s02, dq, sub).then_inc(own, one(own))
    stt(out=Y[:, 1:4:2, :], in0=Y[:, 1:4:2, :], scalar=C22, in1=G, op0=mul, op1=add).then_inc(own, one(own))
    stt(out=Y[:, 5:8:2, :], in0=Y[:, 5:8:2, :], scalar=C22, in1=Bh, op0=mul, op1=add).then_inc(own, one(own))
    dve.wait_ge(own, so_far(own))
    tt(Y[:, 0:5:4, :], T[:, 10:13:2, :], w, add).then_inc(own, one(own))
    tt(Y[:, 2:7:4, :], T[:, 11:14:2, :], X[:, 2:7:4, :], mul).then_inc(own, one(own))
    tt(Y[:, 1:8:2, :], Y[:, 1:8:2, :], X[:, 1:8:2, :], mul).then_inc(own, one(own))
    dve.wait_ge(own, so_far(own))
    tt(Y[:, 0:5:4, :], Y[:, 0:5:4, :], X[:, 0:5:4, :], mul).then_inc(done, one(done))


def hyena_stage(nc, dram, scratch, own, hT, w_sb, w_loaded, mix):
    own_dve, own_act, one, so_far = own
    R = 2 * ORDER
    tiles = [("code", 0, C0, 2 * RANK)] + [("qk", j, Q0 + P * j, P) for j in range(2 * QK // P)]
    tiles += [("vg", (c, th), V0 + WC * c, WC) for c in range(2 * GW // WC) for th in range(2)]
    loads = ATT_LOADS
    load_of = [next(i for i, (c, n) in enumerate(loads) if c <= t[2] < c + n) for t in tiles]
    after_round = [2, 5, 8, 11, len(tiles)]
    with ExitStack() as ctx:
        sb = lambda name, shape, dt=F32: ctx.enter_context(nc.sbuf_tensor(name, shape, dt))
        sem = lambda name: ctx.enter_context(nc.semaphore(name))
        fwd = sb("m_fwd", [P, GROUPS, 4, P])
        inv = sb("m_inv", [P, GROUPS, 4, P])
        z = mix[:, :, GW:D]
        V = sb("m_V", [P, 2 * GROUPS, HALF])
        T = sb("m_T", [P, 20, HALF])
        K = sb("m_K", [P, GROUPS, 2, HALF])
        gate = sb("m_gate", [P, TT, HALF])
        M = sb("m_M", [P, 2, 2, HALF])
        Y = sb("m_Y", [P, 2, 2, HALF])
        stage = sb("m_stage", [P, 2, L])
        psU = ctx.enter_context(nc.psum_tensor("psU", [P, 2, 512], F32))
        psZ = ctx.enter_context(nc.psum_tensor("psZ", [P, 2, 512], F32))
        acc = ctx.enter_context(nc.psum_tensor("m_acc", [P, 2, L], F32))

        s_tab, s_inv = sem("m_forward_table"), sem("m_inverse_table")
        s_z = [sem(f"m_z_loaded{h}") for h in range(2)]
        s_K = sem("m_K_loaded")
        s_gate = sem("m_gate_loaded")
        s_w = [sem(f"m_w_loaded{i}") for i in range(2)]
        s_tree = sem("m_tree_done")
        s_u = sem("m_data_spectrum")
        s_mult = sem("m_spectrum_taken")
        s_y = sem("m_product_ready")
        s_zf = sem("m_inverse_product")
        s_zt = sem("m_inverse_taken")
        s_gated = sem("m_round_done")
        s_acc, s_stage = sem("m_tile_product"), sem("m_tile_staged")
        s_store = [sem(f"m_tile_stored{i}") for i in range(2)]

        with nc.Block() as block:
            @block.sync
            def _(sp):
                def half_load(h):
                    sp.dma_start(mix[:, :, GW + HALF * h:GW + HALF * h + HALF],
                                 scratch["hy"][0, :, HALF * h:HALF * h + HALF].rearrange("(a p) c -> p a c", p=P)).then_inc(s_z[h], 16)

                half_load(0)
                sp.dma_start(fwd[:], dram["c_fwd"].rearrange("p (g q c) -> p g q c", g=GROUPS, q=4)).then_inc(s_tab, 16)
                for r in range(R):
                    o, h = r // 2, r % 2
                    if r:
                        sp.wait_ge(s_y, 8 * r)
                    sp.dma_start(K[:], scratch["spec"][o, h]).then_inc(s_K, 16)
                    if r == 0:
                        sp.dma_start(inv[:], dram["c_inv"].rearrange("p (g q c) -> p g q c", g=GROUPS, q=4)).then_inc(s_inv, 16)
                    else:
                        sp.wait_ge(s_gated, r)
                    sp.dma_start(gate[:], scratch["hy"][1 + o, :, HALF * h:HALF * h + HALF].rearrange("(a p) c -> p a c", p=P)).then_inc(s_gate, 16)
                    if r == 0:
                        half_load(1)

            @block.gpsimd
            def _(pool):
                def load(i):
                    c, n = loads[i]
                    pool.dma_start(w_sb[:, i % 2, :, 0:n], dram["w_in"][0, :, c:c + n].rearrange("(k p) n -> p k n", p=P)).then_inc(s_w[i % 2], 16)

                for i, (kind, j, col, n) in enumerate(tiles):
                    pool.wait_ge(s_stage, i + 1)
                    src = stage[:, i % 2, :]
                    if kind == "code":
                        dst, src = scratch["code"][:], stage[0:2 * RANK, i % 2, :]
                    elif kind == "qk":
                        dst = scratch["qk"][j]
                    else:
                        c, th = j
                        dst = scratch["vg"][c // 2, 512 * th:512 * th + 512, WC * (c % 2):WC * (c % 2) + WC].rearrange("(a p) c -> p a c", p=P)
                        src = src.rearrange("p (a c) -> p a c", c=WC)
                    if i + 1 < len(tiles) and load_of[i + 1] != load_of[i] and load_of[i] + 2 < len(loads):
                        load(load_of[i] + 2)
                    pool.dma_start(dst, src).then_inc(s_store[i % 2], 16)
                pool.wait_ge(s_store[0], 16 * ((len(tiles) + 1) // 2))
                pool.wait_ge(s_store[1], 16 * (len(tiles) // 2))

            @block.tensor
            def _(pe):
                def product(i):
                    kind, j, col, n = tiles[i]
                    g = load_of[i]
                    w, off = w_sb[:, g % 2], col - loads[g][0]
                    if g < WB:
                        pe.wait_ge(w_loaded[g], 16 * (HY_LOADS // WB + 1))
                    else:
                        pe.wait_ge(s_w[g % 2], 16 * (g // 2))
                    if i >= 2:
                        pe.wait_ge(s_stage, i - 1)
                    if kind == "vg":
                        for tt in range(4):
                            tok = 4 * j[1] + tt
                            for k in range(DT):
                                m = pe.matmul(acc[:, i % 2, WC * tt:WC * tt + WC], hT[:, k, P * tok:P * tok + P], w[:, k, :],
                                              start=(k == 0), stop=(k == DT - 1))
                    else:
                        for c in range(2):
                            for k in range(DT):
                                m = pe.matmul(acc[0:n, i % 2, 512 * c:512 * c + 512], w[:, k, off:off + n],
                                              hT[:, k, 512 * c:512 * c + 512], start=(k == 0), stop=(k == DT - 1))
                    m.then_inc(s_acc, 1)

                def hyena(r):
                    pe.wait_ge(s_tree, r + 1)
                    for i in range(GROUPS + 2):
                        if i < GROUPS:
                            n = GROUPS * r + i
                            if n >= 2:
                                pe.wait_ge(s_mult, n - 1)
                            for part in range(2):
                                for slot in range(2):
                                    mm = pe.matmul(psU[:, n % 2, HALF * part:HALF * part + HALF], fwd[:, i, 2 * part + slot, :],
                                                   V[:, 2 * i + slot, :], start=(slot == 0), stop=(slot == 1))
                            mm.then_inc(s_u, 1)
                        if i >= 2:
                            gi, n = i - 2, GROUPS * r + i - 2
                            pe.wait_ge(s_y, n + 1)
                            if n >= 2:
                                pe.wait_ge(s_zt, n - 1)
                            for slot in range(2):
                                for part in range(2):
                                    mm = pe.matmul(psZ[:, n % 2, HALF * slot:HALF * slot + HALF], inv[:, gi, 2 * part + slot, :],
                                                   Y[:, n % 2, part, :], start=(part == 0), stop=(part == 1))
                            mm.then_inc(s_zf, 1)

                for i in range(after_round[0]):
                    product(i)
                pe.wait_ge(s_tab, 16)
                pe.wait_ge(s_inv, 16)
                for r in range(R):
                    hyena(r)
                    for i in range(after_round[r], after_round[r + 1]):
                        product(i)

            @block.vector
            def _(dve):
                def products(r):
                    dve.wait_ge(s_K, 16 * (r + 1))
                    for i in range(GROUPS):
                        n = GROUPS * r + i
                        dve.wait_ge(s_u, n + 1)
                        U = psU[:, n % 2, :].rearrange("p (a c) -> p a c", a=2)
                        if so_far(s_tree):
                            dve.wait_ge(s_tree, so_far(s_tree))
                        if so_far(s_y):
                            dve.wait_ge(s_y, so_far(s_y))
                        dve.tensor_tensor(M[:, 0], U, K[:, i], ALU.mult).then_inc(own_dve, one(own_dve))
                        dve.tensor_tensor(M[:, 1], U, K[:, i, ::-1, :], ALU.mult).then_inc(s_mult, one(s_mult))
                        if n >= 2:
                            dve.wait_ge(s_zf, n - 1)
                        dve.wait_ge(s_mult, so_far(s_mult))
                        dve.tensor_tensor(Y[:, n % 2, 0, :], M[:, 0, 0, :], M[:, 0, 1, :], ALU.subtract).then_inc(own_dve, one(own_dve))
                        last = dve.tensor_tensor(Y[:, n % 2, 1, :], M[:, 1, 0, :], M[:, 1, 1, :], ALU.add)
                        if i == 0:
                            last.then_inc(own_dve, one(own_dve))
                            dve.wait_ge(own_dve, so_far(own_dve))
                            last = dve.tensor_copy(Y[0:1, n % 2], M[0:1, 0])
                        last.then_inc(s_y, one(s_y))

                def forward(r):
                    if r < 2:
                        dve.wait_ge(s_z[r], 16)
                    else:
                        dve.wait_ge(s_gated, r - 1)
                    if r:
                        dve.wait_ge(s_gated, so_far(s_gated))
                    forward_tree(dve, own_dve, one, so_far, z[:, :, HALF * (r % 2):HALF * (r % 2) + HALF], V[:], T[:], s_tree)

                def inverse(r):
                    dve.wait_ge(s_zt, GROUPS * (r + 1))
                    dve.wait_ge(s_gate, 16 * (r + 1))
                    dve.wait_ge(s_tree, so_far(s_tree))
                    inverse_tree(dve, own_dve, one, so_far, V[:], z[:, :, HALF * (r % 2):HALF * (r % 2) + HALF], gate[:], T[:], s_gated)

                forward(0)
                for r in range(R):
                    products(r)
                    inverse(r)
                    if r + 1 < R:
                        forward(r + 1)

            @block.scalar
            def _(act):
                def inverse(r):
                    for i in range(GROUPS):
                        n = GROUPS * r + i
                        act.wait_ge(s_zf, n + 1)
                        act.activation(V[:, 2 * i:2 * i + 2, :], psZ[:, n % 2, :].rearrange("p (a c) -> p a c", a=2), ACT.Identity).then_inc(s_zt, one(s_zt))

                def take_tile(i):
                    kind, _, col, n = tiles[i]
                    act.wait_ge(s_acc, i + 1)
                    if i >= 2:
                        act.wait_ge(s_store[i % 2], 16 * (i // 2))
                    scale = DK ** -0.5 if kind == "qk" and col < K0 else 1.0
                    rows = min(n, P)
                    act.activation(stage[0:rows, i % 2, :], acc[0:rows, i % 2, :], ACT.Identity, scale=scale).then_inc(s_stage, one(s_stage))

                for i in range(after_round[0]):
                    take_tile(i)
                for r in range(R):
                    inverse(r)
                    for i in range(after_round[r], after_round[r + 1]):
                        take_tile(i)


def attention_stage(nc, dram, scratch, own, mix, w_out, w_out_loaded):
    own_dve, own_act, one, so_far = own
    CH = 64
    NCH = L // CH
    R = 4
    with ExitStack() as ctx:
        sb = lambda name, shape, dt=F32: ctx.enter_context(nc.sbuf_tensor(name, shape, dt))
        ps = lambda name: ctx.enter_context(nc.psum_tensor(name, [P, 4, 512], F32))
        sem = lambda name: ctx.enter_context(nc.semaphore(name))
        ident = sb("m_ident", [P, P])
        q = sb("m_q", [P, 2, L])
        k = sb("m_k", [P, 2, L])
        v = sb("m_v", [P, 2, TT, 2 * DV])
        g = sb("m_g", [P, TT, 2 * DV])
        code = sb("m_code", [2 * RANK, L])
        wa = sb("m_wa", [2 * RANK, 2, QK])
        ba = sb("m_ba", [P, 2, 2])
        qd, ki = ([sb(f"m_{name}{i}", [P, L]) for i in range(R)] for name in ("qd", "ki"))
        logs_df = [[sb(f"m_{name}{i}", [P, L])[:] for name in ("b", "df")] for i in range(2)]
        starts = sb("m_starts", [P, L], mybir.dt.uint8)
        dec = sb("m_dec", [P, R, NCH])
        kT = sb("m_kT", [P, TT, P])
        S = sb("m_S", [P, R, NCH, DV])
        mask = sb("m_mask", [P, 2, P], I32)
        sc = sb("m_sc", [P, 2, 2, P])
        nw = sb("m_nw", [P, DV])
        rs = sb("m_rs", [P, 4, 2 * TT])
        psG, psS = ps("psG"), ps("psS")

        s_id = sem("m_identity")
        s_gl = sem("m_gla_constants")
        s_qk = sem("m_qk_loaded")
        s_vg, s_g = sem("m_v_loaded"), sem("m_g_loaded")
        s_gf = sem("m_psG_filled")
        s_gt = sem("m_psG_taken")
        s_gx = sem("m_logs_ready")
        s_b = sem("m_cumsum_ready")
        s_df = sem("m_chunk_rest_ready")
        s_ex = sem("m_exps_ready")
        s_qd = sem("m_decayed_ready")
        s_S = sem("m_states_ready")
        s_sf = sem("m_scores_filled")
        s_sm = sem("m_scores_masked")
        s_zero = sem("m_scores_zeroed")
        s_ss = sem("m_head_variance")
        s_rt = sem("m_head_root")
        s_sg = sem("m_silu_ready")
        s_gn = sem("m_silu_times_norm")
        s_on = sem("m_heads_done")
        chunk_fills = [2, 6, 10, 13]
        head_fills = [16, 16 + TT]

        with nc.Block() as block:
            @block.sync
            def _(sp):
                sp.dma_start(code[:], scratch["code"]).then_inc(s_gl, 16)
                sp.wait_ge(s_zero, 1)
                sp.dma_start(wa[0:RANK, 0, :], dram["gla_wa_f"][0]).then_inc(s_gl, 16)
                sp.dma_start(wa[RANK:2 * RANK, 1, :], dram["gla_wa_b"][0]).then_inc(s_gl, 16)
                sp.dma_start(ba[:], dram["l_gate_b"]).then_inc(s_gl, 16)
                sp.dma_start(mask[:], dram["c_mask"]).then_inc(s_gl, 16)
                sp.dma_start(nw[:], dram["gla_norm_w"][0].partition_broadcast(P)).then_inc(s_gl, 16)
                sp.dma_start(ident[:], dram["c_ident"]).then_inc(s_id, 16)
                for t, i in ((q, 0), (k, 2)):
                    sp.dma_start(t[:], scratch["qk"][i:i + 2].rearrange("h p l -> p h l")).then_inc(s_qk, 16)
                def heads(i, ht):
                    return scratch["vg"][i, :, 2 * DV * ht:2 * DV * ht + 2 * DV].rearrange("(a p) c -> p a c", p=P)

                for ht in range(2):
                    sp.dma_start(v[:, ht], heads(0, ht)).then_inc(s_vg, 16)
                sp.dma_start(g[:], heads(1, 0)).then_inc(s_g, 16)
                for c in range(2):
                    sp.dma_start(w_out[:, :, 512 * c:512 * c + 512],
                                 dram["w_out"][0, :, 512 * c:512 * c + 512].rearrange("(k p) n -> p k n", p=P)).then_inc(w_out_loaded[c], 16)
                sp.wait_ge(s_on, 1)
                sp.dma_start(g[:], heads(1, 1)).then_inc(s_g, 16)

            @block.gpsimd
            def _(pool):
                pool.memset(wa[:], 0.0).then_inc(s_zero, 1)
                pool.memset(sc[:], 0.0).then_inc(s_zero, 1)
                pool.memset(starts[:], 1).then_inc(s_zero, 1)
                pool.wait_ge(s_zero, 3)
                pool.memset(starts[:].rearrange("p (n c) -> p n c", c=CH)[:, :, 0:1], 0).then_inc(s_zero, 1)
                pool.wait_ge(s_gl, 16 * 6)
                for ht in range(2):
                    pool.wait_ge(s_sg, ht + 1)
                    gv = g[:].rearrange("p a (x d) -> p (a x) d", d=DV)
                    pool.tensor_tensor(gv, gv, nw[:].unsqueeze(1).to_broadcast([P, 2 * TT, DV]), ALU.mult).then_inc(s_gn, 1)

            @block.tensor
            def _(pe):
                fills = [0]

                def next_fill():
                    if fills[0] >= 2:
                        pe.wait_ge(s_gt, fills[0] - 1)
                    fills[0] += 1
                    half = (fills[0] - 1) % 2
                    return psG[:, 2 * half:2 * half + 2, :]

                def gate_logits(r):
                    ht, dr = r // 2, r % 2
                    bank = next_fill()
                    for c in range(2):
                        m = pe.matmul(bank[:, c, :], wa[:, dr, P * ht:P * ht + P], code[:, 512 * c:512 * c + 512], start=True, stop=True)
                    m.then_inc(s_gf, 1)

                def chunk_products(r):
                    ht, dr = r // 2, r % 2
                    df = logs_df[dr][1]
                    pe.wait_ge(s_qd, r + 1)
                    bank = next_fill()
                    for t in range(TT):
                        m = pe.transpose(bank[:, t // 4, P * (t % 4):P * (t % 4) + P], df[:, P * t:P * t + P], ident[:])
                    m.then_inc(s_gf, 1)
                    if dr == 0:
                        pe.wait_ge(s_vg, 32)
                    for batch in range(2):
                        bank = next_fill()
                        if batch == 0:
                            pe.wait_ge(s_gt, chunk_fills[r] + 1)
                        for i in range(8):
                            n = 8 * batch + i
                            rows = slice(CH * (n % 2), CH * (n % 2) + CH)
                            for hd in range(2):
                                m = pe.matmul(bank[CH * hd:CH * hd + CH, n % 2, DV * (i // 2):DV * (i // 2) + DV],
                                              kT[rows, n // 2, CH * hd:CH * hd + CH], v[rows, ht, n // 2, DV * hd:DV * hd + DV],
                                              start=True, stop=True)
                        m.then_inc(s_gf, 1)

                def scores(ht, t):
                    n = TT * ht + t
                    if n >= 2:
                        pe.wait_ge(s_sm, n - 1)
                    for hd in range(2):
                        rows = slice(DK * hd, DK * hd + DK)
                        for dr in range(2):
                            m = pe.matmul(psS[:, 2 * (t % 2) + hd, P * dr:P * dr + P], ki[2 * ht + dr][rows, P * t:P * t + P], qd[2 * ht + dr][rows, P * t:P * t + P],
                                          start=True, stop=True)
                    m.then_inc(s_sf, 1)

                def heads_out(ht):
                    pe.wait_ge(s_S, 2 * ht + 2)
                    scores(ht, 0)
                    for t in range(TT):
                        if t + 1 < TT:
                            scores(ht, t + 1)
                        pe.wait_ge(s_sm, TT * ht + t + 1)
                        bank = next_fill()
                        for hd in range(2):
                            rows = slice(DK * hd, DK * hd + DK)
                            m = pe.matmul(bank[:, hd, 0:DV], sc[:, t % 2, hd, :], v[:, ht, t, DV * hd:DV * hd + DV],
                                          start=True, stop=False, skip_group_check=True)
                            for c in range(2):
                                n = 2 * t + c
                                for dr, before in ((0, n - 1), (1, n + 1)):
                                    if 0 <= before < NCH:
                                        m = pe.matmul(bank[CH * c:CH * c + CH, hd, 0:DV], qd[2 * ht + dr][rows, CH * n:CH * n + CH],
                                                      S[rows, 2 * ht + dr, before, :], start=False, stop=False, skip_group_check=True)
                        m.then_inc(s_gf, 1)

                pe.wait_ge(s_gl, 16 * 6)
                gate_logits(0)
                gate_logits(1)
                pe.wait_ge(s_id, 16)
                chunk_products(0)
                gate_logits(2)
                chunk_products(1)
                gate_logits(3)
                chunk_products(2)
                chunk_products(3)
                heads_out(0)
                heads_out(1)

            @block.vector
            def _(dve):

                def cumulate(r):
                    dr = r % 2
                    gx, ab, (b, df) = qd[r][:], ki[r][:], logs_df[dr]
                    dve.wait_ge(s_gx, r + 1)
                    dve.scalar_tensor_tensor(out=gx, in0=gx, scalar=0.0, in1=ab, op0=ALU.min, op1=ALU.subtract).then_inc(own_dve, one(own_dve))
                    dve.wait_ge(own_dve, so_far(own_dve))
                    f = (lambda t: t) if dr == 0 else (lambda t: t[:, ::-1])
                    dve.tensor_tensor_scan(f(b), starts[:], f(gx), 0.0, ALU.mult, ALU.add).then_inc(s_b, one(s_b))
                    dve.wait_ge(s_b, so_far(s_b))
                    bc = b.rearrange("p (n c) -> p n c", c=CH)
                    end = bc[:, :, CH - 1:CH] if dr == 0 else bc[:, :, 0:1]
                    dve.tensor_tensor(df.rearrange("p (n c) -> p n c", c=CH), end.to_broadcast([P, NCH, CH]), bc, ALU.subtract).then_inc(s_df, one(s_df))

                def decayed(r):
                    dr = r % 2
                    gx, ab, (b, df) = qd[r][:], ki[r][:], logs_df[dr]
                    dve.wait_ge(s_ex, r + 1)
                    dve.wait_ge(s_qk, 32)
                    dve.tensor_tensor(gx, q[:, r // 2], gx, ALU.mult).then_inc(own_dve, one(own_dve))
                    dve.tensor_tensor(ab, k[:, r // 2], ab, ALU.mult).then_inc(own_dve, one(own_dve))
                    dve.tensor_tensor(df, k[:, r // 2], df, ALU.mult).then_inc(s_qd, one(s_qd))

                def states(r):
                    ht, dr = r // 2, r % 2
                    dve.wait_ge(s_gt, chunk_fills[r] + 3)
                    order = range(1, NCH - 1) if dr == 0 else range(NCH - 2, 0, -1)
                    for i, n in enumerate(order):
                        if so_far(s_qd):
                            dve.wait_ge(s_qd, so_far(s_qd))
                        if so_far(own_dve):
                            dve.wait_ge(own_dve, so_far(own_dve))
                        prev = n - 1 if dr == 0 else n + 1
                        ins = dve.scalar_tensor_tensor(out=S[:, r, n, :], in0=S[:, r, prev, :], scalar=dec[:, r, n:n + 1],
                                                       in1=S[:, r, n, :], op0=ALU.mult, op1=ALU.add)
                        if i == NCH - 3:
                            ins.then_inc(s_S, one(s_S))
                        else:
                            ins.then_inc(own_dve, one(own_dve))

                def causal(ht, ts):
                    for t in ts:
                        dve.wait_ge(s_sf, TT * ht + t + 1)
                        if t >= 2:
                            dve.wait_ge(s_gf, head_fills[ht] + t - 1)
                        elif t == 0:
                            dve.wait_ge(s_gl, 16 * 6)
                        for dr in range(2):
                            m = mask[:, dr, :].unsqueeze(1).to_broadcast([P, 2, P])
                            ins = dve.copy_predicated(sc[:, t % 2], m, psS[:, 2 * (t % 2):2 * (t % 2) + 2, P * dr:P * dr + P])
                            if dr == 0:
                                ins.then_inc(own_dve, one(own_dve))
                                dve.wait_ge(own_dve, so_far(own_dve))
                            else:
                                ins.then_inc(s_sm, one(s_sm))

                def of_heads(a):
                    return a.rearrange("p a (x d) -> p a x d", d=DV)

                def head_squares(ht):
                    o, nt = of_heads(mix[:, :, 2 * DV * ht:2 * DV * ht + 2 * DV]), of_heads(v[:, ht])
                    dve.wait_ge(s_gt, head_fills[ht] + TT)
                    dve.tensor_tensor(nt, o, o, ALU.mult).then_inc(own_dve, one(own_dve))
                    dve.wait_ge(own_dve, so_far(own_dve))
                    dve.tensor_reduce(rs[:, 3, :], nt.rearrange("p a x d -> p (a x) d"), AX_X, ALU.add).then_inc(own_dve, one(own_dve))
                    dve.wait_ge(own_dve, so_far(own_dve))
                    dve.tensor_scalar(rs[:, 0, :], rs[:, 3, :], 1.0 / DV, EPS, ALU.mult, ALU.add).then_inc(s_ss, one(s_ss))

                def head_norm(ht):
                    o, nt = of_heads(mix[:, :, 2 * DV * ht:2 * DV * ht + 2 * DV]), of_heads(v[:, ht])
                    dve.wait_ge(s_rt, ht + 1)
                    dve.reciprocal(rs[:, 2, :], rs[:, 1, :]).then_inc(own_dve, one(own_dve))
                    newton(dve, own_dve, one, so_far, rs)
                    per_head = rs[:, 2, :].rearrange("p (a x) -> p a x", x=2).unsqueeze(3).to_broadcast([P, TT, 2, DV])
                    dve.tensor_tensor(nt, o, per_head, ALU.mult).then_inc(own_dve, one(own_dve))
                    dve.wait_ge(s_gn, ht + 1)
                    dve.wait_ge(own_dve, so_far(own_dve))
                    dve.tensor_tensor(o, nt, of_heads(g[:]), ALU.mult).then_inc(s_on, one(s_on))

                dve.wait_ge(s_zero, 4)
                cumulate(0)
                cumulate(1)
                decayed(0)
                decayed(1)
                states(0)
                cumulate(2)
                decayed(2)
                states(1)
                cumulate(3)
                decayed(3)
                states(2)
                states(3)
                causal(0, range(TT))
                causal(1, (0,))
                head_squares(0)
                causal(1, (1, 2))
                head_norm(0)
                causal(1, range(3, TT))
                head_squares(1)
                head_norm(1)

            @block.scalar
            def _(act):
                taken = [0]
                act.wait_ge(s_gl, 16 * 6)

                def wait_fill():
                    taken[0] += 1
                    act.wait_ge(s_gf, taken[0])
                    half = (taken[0] - 1) % 2
                    return psG[:, 2 * half:2 * half + 2, :]

                def logs(r):
                    ht, dr = r // 2, r % 2
                    gx, ab, (b, df) = qd[r][:], ki[r][:], logs_df[dr]
                    bank = wait_fill()
                    if so_far(s_gt):
                        act.wait_ge(s_gt, so_far(s_gt))
                    if so_far(s_rt):
                        act.wait_ge(s_rt, so_far(s_rt))
                    act.activation(gx, bank, ACT.Identity, bias=ba[:, dr, ht:ht + 1]).then_inc(s_gt, one(s_gt))
                    act.wait_ge(s_gt, so_far(s_gt))
                    act.activation(ab, gx, ACT.Abs).then_inc(own_act, one(own_act))
                    act.wait_ge(own_act, so_far(own_act))
                    act.activation(ab, ab, ACT.Exp, scale=-1.0).then_inc(own_act, one(own_act))
                    act.wait_ge(own_act, so_far(own_act))
                    act.activation(ab, ab, ACT.Ln, bias=1.0).then_inc(s_gx, one(s_gx))

                def exps(r):
                    dr = r % 2
                    gx, ab, (b, df) = qd[r][:], ki[r][:], logs_df[dr]
                    act.wait_ge(s_b, r + 1)
                    end = b.rearrange("p (n c) -> p n c", c=CH)[:, :, (CH - 1) * (1 - dr)]
                    act.activation(dec[:, r, :], end, ACT.Exp, scale=1.0 / TAU).then_inc(own_act, one(own_act))
                    act.activation(gx, b, ACT.Exp, scale=1.0 / TAU).then_inc(own_act, one(own_act))
                    act.activation(ab, b, ACT.Exp, scale=-1.0 / TAU).then_inc(own_act, one(own_act))
                    act.wait_ge(s_df, r + 1)
                    act.activation(df, df, ACT.Exp, scale=1.0 / TAU).then_inc(s_ex, one(s_ex))

                def take_products(r):
                    dr = r % 2
                    bank = wait_fill()
                    act.activation(kT[:], bank.rearrange("p a (t c) -> p (a t) c", c=P), ACT.Identity).then_inc(s_gt, one(s_gt))
                    for batch in range(2):
                        bank = wait_fill()
                        for par in range(2):
                            ins = act.activation(S[:, r, 8 * batch + par:8 * batch + 8:2, :], bank[:, par, :].rearrange("p (i d) -> p i d", d=DV), ACT.Identity)
                            if par:
                                ins.then_inc(s_gt, one(s_gt))
                            else:
                                ins.then_inc(own_act, one(own_act))

                def take_heads(ht, ts):
                    for t in ts:
                        bank = wait_fill()
                        act.activation(mix[:, t, 2 * DV * ht:2 * DV * ht + 2 * DV].rearrange("p (x d) -> p x d", d=DV), bank[:, :, 0:DV],
                                       ACT.Identity).then_inc(s_gt, one(s_gt))

                def silu(ht):
                    act.wait_ge(s_g, 16 * (ht + 1))
                    act.activation(g[:], g[:], ACT.Silu).then_inc(s_sg, one(s_sg))

                def root(ht):
                    act.wait_ge(s_ss, ht + 1)
                    act.activation(rs[:, 1, :], rs[:, 0, :], ACT.Sqrt).then_inc(s_rt, one(s_rt))

                logs(0)
                logs(1)
                exps(0)
                exps(1)
                take_products(0)
                logs(2)
                exps(2)
                take_products(1)
                logs(3)
                exps(3)
                take_products(2)
                take_products(3)
                silu(0)
                take_heads(0, range(TT))
                take_heads(1, (0, 1))
                root(0)
                take_heads(1, range(2, TT - 1))
                silu(1)
                take_heads(1, (TT - 1,))
                root(1)


RING = 8
NGU, NDN = 16, 8
PER = NGU + NDN
SPLIT = 4


def load_piece(sp, dram, ring, piece_loaded, e, i):
    slot = ring[:, i % RING, :]
    if isinstance(e, int) and e == NE:
        src = dram["w_ple_gate"][0, 2 * P * i:2 * P * i + 2 * P, :].rearrange("(k p) c -> p k c", p=P)
        dst = slot.rearrange("p (k c) -> p k c", k=2)
    elif i < NGU:
        n, m, half = i // 4, (i // 2) % 2, i % 2
        w = dram[("w_gate_e", "w_up_e")[m]][0]
        src = w[bass.ds(e, 1), 512 * half:512 * half + 512, 512 * n:512 * n + 512].rearrange("o (k p) c -> (o p) k c", p=P)
        dst = slot.rearrange("p (k c) -> p k c", k=4)
    else:
        j = i - NGU
        src = dram["w_down_e"][0, bass.ds(e, 1), 2 * P * j:2 * P * j + 2 * P, :].rearrange("o (k p) c -> (o p) k c", p=P)
        dst = slot.rearrange("p (k c) -> p k c", k=2)
    sp.dma_start(dst, src).then_inc(piece_loaded[i % RING], 16)


def residual_stage(nc, dram, scratch, own, tile_loaded, loads_before, ring, piece_loaded, wh, wl, mix, s_w):
    own_dve, own_act, one, so_far = own
    with ExitStack() as ctx:
        sb = lambda name, shape, dt=F32: ctx.enter_context(nc.sbuf_tensor(name, shape, dt))
        ps = lambda name, n: ctx.enter_context(nc.psum_tensor(name, [P, n, 512], F32))
        sem = lambda name: ctx.enter_context(nc.semaphore(name))
        x = sb("o_x", [P, TT, D])
        mixh = sb("o_mixh", [P, 2, DT, P], F32R)
        mixl = sb("o_mixl", [P, 2, DT, P], F32R)
        h = sb("o_h", [P, 2, D])
        hT = sb("o_hT", [P, 2, DT, P])
        sq = sb("o_sq", [P, D])
        wr = sb("o_wr", [P, DT, NE])
        lnw = sb("o_lnw", [P, DT])
        ident = sb("o_ident", [P, P])
        ssq = sb("o_ssq", [P, TT])
        rs = sb("o_rs", [P, 4, TT])
        lg = sb("o_lg", [P, TT, NE])
        ex = sb("o_ex", [P, TT, NE])
        st = sb("o_st", [P, 4, TT])
        pr = sb("o_pr", [P, TT, NE])
        prc = sb("o_prc", [P, NE, TT])
        pT = sb("o_pT", [NE, L])
        psT, psO, psH, psR = ps("o_psT", 2), ps("o_psO", 3), ps("o_psH", 2), ps("o_psR", 1)

        s_c, s_wr = sem("o_constants"), sem("o_router_loaded")
        x_loaded = loads_before + 16
        s_wh, s_wl = sem("o_wh_ready"), sem("o_wl_ready")
        s_tf, s_th, s_tl = sem("o_mixT_filled"), sem("o_mixh_ready"), sem("o_mixl_ready")
        s_of, s_ot = sem("o_product"), sem("o_residual_added")
        s_sq, s_var, s_rt = sem("o_squares"), sem("o_variance"), sem("o_root")
        s_h = sem("o_normed")
        s_hf, s_hT = sem("o_hT_filled"), sem("o_hT_taken")
        s_lg = sem("o_logits")
        s_sub, s_ex = sem("o_logits_less_max"), sem("o_exps")
        s_pr, s_pf, s_pT = sem("o_probs"), sem("o_probs_transposed"), sem("o_probs_by_row")
        s_sth = [sem(f"o_h_stored{i}") for i in range(2)]
        s_str, s_stp = sem("o_r_stored"), sem("o_probs_stored")

        with nc.Block() as block:
            @block.sync
            def _(sp):
                sp.dma_start(ident[:], dram["c_ident"]).then_inc(s_c, 16)
                sp.dma_start(lnw[:], dram["l_ln_ffn"]).then_inc(s_c, 16)
                for t in range(TT):
                    sp.dma_start(x[:, t, :], dram["x"][0, P * t:P * t + P, :]).then_inc(tile_loaded[t], 16)
                    if t == 0:
                        sp.dma_start(wr[:], dram["w_router"][0].rearrange("(k p) n -> p k n", p=P)).then_inc(s_wr, 16)
                for i in range(RING):
                    if i == 0:
                        sp.wait_ge(s_wl, SPLIT)
                    if i == SPLIT:
                        sp.wait_ge(s_tf, 2 * TT)
                    load_piece(sp, dram, ring, piece_loaded, 0, i)
                sp.wait_ge(s_pr, 2)
                sp.dma_start(scratch["pcol"].rearrange("e p t -> p e t"), prc[:]).then_inc(s_stp, 16)
                sp.wait_ge(s_pT, 1)
                sp.dma_start(scratch["prow"], pT[:]).then_inc(s_stp, 16)
                sp.wait_ge(s_stp, 32)

            @block.gpsimd
            def _(pool):
                for t in range(TT):
                    pool.wait_ge(s_ot, 2 * t + 2)
                    pool.dma_start(scratch["r"][P * t:P * t + P, :], x[:, t, :]).then_inc(s_str, 16)
                    pool.wait_ge(s_h, t + 1)
                    pool.dma_start(scratch["h2"][P * t:P * t + P, :], h[:, t % 2, :]).then_inc(s_sth[t % 2], 16)
                pool.wait_ge(s_str, 16 * TT)
                for i in range(2):
                    pool.wait_ge(s_sth[i], 16 * TT // 2)

            @block.tensor
            def _(pe):
                pe.wait_ge(s_c, 32)
                fills = [0]

                def mix_transposes(t):
                    for c in range(2):
                        if fills[0] >= 2:
                            pe.wait_ge(s_tl, fills[0] - 1)
                        for i in range(4):
                            k = 4 * c + i
                            m = pe.transpose(psT[:, c, P * i:P * i + P], mix[:, t, P * k:P * k + P], ident[:])
                        m.then_inc(s_tf, 1)
                        fills[0] += 1

                def product(t):
                    pe.wait_ge(s_tl, 2 * t + 2)
                    for c in range(2):
                        n = 2 * t + c
                        if n >= 3:
                            pe.wait_ge(s_ot, n - 2)
                        for k in range(DT):
                            if n == 0 and k % 2 == 0:
                                pe.wait_ge(s_wl, k // 2 + 1)
                            cols = slice(D * (k % 2) + 512 * c, D * (k % 2) + 512 * c + 512)
                            for j, (a, b) in enumerate(((mixh, wh), (mixl, wh), (mixh, wl))):
                                m = pe.matmul(psO[:, n % 3, :], a[:, t % 2, k, :], b[:, k // 2, cols],
                                              start=(k == 0 and j == 0), stop=(k == DT - 1 and j == 2))
                        m.then_inc(s_of, 1)

                def h_transposes(t):
                    pe.wait_ge(s_h, t + 1)
                    for c in range(2):
                        if t:
                            pe.wait_ge(s_hT, 2 * (t - 1) + c + 1)
                        for i in range(4):
                            k = 4 * c + i
                            m = pe.transpose(psH[:, c, P * i:P * i + P], h[:, t % 2, P * k:P * k + P], ident[:])
                        m.then_inc(s_hf, 1)

                def router(t):
                    pe.wait_ge(s_hT, 2 * t + 2)
                    if t == 0:
                        pe.wait_ge(s_wr, 16)
                    for k in range(DT):
                        m = pe.matmul(psR[:, 0, NE * t:NE * t + NE], hT[:, t % 2, k, :], wr[:, k, :], start=(k == 0), stop=(k == DT - 1))
                    m.then_inc(s_lg, 1)

                for i in range(TT + 3):
                    if i < TT:
                        mix_transposes(i)
                    if 1 <= i <= TT:
                        product(i - 1)
                    if 2 <= i <= TT + 1:
                        h_transposes(i - 2)
                    if i >= 3:
                        router(i - 3)
                pe.wait_ge(s_pr, 1)
                for t in range(TT):
                    m = pe.transpose(psT[0:NE, t // 4, P * (t % 4):P * (t % 4) + P], pr[:, t, :], ident[:])
                m.then_inc(s_pf, 1)

            @block.scalar
            def _(act):
                for i in range(TT + 1):
                    if i < TT:
                        if i >= 2:
                            act.wait_ge(s_of, 2 * (i - 2) + 2)
                        for c in range(2):
                            act.wait_ge(s_tf, 2 * i + c + 1)
                            act.activation(mixh[:, i % 2, 4 * c:4 * c + 4, :], psT[:, c, :].rearrange("p (k c) -> p k c", k=4),
                                           ACT.Identity).then_inc(s_th, one(s_th))
                    if i == 0:
                        for j in range(SPLIT):
                            act.wait_ge(s_w[0], 16)
                            act.wait_ge(s_w[1], 16)
                            act.activation(wh[:, j, :], ring[:, j, :], ACT.Identity).then_inc(s_wh, one(s_wh))
                    if i >= 1:
                        t = i - 1
                        act.wait_ge(s_ot, 2 * t + 2)
                        if so_far(s_th):
                            act.wait_ge(s_th, so_far(s_th))
                        if so_far(s_rt):
                            act.wait_ge(s_rt, so_far(s_rt))
                        act.activation(sq[:], x[:, t, :], ACT.Square, accum_out=ssq[:, t:t + 1]).then_inc(s_sq, one(s_sq))
                        act.wait_ge(s_var, t + 1)
                        act.activation(rs[:, 1, t:t + 1], rs[:, 0, t:t + 1], ACT.Sqrt).then_inc(s_rt, one(s_rt))
                act.wait_ge(s_sub, 1)
                act.activation(ex[:], lg[:], ACT.Exp).then_inc(s_ex, one(s_ex))
                act.wait_ge(s_pf, 1)
                act.activation(pT[:], psT[0:NE].rearrange("p a c -> p (a c)"), ACT.Identity).then_inc(s_pT, one(s_pT))

            @block.vector
            def _(dve):
                def mix_low(t):
                    for c in range(2):
                        dve.wait_ge(s_th, 2 * t + c + 1)
                        dve.tensor_tensor(mixl[:, t % 2, 4 * c:4 * c + 4, :], psT[:, c, :].rearrange("p (k c) -> p k c", k=4),
                                          mixh[:, t % 2, 4 * c:4 * c + 4, :], ALU.subtract).then_inc(s_tl, one(s_tl))

                dve.wait_ge(s_c, 32)
                mix_low(0)
                for j in range(SPLIT):
                    dve.wait_ge(s_wh, j + 1)
                    dve.tensor_tensor(wl[:, j, :], ring[:, j, :], wh[:, j, :], ALU.subtract).then_inc(s_wl, one(s_wl))
                mix_low(1)
                for i in range(TT + 1):
                    if i < TT:
                        t = i
                        dve.wait_ge(tile_loaded[t], x_loaded)
                        for c in range(2):
                            n = 2 * t + c
                            dve.wait_ge(s_of, n + 1)
                            xs = x[:, t, 512 * c:512 * c + 512]
                            dve.tensor_tensor(xs, xs, psO[:, n % 3, :], ALU.add).then_inc(s_ot, one(s_ot))
                        dve.wait_ge(s_sq, t + 1)
                        dve.wait_ge(s_ot, so_far(s_ot))
                        dve.tensor_scalar(rs[:, 0, t:t + 1], ssq[:, t:t + 1], 1.0 / D, EPS, ALU.mult, ALU.add).then_inc(s_var, one(s_var))
                        dve.wait_ge(s_rt, t + 1)
                        dve.reciprocal(rs[:, 2, t:t + 1], rs[:, 1, t:t + 1]).then_inc(own_dve, one(own_dve))
                        newton(dve, own_dve, one, so_far, rs[:, :, t:t + 1])
                        if t >= 2:
                            dve.wait_ge(s_sth[t % 2], 16 * (t // 2))
                            dve.wait_ge(s_hf, 2 * (t - 2) + 2)
                        dve.tensor_scalar(h[:, t % 2, :], x[:, t, :], rs[:, 2, t:t + 1], None, ALU.mult).then_inc(s_h, one(s_h))
                        if t + 2 < TT:
                            mix_low(t + 2)
                    if i >= 1:
                        t = i - 1
                        if t >= 2:
                            dve.wait_ge(s_lg, t - 1)
                        for c in range(2):
                            dve.wait_ge(s_hf, 2 * t + c + 1)
                            lw = lnw[:, 4 * c:4 * c + 4].unsqueeze(2).to_broadcast([P, 4, P])
                            dve.tensor_tensor(hT[:, t % 2, 4 * c:4 * c + 4, :], psH[:, c, :].rearrange("p (k c) -> p k c", k=4), lw, ALU.mult).then_inc(s_hT, one(s_hT))
                dve.wait_ge(s_lg, TT)
                dve.tensor_copy(lg[:], psR[:, 0, 0:TT * NE].rearrange("p (t e) -> p t e", e=NE)).then_inc(own_dve, one(own_dve))
                dve.wait_ge(own_dve, so_far(own_dve))
                dve.tensor_reduce(st[:, 0, :], lg[:], AX_X, ALU.max).then_inc(own_dve, one(own_dve))
                dve.wait_ge(own_dve, so_far(own_dve))
                dve.tensor_tensor(lg[:], lg[:], st[:, 0, :].unsqueeze(2).to_broadcast([P, TT, NE]), ALU.subtract).then_inc(s_sub, one(s_sub))
                dve.wait_ge(s_ex, 1)
                dve.tensor_reduce(st[:, 1, :], ex[:], AX_X, ALU.add).then_inc(own_dve, one(own_dve))
                dve.wait_ge(own_dve, so_far(own_dve))
                dve.reciprocal(st[:, 2, :], st[:, 1, :]).then_inc(own_dve, one(own_dve))
                dve.wait_ge(own_dve, so_far(own_dve))
                dve.tensor_tensor(pr[:], ex[:], st[:, 2, :].unsqueeze(2).to_broadcast([P, TT, NE]), ALU.mult).then_inc(s_pr, one(s_pr))
                dve.wait_ge(s_pr, so_far(s_pr))
                dve.tensor_copy(prc[:].rearrange("p e t -> p t e"), pr[:]).then_inc(s_pr, one(s_pr))


def expert_stage(nc, dram, scratch, ring, piece_loaded, wh, wl, p, wp, p_loaded):
    with ExitStack() as ctx:
        sb = lambda name, shape, dt=F32: ctx.enter_context(nc.sbuf_tensor(name, shape, dt))
        ps = lambda name, n: ctx.enter_context(nc.psum_tensor(name, [P, n, 512], F32))
        sem = lambda name: ctx.enter_context(nc.semaphore(name))
        xg = sb("e_xg", [P, D])
        xT = sb("e_xT", [P, DT, P])
        xh = sb("e_xh", [P, 2, DT, P], F32R)
        xl = sb("e_xl", [P, 2, DT, P], F32R)
        sg = sb("e_sg", [P, 512])
        hid = sb("e_hid", [P, 2, 512])
        hidT = sb("e_hidT", [P, FF // P, P])
        y = sb("e_y", [P, D])
        ident = sb("e_ident", [P, P])
        lnw = sb("e_lnw", [P, DT])
        prow = sb("e_prow", [P, L])
        pcol = sb("e_pcol", [P, TT])
        cmp = sb("e_cmp", [P, L])
        lower = sb("e_lower", [P, P])
        iota = sb("e_iota", [P, P])
        cnt = sb("e_cnt", [P, TT, 3])
        rank = sb("e_rank", [P, TT])
        hot = sb("e_hot", [P, TT, P])
        vals = sb("e_vals", [P, TT, 2])
        idx = sb("e_idx", [P, 2, 1], I32)
        gate = sb("e_gate", [P, 2])
        psG, psU, psT, psY = ps("e_psG", 2), ps("e_psU", 2), ps("e_psT", 2), ps("e_psY", 2)

        s_c = sem("e_constants")
        own_dve = sem("e_own_dve")
        s_p = sem("e_probs_loaded")
        s_rank = sem("e_ranked")
        s_hot = sem("e_slots_ready")
        s_rf, s_rt = sem("e_route_filled"), sem("e_route_taken")
        s_g = sem("e_gathered")
        s_xf, s_xt = sem("e_x_transposed"), sem("e_x_taken")
        s_xh, s_xl = sem("e_xh_ready"), sem("e_xl_ready")
        s_hi, s_lo = sem("e_hi_ready"), sem("e_lo_ready")
        s_gu = sem("e_piece_multiplied")
        s_sg, s_hid = sem("e_silu_ready"), sem("e_hidden_ready")
        s_hf, s_ht = sem("e_hid_transposed"), sem("e_hidT_ready")
        s_dn = sem("e_down_multiplied")
        s_y = sem("e_y_ready")
        s_sc = sem("e_scattered")

        with nc.Block() as block:
            @block.sync
            def _(sp):
                def probs(e):
                    sp.dma_start(prow[:], scratch["prow"][bass.ds(e, 1), :].to_broadcast([P, L])).then_inc(s_p, 16)
                    sp.dma_start(pcol[:], scratch["pcol"][bass.ds(e, 1)].rearrange("o p t -> (o p) t")).then_inc(s_p, 16)

                def body(e, par, last, first=False):
                    for i in range(PER):
                        if first and i < RING:
                            continue
                        if i < RING:
                            sp.wait_ge(s_dn, NDN * e + i + 1 - NDN)
                        else:
                            sp.wait_ge(s_lo, NGU * e + i - RING + 1)
                        load_piece(sp, dram, ring, piece_loaded, e, i)
                        if i == RING and not last:
                            sp.wait_ge(s_rank, e + 1)
                            probs(e + 1)

                probs(0)
                sp.dma_start(lnw[:], dram["l_ln_ffn"]).then_inc(s_c, 16)
                sp.dma_start(ident[:], dram["c_ident"]).then_inc(s_c, 16)
                sp.dma_start(lower[:], dram["c_lower"]).then_inc(s_c, 16)
                sp.dma_start(iota[:], dram["c_iota"]).then_inc(s_c, 16)
                sp.dma_start(vals[:, :, 0:1], dram["c_tok"].unsqueeze(2), allow_slow_non_contiguous=True).then_inc(s_c, 16)
                body(0, 0, False, first=True)
                body(1, 1, False)
                with sp.Fori(2, NE - 2, 2) as e:
                    body(e, 0, False)
                    body(e + 1, 1, False)
                body(NE - 2, 0, False)
                body(NE - 1, 1, True)
                for i in range(SPLIT):
                    sp.wait_ge(s_dn, NDN * NE + i + 1 - NDN)
                    load_piece(sp, dram, ring, piece_loaded, NE, i)
                sp.dma_start(p[:], dram["p"][0, 0].rearrange("(t p) c -> p t c", p=P)).then_inc(p_loaded, 16)
                sp.dma_start(wp[:], dram["w_ple_proj"][0].rearrange("(k p) c -> p k c", p=P)).then_inc(p_loaded, 16)

            @block.gpsimd
            def _(pool):
                def gather(e, par):
                    pool.wait_ge(s_rt, e + 1)
                    pool.indirect_dma_start(xg[:], None, scratch["h2"], bass.IndirectOffsetOnAxis(ap=idx[:, par, :], axis=0)).then_inc(s_g, 16)

                def body(e, par, last):
                    if not last:
                        pool.wait_ge(s_xf, e + 1)
                        gather(e + 1, 1 - par)
                    pool.wait_ge(s_y, e + 1)
                    pool.indirect_dma_start(scratch["r"], bass.IndirectOffsetOnAxis(ap=idx[:, par, :], axis=0), y[:], None,
                                            compute_op=ALU.add).then_inc(s_sc, 16)
                    pool.wait_ge(s_sc, 16 * e + 16)

                gather(0, 0)
                for e in range(NE):
                    body(e, e % 2, e == NE - 1)

            @block.tensor
            def _(pe):
                def route(e):
                    pe.wait_ge(s_hot, e + 1)
                    for t in range(TT):
                        m = pe.matmul(psT[:, 0, 0:2], hot[:, t, :], vals[:, t, :], start=(t == 0), stop=(t == TT - 1))
                    m.then_inc(s_rf, 1)

                def x_transposes(e):
                    pe.wait_ge(s_rt, e + 1)
                    pe.wait_ge(s_g, 16 * e + 16)
                    for k in range(DT):
                        m = pe.transpose(psT[:, k // 4, P * (k % 4):P * (k % 4) + P], xg[:, P * k:P * k + P], ident[:])
                    m.then_inc(s_xf, 1)

                def hid_transposes(e, n):
                    pe.wait_ge(s_hid, 4 * e + n + 1)
                    if n >= 2:
                        pe.wait_ge(s_ht, 4 * e + n - 1)
                    for i in range(4):
                        m = pe.transpose(psT[:, n % 2, P * i:P * i + P], hid[:, n % 2, P * i:P * i + P], ident[:])
                    m.then_inc(s_hf, 1)

                def body(e, par, last):
                    pe.wait_ge(s_xh, e + 1)
                    pe.wait_ge(s_xl, e + 1)
                    for n in range(4):
                        for m_, bank in ((0, psG), (1, psU)):
                            if n < 2:
                                pe.wait_ge(s_hid, 4 * e + n - 2 + 1) if not (isinstance(e, int) and e == 0) else None
                            else:
                                pe.wait_ge(s_hid, 4 * e + n - 2 + 1)
                            for half in range(2):
                                i = 4 * n + 2 * m_ + half
                                pe.wait_ge(s_lo, NGU * e + i + 1)
                                for k in range(4):
                                    kk = 4 * half + k
                                    for j, (a, b) in enumerate(((xh, wh), (xl, wh), (xh, wl))):
                                        mm = pe.matmul(bank[:, n % 2, :], a[:, par, kk, :], b[:, i % SPLIT, 512 * k:512 * k + 512],
                                                       start=(kk == 0 and j == 0), stop=(kk == DT - 1 and j == 2))
                                mm.then_inc(s_gu, 1)
                        if n >= 1:
                            hid_transposes(e, n - 1)
                    for j in range(NDN):
                        i = NGU + j
                        pe.wait_ge(piece_loaded[i % RING], 16 * (PER // RING) * e + 16 * (i // RING + 1))
                        if j == 0:
                            if not (isinstance(e, int) and e == 0):
                                pe.wait_ge(s_y, e)
                        if j % 2 == 0:
                            pe.wait_ge(s_ht, 4 * e + j // 2 + 1)
                        wdn = ring[:, i % RING, :].rearrange("p (k c) -> p k c", k=2)
                        for k in range(2):
                            for c in range(2):
                                mm = pe.matmul(psY[:, c, :], hidT[:, 2 * j + k, :], wdn[:, k, 512 * c:512 * c + 512],
                                               start=(j == 0 and k == 0), stop=(j == NDN - 1 and k == 1))
                        mm.then_inc(s_dn, 1)
                        if j == 1:
                            hid_transposes(e, 3)
                        if j == 5 and not last:
                            pe.wait_ge(s_ht, 4 * e + 4)
                            route(e + 1)
                    if not last:
                        x_transposes(e + 1)

                pe.wait_ge(s_c, 80)
                route(0)
                x_transposes(0)
                body(0, 0, False)
                body(1, 1, False)
                with pe.Fori(2, NE - 2, 2) as e:
                    body(e, 0, False)
                    body(e + 1, 1, False)
                body(NE - 2, 0, False)
                body(NE - 1, 1, True)

            @block.scalar
            def _(act):
                def hi(e, i):
                    act.wait_ge(piece_loaded[i % RING], 16 * (PER // RING) * e + 16 * (i // RING + 1))
                    if not (isinstance(e, int) and e == 0 and i < SPLIT):
                        act.wait_ge(s_gu, NGU * e + i - SPLIT + 1)
                    act.activation(wh[:, i % SPLIT, :], ring[:, i % RING, :], ACT.Identity).then_inc(s_hi, 1)

                def silu(e, n):
                    act.wait_ge(s_gu, NGU * e + 4 * n + 2)
                    if n or not (isinstance(e, int) and e == 0):
                        act.wait_ge(s_hid, 4 * e + n)
                    act.activation(sg[:], psG[:, n % 2, :], ACT.Silu).then_inc(s_sg, 1)

                def take_hid(e, n):
                    act.wait_ge(s_hf, 4 * e + n + 1)
                    act.activation(hidT[:, 4 * n:4 * n + 4, :], psT[:, n % 2, :].rearrange("p (k c) -> p k c", k=4), ACT.Identity).then_inc(s_ht, 1)

                def x_high(e, par):
                    act.wait_ge(s_xt, e + 1)
                    act.activation(xh[:, par], xT[:], ACT.Identity).then_inc(s_xh, 1)

                def body(e, par, last):
                    for i in range(SPLIT, NGU):
                        hi(e, i)
                        if i in (5, 9, 13):
                            silu(e, (i - 5) // 4)
                        if i == 11 or i == 15:
                            take_hid(e, (i - 11) // 4)
                    silu(e, 3)
                    take_hid(e, 2)
                    take_hid(e, 3)
                    for i in range(SPLIT):
                        hi(e + 1, i)
                    if not last:
                        x_high(e + 1, 1 - par)
                    act.wait_ge(s_dn, NDN * e + NDN)
                    if not (isinstance(e, int) and e == 0):
                        act.wait_ge(s_sc, 16 * e)
                    act.activation(y[:].rearrange("p (a c) -> p a c", a=2), psY[:], ACT.Identity, scale=gate[:, par:par + 1]).then_inc(s_y, 1)

                for i in range(SPLIT):
                    hi(0, i)
                x_high(0, 0)
                body(0, 0, False)
                body(1, 1, False)
                with act.Fori(2, NE - 2, 2) as e:
                    body(e, 0, False)
                    body(e + 1, 1, False)
                body(NE - 2, 0, False)
                body(NE - 1, 1, True)

            @block.vector
            def _(dve):
                own_before = [0]
                one, so_far = raise_counts()

                def ranks(e, ts):
                    if ts[0] == 0:
                        dve.wait_ge(s_p, 32 * e + 32)
                        dve.memset(cnt[:, 0, 0:1], 0.0).then_inc(own_dve, one(own_dve))
                    for t in ts:
                        own_p = pcol[:, t:t + 1]
                        a = P * t
                        dve.wait_ge(own_dve, own_before[0] + so_far(own_dve))
                        if t:
                            dve.tensor_scalar(cmp[:, 0:a], prow[:, 0:a], own_p, None, ALU.is_ge, ALU.add,
                                              accum_out=cnt[:, t, 0:1]).then_inc(own_dve, one(own_dve))
                        dve.tensor_scalar(cmp[:, a:L], prow[:, a:L], own_p, None, ALU.is_gt, ALU.add,
                                          accum_out=cnt[:, t, 1:2]).then_inc(own_dve, one(own_dve))
                        dve.scalar_tensor_tensor(out=hot[:, t, :], in0=prow[:, a:a + P], scalar=own_p, in1=lower[:],
                                                 op0=ALU.is_equal, op1=ALU.mult, accum_out=cnt[:, t, 2:3]).then_inc(own_dve, one(own_dve))

                def slots(e):
                    dve.wait_ge(own_dve, own_before[0] + so_far(own_dve))
                    dve.tensor_reduce(rank[:], cnt[:], AX_X, ALU.add).then_inc(own_dve, one(own_dve))
                    dve.tensor_copy(vals[:, :, 1:2], pcol[:].unsqueeze(2)).then_inc(s_rank, 1)
                    dve.wait_ge(own_dve, own_before[0] + so_far(own_dve))
                    for t in range(TT - 1):
                        dve.tensor_scalar(hot[:, t, :], iota[:], rank[:, t:t + 1], None, ALU.is_equal).then_inc(own_dve, one(own_dve))
                    dve.tensor_scalar(hot[:, TT - 1, :], iota[:], rank[:, TT - 1:TT], None, ALU.is_equal).then_inc(s_hot, 1)

                def take_route(e, par):
                    dve.wait_ge(s_rf, e + 1)
                    if not (isinstance(e, int) and e < 2):
                        dve.wait_ge(s_sc, 16 * (e - 1))
                    dve.tensor_copy(gate[:, par:par + 1], psT[:, 0, 1:2]).then_inc(own_dve, one(own_dve))
                    dve.tensor_copy(idx[:, par, :], psT[:, 0, 0:1]).then_inc(s_rt, 1)

                def take_x(e, par):
                    dve.wait_ge(s_xf, e + 1)
                    dve.tensor_tensor(xT[:], psT[:].rearrange("p a (k c) -> p (a k) c", c=P),
                                      lnw[:].unsqueeze(2).to_broadcast([P, DT, P]), ALU.mult).then_inc(s_xt, 1)
                    dve.wait_ge(s_xh, e + 1)
                    dve.tensor_tensor(xl[:, par], xT[:], xh[:, par], ALU.subtract).then_inc(s_xl, 1)

                def lo(e, i):
                    dve.wait_ge(s_hi, NGU * e + i + 1)
                    dve.tensor_tensor(wl[:, i % SPLIT, :], ring[:, i % RING, :], wh[:, i % SPLIT, :], ALU.subtract).then_inc(s_lo, 1)

                def hidden(e, n):
                    dve.wait_ge(s_sg, 4 * e + n + 1)
                    dve.wait_ge(s_gu, NGU * e + 4 * n + 4)
                    if n >= 2:
                        dve.wait_ge(s_hf, 4 * e + n - 1)
                    dve.tensor_tensor(hid[:, n % 2, :], sg[:], psU[:, n % 2, :], ALU.mult).then_inc(s_hid, 1)

                def body(e, par, last):
                    for i in range(SPLIT, NGU):
                        lo(e, i)
                        if i in (7, 11, 15):
                            hidden(e, (i - 7) // 4)
                        if i in (5, 8, 10, 13) and not last:
                            ranks(e + 1, [(5, 8, 10, 13).index(i)])
                    hidden(e, 3)
                    if not last:
                        ranks(e + 1, [4, 5, 6, 7])
                        slots(e + 1)
                        take_route(e + 1, 1 - par)
                    lo(e + 1, 0)
                    lo(e + 1, 1)
                    if not last:
                        take_x(e + 1, 1 - par)
                    lo(e + 1, 2)
                    lo(e + 1, 3)

                dve.wait_ge(s_c, 80)
                ranks(0, range(TT))
                slots(0)
                take_route(0, 0)
                for i in range(SPLIT):
                    lo(0, i)
                take_x(0, 0)
                before = so_far(own_dve)
                body(0, 0, False)
                per_expert = so_far(own_dve) - before
                body(1, 1, False)
                with dve.Fori(2, NE - 2, 2) as e:
                    one, so_far = raise_counts()
                    own_before[0] = before + per_expert * e
                    body(e, 0, False)
                    body(e + 1, 1, False)
                one, so_far = raise_counts()
                own_before[0] = before + per_expert * (NE - 2)
                body(NE - 2, 0, False)
                body(NE - 1, 1, True)


def embed_stage(nc, dram, scratch, own, out, tile_loaded, loads_before, ring, wh, wl, p, wp, s_p):
    own_dve, own_act, one, so_far = own
    SHARED = (((0, 2), (2, 5), (5, 8)), ((0, 4), (4, 7), (7, 8)))
    with ExitStack() as ctx:
        sb = lambda name, shape, dt=F32: ctx.enter_context(nc.sbuf_tensor(name, shape, dt))
        ps = lambda name, n: ctx.enter_context(nc.psum_tensor(name, [P, n, 512], F32))
        sem = lambda name: ctx.enter_context(nc.semaphore(name))
        r, emb = (ring[:, RING // 2 * i:RING // 2 * (i + 1), :].rearrange("p a (b c) -> p (a b) c", c=D) for i in range(2))
        pT = sb("f_pT", [P, 2, 2, P])
        h = sb("f_h", [P, 2, D])
        hT = sb("f_hT", [P, DT, P])
        hh = sb("f_hh", [P, 2, DT, P], F32R)
        hl = sb("f_hl", [P, 2, DT, P], F32R)
        sg = sb("f_sg", [P, D])
        sq = sb("f_sq", [P, D])
        lnw = sb("f_lnw", [P, DT])
        fin = sb("f_fin", [P, D])
        ident = sb("f_ident", [P, P])
        ssq = sb("f_ssq", [P, 2, TT])
        rs = sb("f_rs", [P, 2, 4, TT])
        psT, psP, psG = ps("f_psT", 2), ps("f_psP", 2), ps("f_psG", 4)

        s_c, s_fin = sem("f_constants"), sem("f_final_w_loaded")
        s_pt, s_pT = sem("f_p_transposed"), sem("f_pT_taken")
        s_pp, s_emb = sem("f_embedding_product"), sem("f_embedding_taken")
        s_sq, s_var, s_rt = sem("f_squares"), sem("f_variance"), sem("f_root")
        s_h, s_hf = sem("f_normed"), sem("f_h_transposed")
        s_hT, s_hh, s_hl = sem("f_hT_ready"), sem("f_hh_ready"), sem("f_hl_ready")
        s_g, s_sg, s_r2 = sem("f_gate_product"), sem("f_gate_ready"), sem("f_embedding_added")
        s_out, s_st = sem("f_out_ready"), sem("f_stored")

        with nc.Block() as block:
            @block.sync
            def _(sp):
                sp.dma_start(ident[:], dram["c_ident"]).then_inc(s_c, 16)
                sp.dma_start(lnw[:], dram["l_ln_ple"]).then_inc(s_c, 16)
                for t in range(TT):
                    sp.dma_start(r[:, t, :], scratch["r"][P * t:P * t + P, :]).then_inc(tile_loaded[t], 16)
                sp.dma_start(fin[:], dram["final_norm_w"].unsqueeze(0).to_broadcast([P, D])).then_inc(s_fin, 16)
                for t in range(TT):
                    sp.wait_ge(s_out, t + 1)
                    sp.dma_start(out[0, P * t:P * t + P, :], r[:, t, :]).then_inc(s_st, 16)
                sp.wait_ge(s_st, 16 * TT)

            @block.tensor
            def _(pe):
                pe.wait_ge(s_c, 32)
                pe.wait_ge(s_p, 32)
                for i in range(TT + 1):
                    if i < TT:
                        if i >= 2:
                            pe.wait_ge(s_pT, i - 1)
                        for k in range(2):
                            m = pe.transpose(psT[:, i % 2, P * k:P * k + P], p[:, i, P * k:P * k + P], ident[:])
                        m.then_inc(s_pt, 1)
                    if i >= 1:
                        t = i - 1
                        pe.wait_ge(s_pT, t + 1)
                        for c in range(2):
                            if t:
                                pe.wait_ge(s_emb, 2 * t + c - 1)
                            for k in range(2):
                                m = pe.matmul(psP[:, c, :], pT[:, t % 2, k, :], wp[:, k, 512 * c:512 * c + 512], start=(k == 0), stop=(k == 1))
                            m.then_inc(s_pp, 1)
                pe.wait_ge(s_pT, TT)
                for i in range(TT + 1):
                    if i < TT:
                        pe.wait_ge(s_h, i + 1)
                        if i:
                            pe.wait_ge(s_hT, i)
                        for k in range(DT):
                            m = pe.transpose(psT[:, k // 4, P * (k % 4):P * (k % 4) + P], h[:, i % 2, P * k:P * k + P], ident[:])
                        m.then_inc(s_hf, 1)
                    if i >= 1:
                        t = i - 1
                        pe.wait_ge(s_hh, t + 1)
                        pe.wait_ge(s_hl, t + 1)
                        for c in range(2):
                            n = 2 * t + c
                            if n >= 4:
                                pe.wait_ge(s_sg, n - 3)
                            for k in range(DT):
                                for j, (a, b) in enumerate(((hh, wh), (hl, wh), (hh, wl))):
                                    m = pe.matmul(psG[:, n % 4, :], a[:, t % 2, k, :], b[:, k // 2, D * (k % 2) + 512 * c:D * (k % 2) + 512 * c + 512],
                                                  start=(k == 0 and j == 0), stop=(k == DT - 1 and j == 2))
                            m.then_inc(s_g, 1)

            @block.scalar
            def _(act):

                def embedding(t):
                    act.wait_ge(s_pt, t + 1)
                    if t >= 2:
                        act.wait_ge(s_pp, 2 * (t - 2) + 2)
                    act.activation(pT[:, t % 2], psT[:, t % 2, 0:2 * P].rearrange("p (k c) -> p k c", k=2), ACT.Identity).then_inc(s_pT, one(s_pT))

                def take_embedding(t):
                    for c in range(2):
                        act.wait_ge(s_pp, 2 * t + c + 1)
                        act.activation(emb[:, t, 512 * c:512 * c + 512], psP[:, c, :], ACT.Identity).then_inc(s_emb, one(s_emb))

                def square(phase, t):
                    if so_far(s_pT):
                        act.wait_ge(s_pT, so_far(s_pT))
                    if so_far(s_emb):
                        act.wait_ge(s_emb, so_far(s_emb))
                    if so_far(s_sg):
                        act.wait_ge(s_sg, so_far(s_sg))
                    act.activation(sq[:], r[:, t, :], ACT.Square, accum_out=ssq[:, phase, t:t + 1]).then_inc(s_sq, one(s_sq))

                def root(phase, t):
                    for n, (a, b) in enumerate(SHARED[phase]):
                        if b == t + 1:
                            act.wait_ge(s_var, n + 1 + phase * len(SHARED[0]))
                            act.activation(rs[:, phase, 1, a:b], rs[:, phase, 0, a:b], ACT.Sqrt).then_inc(s_rt, 1)

                for t in range(TT):
                    embedding(t)
                    if t:
                        take_embedding(t - 1)
                    act.wait_ge(tile_loaded[t], loads_before + 16)
                    square(0, t)
                    root(0, t)
                take_embedding(TT - 1)
                for i in range(TT + 1):
                    if i < TT:
                        act.wait_ge(s_hT, i + 1)
                        if i >= 2:
                            act.wait_ge(s_g, 2 * (i - 2) + 2)
                        act.activation(hh[:, i % 2], hT[:], ACT.Identity).then_inc(s_hh, 1)
                    if i >= 1:
                        t = i - 1
                        if t:
                            act.wait_ge(s_r2, t)
                        for c in range(2):
                            act.wait_ge(s_g, 2 * t + c + 1)
                            act.activation(sg[:, 512 * c:512 * c + 512], psG[:, (2 * t + c) % 4, :], ACT.Sigmoid).then_inc(s_sg, one(s_sg))
                        act.wait_ge(s_r2, t + 1)
                        square(1, t)
                        root(1, t)

            @block.vector
            def _(dve):

                def inverse_root(phase, a, b, n):
                    dve.wait_ge(s_sq, phase * TT + b)
                    if so_far(s_r2):
                        dve.wait_ge(s_r2, so_far(s_r2))
                    dve.tensor_scalar(rs[:, phase, 0, a:b], ssq[:, phase, a:b], 1.0 / D, EPS, ALU.mult, ALU.add).then_inc(s_var, one(s_var))
                    dve.wait_ge(s_rt, n + 1)
                    dve.reciprocal(rs[:, phase, 2, a:b], rs[:, phase, 1, a:b]).then_inc(own_dve, one(own_dve))
                    newton(dve, own_dve, one, so_far, rs[:, phase, :, a:b])

                def normed(t):
                    if t >= 2:
                        dve.wait_ge(s_hf, t - 1)
                    dve.tensor_scalar(h[:, t % 2, :], r[:, t, :], rs[:, 0, 2, t:t + 1], None, ALU.mult).then_inc(s_h, one(s_h))

                for n, (a, b) in enumerate(SHARED[0]):
                    inverse_root(0, a, b, n)
                    if n == 0:
                        normed(0)
                dve.wait_ge(s_c, 32)
                dve.wait_ge(s_fin, 16)
                for i in range(TT + 1):
                    if i < TT:
                        if i + 1 < TT:
                            normed(i + 1)
                        dve.wait_ge(s_hf, i + 1)
                        if so_far(s_h):
                            dve.wait_ge(s_h, so_far(s_h))
                        if so_far(s_r2):
                            dve.wait_ge(s_r2, so_far(s_r2))
                        dve.tensor_tensor(hT[:], psT[:].rearrange("p a (k c) -> p (a k) c", c=P),
                                                     lnw[:].unsqueeze(2).to_broadcast([P, DT, P]), ALU.mult).then_inc(s_hT, one(s_hT))
                        dve.wait_ge(s_hh, i + 1)
                        dve.wait_ge(s_hT, so_far(s_hT))
                        dve.tensor_tensor(hl[:, i % 2], hT[:], hh[:, i % 2], ALU.subtract).then_inc(s_hl, one(s_hl))
                    if i >= 1:
                        t = i - 1
                        dve.wait_ge(s_sg, 2 * t + 2)
                        dve.wait_ge(s_emb, 2 * t + 2)
                        dve.tensor_tensor(emb[:, t, :], emb[:, t, :], sg[:], ALU.mult).then_inc(own_dve, one(own_dve))
                        dve.wait_ge(own_dve, so_far(own_dve))
                        dve.tensor_tensor(r[:, t, :], r[:, t, :], emb[:, t, :], ALU.add).then_inc(s_r2, one(s_r2))
                        for n, (a, b) in enumerate(SHARED[1]):
                            if b == t + 1:
                                inverse_root(1, a, b, len(SHARED[0]) + n)
                                for u in range(a, b):
                                    dve.scalar_tensor_tensor(out=r[:, u, :], in0=r[:, u, :], scalar=rs[:, 1, 2, u:u + 1], in1=fin[:],
                                                                        op0=ALU.mult, op1=ALU.mult).then_inc(s_out, one(s_out))


def program(nc, dram, out):
    scratch = {name: nc.dram_tensor("s_" + name, shape, F32, kind="Internal").ap() for name, shape in {
        "hy": (3, L, HW), "code": (2 * RANK, L), "qk": (2 * QK // P, P, L), "vg": (2, L, GW),
        "spec": (ORDER, 2, P, GROUPS, 2, HALF), "r": (L, D), "h2": (L, D), "prow": (NE, L), "pcol": (NE, P, TT)}.items()}
    sem = nc.alloc_semaphore
    own = (sem("own_dve"), sem("own_act"), *raise_counts())
    tile_loaded = [sem(f"tile_loaded{t}") for t in range(TT)]
    w_in_loaded = [sem(f"w_in_loaded{i}") for i in range(WB)]
    w_out_loaded = [sem(f"w_out_loaded{c}") for c in range(2)]
    piece_loaded = [sem(f"piece_loaded{i}") for i in range(RING)]
    p_loaded = sem("ple_loaded")
    with nc.sbuf_tensor("ring", [P, RING, 2 * D], F32, side="right") as ring:
        first, second = (ring[:, RING // 2 * i:RING // 2 * (i + 1), :].rearrange("p a (b c) -> p (a b) c", c=D) for i in range(2))
        with nc.sbuf_tensor("w_in", [P, WB, DT, WC], F32, side="right") as w_in:
            filter_stage(nc, dram, scratch, own, tile_loaded, first, second, w_in, w_in_loaded)
            hyena_stage(nc, dram, scratch, own, first, w_in, w_in_loaded, second)
        attention_stage(nc, dram, scratch, own, second, first, w_out_loaded)
        with nc.sbuf_tensor("w_high", [P, SPLIT, 2 * D], F32R) as wh, nc.sbuf_tensor("w_low", [P, SPLIT, 2 * D], F32R) as wl:
            residual_stage(nc, dram, scratch, own, tile_loaded, 16, ring, piece_loaded, wh, wl, second, w_out_loaded)
            with nc.sbuf_tensor("ple", [P, TT, PLE], F32) as p, nc.sbuf_tensor("ple_proj", [P, 2, D], F32) as wp:
                expert_stage(nc, dram, scratch, ring, piece_loaded, wh, wl, p, wp, p_loaded)
                embed_stage(nc, dram, scratch, own, out, tile_loaded, 32, ring, wh, wl, p, wp, p_loaded)


INPUTS = ["x", "p", "w_in", "gla_wa_f", "gla_wa_b", "gla_norm_w", "hy_f_w1", "hy_f_w2", "hy_f_w3", "hy_bias", "w_out",
          "w_router", "w_gate_e", "w_up_e", "w_down_e", "w_ple_gate", "w_ple_proj", "final_norm_w"]


def by_partition(a):
    a = np.asarray(a)
    return np.ascontiguousarray(np.moveaxis(a.reshape(*a.shape[:-1], -1, P), -1, 0))


def kernel(**inputs):
    import concourse.bacc as bacc
    from concourse.bass_utils import run_bass_kernel_spmd as run
    nc = bacc.Bacc("TRN2", target_bir_lowering=False, num_devices=1)
    arrays = {name: np.ascontiguousarray(inputs[name]) for name in INPUTS}
    arrays.update(shape_constants())
    arrays["l_ln_mix"] = by_partition(inputs["ln_mix_w"][0])
    arrays["l_ln_ffn"] = by_partition(inputs["ln_ffn_w"][0])
    arrays["l_ln_ple"] = by_partition(inputs["ln_ple_w"][0])
    arrays["l_conv_w"] = by_partition(inputs["hy_conv_w"][0])
    arrays["l_conv_b"] = by_partition(inputs["hy_conv_b"][0])
    arrays["l_gate_b"] = by_partition(np.stack([inputs["gla_ba_f"][0], inputs["gla_ba_b"][0]]))
    arrays["l_filter"] = np.ascontiguousarray(np.stack([inputs[n][0] for n in ("hy_f_b1", "hy_f_freq1", "hy_f_b2", "hy_f_freq2")], 1))
    dram = {name: nc.dram_tensor("in_" + name, a.shape, mybir.dt.from_np(a.dtype), kind="ExternalInput").ap() for name, a in arrays.items()}
    out = nc.dram_tensor("out", (1, L, D), F32, kind="ExternalOutput").ap()
    program(nc, dram, out)
    r = run(nc, [{"in_" + name: a for name, a in arrays.items()}], core_ids=[0])
    return r.results[0]["out"]
```
